# Optimizing a Trainium2 kernel written in Bass

```python
import math
import jax
import jax.numpy as jnp
from jax import lax
import numpy as np

D_MODEL = 1024
BATCH = 1
SEQ = 1024
DEPTH = 1

N_MIXERS = 4
RMS_EPS = 1e-6
Q_BLOCK = 128

SSD_D_INNER = 2 * D_MODEL
SSD_HEAD_DIM = 64
SSD_HEADS = SSD_D_INNER // SSD_HEAD_DIM
SSD_GROUPS = 8
SSD_HEADS_PER_GROUP = SSD_HEADS // SSD_GROUPS
SSD_STATE = 128
SSD_CONV = 4
SSD_CHUNK = 128
SSD_CONV_DIM = SSD_D_INNER + 2 * SSD_GROUPS * SSD_STATE
SSD_IN_DIM = SSD_D_INNER + SSD_CONV_DIM + SSD_HEADS

SB_HEAD_DIM = 64
SB_HEADS = D_MODEL // SB_HEAD_DIM

LRU_WIDTH = 1408
LRU_BLOCKS = 16
LRU_BLOCK_DIM = LRU_WIDTH // LRU_BLOCKS
LRU_CONV = 4
LRU_C = 8.0

DIFF_HEAD_DIM = 64
DIFF_HEADS = D_MODEL // (2 * DIFF_HEAD_DIM)
ROPE_THETA = 10000.0

MOE_GROUPS = 4
MOE_EXPERTS_PER_GROUP = 8
MOE_EXPERTS = MOE_GROUPS * MOE_EXPERTS_PER_GROUP
MOE_TOP_K = 2
MOE_FF = 512
MOE_ROW_BLOCK = 128

kernel_name = 'hybrid_ssd_stickbreak_rglru_diffattn_hmoe'

def n_uses(m):
    return len(range(m, DEPTH, N_MIXERS))

def rms_norm(x, w):
    xf = x.astype(jnp.float32)
    y = xf * lax.rsqrt(jnp.mean(xf * xf, axis=-1, keepdims=True) + RMS_EPS)
    return (y * w.astype(jnp.float32)).astype(x.dtype)

def causal_dwconv(x, w, b):
    width, ch = w.shape
    y = lax.conv_general_dilated(x, w[:, None, :], window_strides=(1,), padding=[(width - 1, 0)],
                                 dimension_numbers=('NWC', 'WIO', 'NWC'), feature_group_count=ch)
    return y + b

def segsum(a):
    t = a.shape[-1]
    c = jnp.cumsum(a, axis=-1)
    s = c[..., :, None] - c[..., None, :]
    return jnp.where(jnp.tril(jnp.ones((t, t), dtype=bool)), s, -jnp.inf)

def rope_tables(positions):
    inv = ROPE_THETA ** (-jnp.arange(0, DIFF_HEAD_DIM, 2, dtype=jnp.float32) / DIFF_HEAD_DIM)
    ang = positions.astype(jnp.float32)[..., None] * inv
    return jnp.cos(ang), jnp.sin(ang)

def apply_rope(x, cos, sin):
    extra = x.ndim - 3
    c = cos.reshape(cos.shape[:2] + (1,) * extra + cos.shape[-1:])
    s = sin.reshape(sin.shape[:2] + (1,) * extra + sin.shape[-1:])
    x1, x2 = jnp.split(x, 2, axis=-1)
    return jnp.concatenate([x1 * c - x2 * s, x2 * c + x1 * s], axis=-1).astype(x.dtype)

def ssd_mixer(u, w_in, conv_w, conv_b, dt_bias, a_log, d_skip, norm_w, w_out):
    f32 = jnp.float32
    bsz, seqlen, _ = u.shape
    G, R, P, N, Q = SSD_GROUPS, SSD_HEADS_PER_GROUP, SSD_HEAD_DIM, SSD_STATE, SSD_CHUNK
    nc = seqlen // Q
    zxbcdt = u @ w_in
    z, xbc, dt = jnp.split(zxbcdt, [SSD_D_INNER, SSD_D_INNER + SSD_CONV_DIM], axis=-1)
    xbc = jax.nn.silu(causal_dwconv(xbc, conv_w, conv_b))
    xs, b_in, c_in = jnp.split(xbc, [SSD_D_INNER, SSD_D_INNER + G * N], axis=-1)
    dt = jax.nn.softplus(dt.astype(f32) + dt_bias.astype(f32))
    a = -jnp.exp(a_log.astype(f32)) * dt
    x_dt = xs.astype(f32).reshape(bsz, nc, Q, G, R, P) * dt.reshape(bsz, nc, Q, G, R, 1)
    bc = b_in.astype(f32).reshape(bsz, nc, Q, G, N)
    cc = c_in.astype(f32).reshape(bsz, nc, Q, G, N)
    a = a.reshape(bsz, nc, Q, G, R).transpose(0, 3, 4, 1, 2)
    a_cum = jnp.cumsum(a, axis=-1)
    decay = jnp.exp(segsum(a))
    cb = jnp.einsum('bclgn,bcsgn->bcgls', cc, bc)
    y_diag = jnp.einsum('bcgls,bgrcls,bcsgrp->bclgrp', cb, decay, x_dt)
    decay_states = jnp.exp(a_cum[..., -1:] - a_cum)
    states = jnp.einsum('bclgn,bgrcl,bclgrp->bcgrpn', bc, decay_states, x_dt)
    chunk_a = jnp.pad(a_cum[..., -1], ((0, 0), (0, 0), (0, 0), (1, 0)))
    decay_chunk = jnp.exp(segsum(chunk_a))
    states = jnp.concatenate([jnp.zeros_like(states[:, :1]), states], axis=1)
    states = jnp.einsum('bgrzc,bcgrpn->bzgrpn', decay_chunk, states)[:, :-1]
    y_off = jnp.einsum('bclgn,bcgrpn,bgrcl->bclgrp', cc, states, jnp.exp(a_cum))
    y = (y_diag + y_off).reshape(bsz, seqlen, SSD_HEADS, P)
    y = y + xs.astype(f32).reshape(bsz, seqlen, SSD_HEADS, P) * d_skip.astype(f32)[:, None]
    y = y.reshape(bsz, seqlen, SSD_D_INNER).astype(u.dtype)
    yg = (y * jax.nn.silu(z)).reshape(bsz, seqlen, G, SSD_D_INNER // G)
    yg = rms_norm(yg, norm_w.reshape(G, SSD_D_INNER // G)).reshape(bsz, seqlen, SSD_D_INNER)
    return yg @ w_out

def stick_breaking_mixer(u, w_in, w_out):
    bsz, seqlen, _ = u.shape
    qkv = (u @ w_in).reshape(bsz, seqlen, 3, SB_HEADS, SB_HEAD_DIM)
    q, k, v = qkv[:, :, 0], qkv[:, :, 1], qkv[:, :, 2]
    scale = SB_HEAD_DIM ** -0.5
    outs = []
    for start in range(0, seqlen, Q_BLOCK):
        end = start + Q_BLOCK
        z = jnp.einsum('bqhd,bkhd->bhqk', q[:, start:end], k[:, :end]).astype(jnp.float32) * scale
        t_idx = jnp.arange(start, end)[:, None]
        s_idx = jnp.arange(end)[None, :]
        past = s_idx < t_idx
        log_beta = jax.nn.log_sigmoid(z)
        log_keep = jnp.where(past, jax.nn.log_sigmoid(-z), 0.0)
        suffix = lax.cumsum(log_keep, axis=3, reverse=True) - log_keep
        wts = jnp.where(past, jnp.exp(log_beta + suffix), 0.0)
        outs.append(jnp.einsum('bhqk,bkhd->bqhd', wts.astype(v.dtype), v[:, :end]))
    o = jnp.concatenate(outs, axis=1).reshape(bsz, seqlen, SB_HEADS * SB_HEAD_DIM)
    return o @ w_out

def _linear_combine(left, right):
    a1, b1 = left
    a2, b2 = right
    return a1 * a2, a2 * b1 + b2

def rglru_mixer(u, w_in, conv_w, conv_b, w_rg, b_rg, w_ig, b_ig, lam, w_out):
    f32 = jnp.float32
    bsz, seqlen, _ = u.shape
    gate_branch, x = jnp.split(u @ w_in, 2, axis=-1)
    x = causal_dwconv(x, conv_w, conv_b)
    xb = x.reshape(bsz, seqlen, LRU_BLOCKS, LRU_BLOCK_DIM)
    r = jax.nn.sigmoid(jnp.einsum('blnd,nde->blne', xb, w_rg) + b_rg).reshape(bsz, seqlen, LRU_WIDTH)
    i = jax.nn.sigmoid(jnp.einsum('blnd,nde->blne', xb, w_ig) + b_ig).reshape(bsz, seqlen, LRU_WIDTH)
    log_a = (-LRU_C * jax.nn.softplus(-lam.astype(f32))) * r.astype(f32)
    a = jnp.exp(log_a)
    bterm = jnp.sqrt(-jnp.expm1(2.0 * log_a)) * (i * x).astype(f32)
    _, h = lax.associative_scan(_linear_combine, (a, bterm), axis=1)
    y = h.astype(u.dtype) * jax.nn.gelu(gate_branch)
    return y @ w_out

def diff_attention_mixer(u, cos, sin, w_in, q_norm, k_norm, lam_q1, lam_k1, lam_q2, lam_k2,
                         sub_norm, w_out, lambda_init):
    bsz, seqlen, _ = u.shape
    H, Dh = DIFF_HEADS, DIFF_HEAD_DIM
    q, k, v = jnp.split(u @ w_in, 3, axis=-1)
    q = apply_rope(rms_norm(q.reshape(bsz, seqlen, H, 2, Dh), q_norm), cos, sin)
    k = apply_rope(rms_norm(k.reshape(bsz, seqlen, H, 2, Dh), k_norm), cos, sin)
    v = v.reshape(bsz, seqlen, H, 2 * Dh)
    f32 = jnp.float32
    lam = (jnp.exp(jnp.sum(lam_q1.astype(f32) * lam_k1.astype(f32)))
           - jnp.exp(jnp.sum(lam_q2.astype(f32) * lam_k2.astype(f32))) + lambda_init)
    scale = Dh ** -0.5
    outs = []
    for start in range(0, seqlen, Q_BLOCK):
        end = start + Q_BLOCK
        sc = jnp.einsum('bqhmd,bkhmd->bhmqk', q[:, start:end], k[:, :end]).astype(f32) * scale
        causal = jnp.arange(end)[None, :] <= jnp.arange(start, end)[:, None]
        p = jax.nn.softmax(jnp.where(causal, sc, -jnp.inf), axis=-1)
        wts = p[:, :, 0] - lam * p[:, :, 1]
        outs.append(jnp.einsum('bhqk,bkhd->bqhd', wts.astype(v.dtype), v[:, :end]))
    o = jnp.concatenate(outs, axis=1)
    o = rms_norm(o, sub_norm) * (1.0 - lambda_init)
    return o.reshape(bsz, seqlen, H * 2 * Dh) @ w_out

def hier_moe(u, w_group, b_group, w_expert, b_expert, w_gate, w_up, w_down):
    f32 = jnp.float32
    bsz, seqlen, d = u.shape
    n_tok = bsz * seqlen
    xf = u.reshape(n_tok, d)
    g_logits = (xf @ w_group).astype(f32) + b_group.astype(f32)
    g_prob = jax.nn.softmax(g_logits, axis=-1)
    g_sel = jnp.argmax(g_logits, axis=-1)
    g_gate = jnp.take_along_axis(g_prob, g_sel[:, None], axis=1)[:, 0]
    e_logits = ((xf @ w_expert).astype(f32) + b_expert.astype(f32)).reshape(n_tok, MOE_GROUPS, MOE_EXPERTS_PER_GROUP)
    e_logits = jnp.take_along_axis(e_logits, g_sel[:, None, None], axis=1)[:, 0]
    top_p, top_i = lax.top_k(jax.nn.softmax(e_logits, axis=-1), MOE_TOP_K)
    top_w = g_gate[:, None] * top_p / jnp.sum(top_p, axis=-1, keepdims=True)
    expert_id = (g_sel[:, None] * MOE_EXPERTS_PER_GROUP + top_i).reshape(-1).astype(jnp.int32)
    weight = top_w.reshape(-1)
    token = jnp.repeat(jnp.arange(n_tok, dtype=jnp.int32), MOE_TOP_K)
    n_assign = n_tok * MOE_TOP_K
    n_rows = -(-(n_assign + MOE_EXPERTS * (MOE_ROW_BLOCK - 1)) // MOE_ROW_BLOCK) * MOE_ROW_BLOCK
    n_blocks = n_rows // MOE_ROW_BLOCK
    order = jnp.argsort(expert_id)
    sorted_e = expert_id[order]
    counts = jnp.bincount(expert_id, length=MOE_EXPERTS)
    padded = (counts + MOE_ROW_BLOCK - 1) // MOE_ROW_BLOCK * MOE_ROW_BLOCK
    pad_end = jnp.cumsum(padded)
    pad_start = pad_end - padded
    grp_start = jnp.cumsum(counts) - counts
    dest = pad_start[sorted_e] + (jnp.arange(n_assign) - grp_start[sorted_e])
    row_token = jnp.zeros((n_rows,), jnp.int32).at[dest].set(token[order])
    row_weight = jnp.zeros((n_rows,), weight.dtype).at[dest].set(weight[order])
    block_expert = jnp.minimum(
        jnp.searchsorted(pad_end, jnp.arange(n_blocks) * MOE_ROW_BLOCK, side='right'), MOE_EXPERTS - 1)
    x_rows = xf[row_token].reshape(n_blocks, MOE_ROW_BLOCK, d)

    def expert_rows(args):
        xb, e = args
        hid = jax.nn.silu(xb @ w_gate[e]) * (xb @ w_up[e])
        return hid @ w_down[e]

    y_rows = lax.map(expert_rows, (x_rows, block_expert)).reshape(n_rows, d)
    y = jnp.zeros_like(xf).at[row_token].add(y_rows * row_weight[:, None].astype(y_rows.dtype))
    return y.reshape(bsz, seqlen, d)

def setup_inputs(seed: int = 0) -> dict:
    key = jax.random.key(seed)
    ks = iter(jax.random.split(key, 64))
    f32 = jnp.float32

    def nrm(shape, scale):
        return jax.random.normal(next(ks), shape, f32) * scale

    def gain(shape):
        return 1.0 + 0.02 * jax.random.normal(next(ks), shape, f32)

    n0, n1, n2, n3 = n_uses(0), n_uses(1), n_uses(2), n_uses(3)
    D = D_MODEL
    x = jax.random.normal(next(ks), (BATCH, SEQ, D), f32)
    positions = jnp.broadcast_to(jnp.arange(SEQ, dtype=jnp.int32), (BATCH, SEQ))
    dt0 = jnp.exp(jax.random.uniform(next(ks), (n0, SSD_HEADS), f32, math.log(1e-3), math.log(1e-1)))
    a0 = jax.random.uniform(next(ks), (n2, LRU_WIDTH), f32, 0.9, 0.999) ** (1.0 / LRU_C)
    return {
        'x': x,
        'positions': positions,
        'norm_mix': gain((DEPTH, D)),
        'norm_ffn': gain((DEPTH, D)),
        'ssd_w_in': nrm((n0, D, SSD_IN_DIM), D ** -0.5),
        'ssd_conv_w': nrm((n0, SSD_CONV, SSD_CONV_DIM), SSD_CONV ** -0.5),
        'ssd_conv_b': nrm((n0, SSD_CONV_DIM), 0.02),
        'ssd_dt_bias': dt0 + jnp.log(-jnp.expm1(-dt0)),
        'ssd_a_log': jnp.log(jax.random.uniform(next(ks), (n0, SSD_HEADS), f32, 1.0, 16.0)),
        'ssd_d': gain((n0, SSD_HEADS)),
        'ssd_norm': gain((n0, SSD_D_INNER)),
        'ssd_w_out': nrm((n0, SSD_D_INNER, D), SSD_D_INNER ** -0.5),
        'sb_w_in': nrm((n1, D, 3 * SB_HEADS * SB_HEAD_DIM), D ** -0.5),
        'sb_w_out': nrm((n1, SB_HEADS * SB_HEAD_DIM, D), (SB_HEADS * SB_HEAD_DIM) ** -0.5),
        'lru_w_in': nrm((n2, D, 2 * LRU_WIDTH), D ** -0.5),
        'lru_conv_w': nrm((n2, LRU_CONV, LRU_WIDTH), LRU_CONV ** -0.5),
        'lru_conv_b': nrm((n2, LRU_WIDTH), 0.02),
        'lru_w_rg': nrm((n2, LRU_BLOCKS, LRU_BLOCK_DIM, LRU_BLOCK_DIM), LRU_BLOCK_DIM ** -0.5),
        'lru_b_rg': nrm((n2, LRU_BLOCKS, LRU_BLOCK_DIM), 0.02),
        'lru_w_ig': nrm((n2, LRU_BLOCKS, LRU_BLOCK_DIM, LRU_BLOCK_DIM), LRU_BLOCK_DIM ** -0.5),
        'lru_b_ig': nrm((n2, LRU_BLOCKS, LRU_BLOCK_DIM), 0.02),
        'lru_lambda': jnp.log(a0) - jnp.log1p(-a0),
        'lru_w_out': nrm((n2, LRU_WIDTH, D), LRU_WIDTH ** -0.5),
        'diff_w_in': nrm((n3, D, 3 * D), D ** -0.5),
        'diff_q_norm': gain((n3, DIFF_HEAD_DIM)),
        'diff_k_norm': gain((n3, DIFF_HEAD_DIM)),
        'diff_lam_q1': nrm((n3, DIFF_HEAD_DIM), 0.1),
        'diff_lam_k1': nrm((n3, DIFF_HEAD_DIM), 0.1),
        'diff_lam_q2': nrm((n3, DIFF_HEAD_DIM), 0.1),
        'diff_lam_k2': nrm((n3, DIFF_HEAD_DIM), 0.1),
        'diff_sub_norm': gain((n3, 2 * DIFF_HEAD_DIM)),
        'diff_w_out': nrm((n3, D, D), D ** -0.5),
        'moe_w_group': nrm((DEPTH, D, MOE_GROUPS), D ** -0.5),
        'moe_b_group': nrm((DEPTH, MOE_GROUPS), 0.01),
        'moe_w_expert': nrm((DEPTH, D, MOE_EXPERTS), D ** -0.5),
        'moe_b_expert': nrm((DEPTH, MOE_EXPERTS), 0.01),
        'moe_w_gate': nrm((DEPTH, MOE_EXPERTS, D, MOE_FF), D ** -0.5),
        'moe_w_up': nrm((DEPTH, MOE_EXPERTS, D, MOE_FF), D ** -0.5),
        'moe_w_down': nrm((DEPTH, MOE_EXPERTS, MOE_FF, D), MOE_FF ** -0.5),
    }

def reference(x, positions, norm_mix, norm_ffn,
              ssd_w_in, ssd_conv_w, ssd_conv_b, ssd_dt_bias, ssd_a_log, ssd_d, ssd_norm, ssd_w_out,
              sb_w_in, sb_w_out,
              lru_w_in, lru_conv_w, lru_conv_b, lru_w_rg, lru_b_rg, lru_w_ig, lru_b_ig, lru_lambda, lru_w_out,
              diff_w_in, diff_q_norm, diff_k_norm, diff_lam_q1, diff_lam_k1, diff_lam_q2, diff_lam_k2,
              diff_sub_norm, diff_w_out,
              moe_w_group, moe_b_group, moe_w_expert, moe_b_expert, moe_w_gate, moe_w_up, moe_w_down):
    cos, sin = rope_tables(positions)
    h = x
    for i in range(DEPTH):
        m, j = i % N_MIXERS, i // N_MIXERS
        u = rms_norm(h, norm_mix[i])
        if m == 0:
            mix = ssd_mixer(u, ssd_w_in[j], ssd_conv_w[j], ssd_conv_b[j], ssd_dt_bias[j], ssd_a_log[j],
                            ssd_d[j], ssd_norm[j], ssd_w_out[j])
        elif m == 1:
            mix = stick_breaking_mixer(u, sb_w_in[j], sb_w_out[j])
        elif m == 2:
            mix = rglru_mixer(u, lru_w_in[j], lru_conv_w[j], lru_conv_b[j], lru_w_rg[j], lru_b_rg[j],
                              lru_w_ig[j], lru_b_ig[j], lru_lambda[j], lru_w_out[j])
        else:
            lambda_init = 0.8 - 0.6 * math.exp(-0.3 * i)
            mix = diff_attention_mixer(u, cos, sin, diff_w_in[j], diff_q_norm[j], diff_k_norm[j],
                                       diff_lam_q1[j], diff_lam_k1[j], diff_lam_q2[j], diff_lam_k2[j],
                                       diff_sub_norm[j], diff_w_out[j], lambda_init)
        h = h + mix
        u = rms_norm(h, norm_ffn[i])
        h = h + hier_moe(u, moe_w_group[i], moe_b_group[i], moe_w_expert[i], moe_b_expert[i],
                         moe_w_gate[i], moe_w_up[i], moe_w_down[i])
    return h


_drawn_inputs = setup_inputs


def setup_inputs(seed=0):
    import zlib

    import numpy as np

    out = dict(_drawn_inputs(seed))
    spreads = {}
    factors = {'ssd_d': 12.736, 'moe_b_group': 30.516, 'moe_b_expert': 5.584, 'norm_ffn': 2.791}
    for name, (base, spread) in spreads.items():
        noise = np.random.default_rng([zlib.crc32(name.encode()), seed]).standard_normal(out[name].shape)
        drawn = base * np.exp(spread * noise) if base else spread * noise
        out[name] = jnp.asarray(drawn.astype(out[name].dtype))
    for name, factor in factors.items():
        out[name] = (out[name] * factor).astype(out[name].dtype)
    return out
```

```python
from contextlib import ExitStack

import concourse.bass as bass
from concourse import mybir

ALU = mybir.AluOpType
ACT = mybir.ActivationFunctionType
AX = mybir.AxisListType
F32 = mybir.dt.float32
F32R = mybir.dt.float32r
I32 = mybir.dt.int32
U32 = mybir.dt.uint32

P = 128
EPS = 1e-6
HEAD_DIM = 64
GROUPS = 8
R = 4
STATE = 128
TAPS = 4
GCH = R * HEAD_DIM
TILES = 6
HALF = 512
UNITS = [(0, 0), (0, 1), (1, 0), (1, 1), (2, 0), (2, 1), (3, 0), (3, 1), (4, 0), (5, 0), (4, 1), (5, 1)]
NU = len(UNITS)
PLAN = {1: [11, NU + 0], 2: [NU + 1], 3: [NU + 2, NU + 3], 4: [NU + 4], 5: [NU + 5, NU + 6],
        6: [NU + 7], 7: [NU + 8, NU + 9], 8: [NU + 10]}
CYCLE = 16
FIRST_PIECES = 2 * TILES
EARLY = {1: [("wo", 2), ("wo", 3), ("wo", 4), ("wo", 5)], 4: [(3, 10), (3, 11)], 6: [(4, 12), (4, 13)],
         7: [(5, 14), (5, 15)]}
LATE = {1: [(1, 6), (1, 7)], 2: [(2, 8), (2, 9)], 8: [(0, 16), (0, 17)]}
TILE_PLACE = [0, 6, 8, 10, 12, 14]
EG = 4
EPG = 8
NE = EG * EPG
MAXB = 52
PADROW = 8192.0


def bcast(ap, shape):
    return ap.to_broadcast(shape)


def mamba(nc, hacc, x, norm_w, w_in, conv_w, conv_b, dt_bias, a_log, d_skip, y_norm, w_out, acum_dram):
    T, D = x.shape
    KD = D // P
    NT = T // P
    NH = GROUPS * R
    DIN = GROUPS * GCH
    XBC = DIN
    DTC = XBC + DIN + 2 * GROUPS * STATE
    CT = (DIN + 2 * GROUPS * STATE) // P
    LASTG = GROUPS - 1

    with ExitStack() as ctx:
        def sb(name, shape, dt=F32):
            return ctx.enter_context(nc.sbuf_tensor(name, shape, dt))

        def sem(name):
            return ctx.enter_context(nc.semaphore(name))

        uTh = sb("uTh", [P, KD, T], F32R)
        uTl = sb("uTl", [P, KD, T], F32R)
        wh = sb("wh", [P, 2, KD, P], F32R)
        wl = sb("wl", [P, 2, KD, P], F32R)
        raw = sb("raw", [P, 2, 512])
        woh = sb("woh", [P, 2, D], F32R)
        wol = sb("wol", [P, 2, D], F32R)
        xr = sb("xr", [P, 2, 3 + HALF])
        v = sb("v", [P, HALF])
        xbc = sb("xbc", [P, 2, 4, T])
        zs = sb("zs", [P, 2, T])
        E = sb("E", [P, 2, R, P])
        xdt = sb("xdt", [P, 2, GCH])
        xds = sb("xds", [P, GCH])
        btok = sb("btok", [P, P])
        cbm = sb("cbm", [P, P])
        S = sb("S", [P, 2, GCH])
        ysb = sb("ysb", [P, GCH])
        ygf = sb("ygf", [P, 2, P])
        sq = sb("sq", [P, 2, P])
        yh = sb("yh", [P, 2, P], F32R)
        yl = sb("yl", [P, 2, P], F32R)
        ms = sb("ms", [P, 2])
        rstd = sb("rstd", [P, 2])
        dtT = sb("dtT", [P, GROUPS, NT, R])
        acum = sb("acum", [P, GROUPS, NT, R])
        eac = sb("eac", [P, GROUPS, NT, R])
        dst = sb("dst", [P, GROUPS, NT, R])
        dch = sb("dch", [P, GROUPS, NT, R])
        ident = sb("ident", [P, P])
        tri = sb("tri", [P, P])
        ones = sb("ones", [P, P])
        cw = sb("cw", [P, TAPS + 1, CT])
        dsk = sb("dsk", [P, 2 * GROUPS])
        nw = sb("nw", [P, 2 * GROUPS])
        alogb = sb("alogb", [P, NH])
        dtb = sb("dtb", [P, NH])
        ssq = sb("ssq", [P, NT])
        msx = sb("msx", [P, NT])
        rsx = sb("rsx", [P, NT])
        mhalf = sb("mhalf", [P, NT])
        wdh = sb("wdh", [P, KD, NH], F32R)
        wdl = sb("wdl", [P, KD, NH], F32R)

        junk, xn, wb = xbc[:, 1, 0, :], xbc[:, 1, 1:3, :], xbc[:, 1, 3, :]
        wdt = xbc[:, 0, 0, 0:KD * NH]
        tmp = [zs[:, j // 4, 256 * (j % 4):256 * (j % 4) + 256] for j in range(8)]
        acs, rows, dall = sq, ygf, ysb[:, 0:NH]

        proj_ps = [ctx.enter_context(nc.psum_tensor(f"proj{j}", [P, 512], F32)) for j in range(2)]
        tcb_ps = [ctx.enter_context(nc.psum_tensor(f"tcb{j}", [P, 4, P], F32)) for j in range(2)]
        y_ps = ctx.enter_context(nc.psum_tensor("y_ps", [P, 2, GCH], F32))
        st_ps = ctx.enter_context(nc.psum_tensor("st_ps", [P, 2, GCH], F32))
        out_ps = [ctx.enter_context(nc.psum_tensor(f"out{j}", [P, 512], F32)) for j in range(2)]

        x_loaded = [sem(f"x_loaded{i}") for i in range(NT)]
        consts_loaded = sem("consts_loaded")
        wdt_loaded = sem("wdt_loaded")
        const_steps = sem("const_steps")
        rows_T = sem("rows_T")
        halved = sem("halved")
        sumsq_done = sem("sumsq_done")
        msx_done = sem("msx_done")
        rsx_done = sem("rsx_done")
        xn_done = sem("xn_done")
        xT_done = sem("xT_done")
        uhi_done = sem("uhi_done")
        ulo_done = sem("ulo_done")
        wd_hi = sem("wd_hi")
        wd_lo = sem("wd_lo")
        dt_mm = sem("dt_mm")
        dt_steps = sem("dt_steps")
        dt_act = sem("dt_act")
        cum_mm = sem("cum_mm")
        cum_act = sem("cum_act")
        acT_mm = sem("acT_mm")
        acT_sb = sem("acT_sb")
        acT_stored = sem("acT_stored")
        raw_loaded = [sem(f"raw_loaded{j}") for j in range(2)]
        w_hi = sem("w_hi")
        w_ready = sem("w_ready")
        proj_done = sem("proj_done")
        raw_copied = sem("raw_copied")
        halo_copied = sem("halo_copied")
        conv_steps = sem("conv_steps")
        tanh_done = sem("tanh_done")
        unit_final = sem("unit_final")
        tcb_done = sem("tcb_done")
        btok_done = sem("btok_done")
        xdt_steps = sem("xdt_steps")
        cbm_done = sem("cbm_done")
        e_loaded = [sem(f"e_loaded{j}") for j in range(2)]
        sub_steps = sem("sub_steps")
        exp_done = sem("exp_done")
        m_done = sem("m_done")
        y_mm = sem("y_mm")
        st_mm = sem("st_mm")
        y_steps = sem("y_steps")
        s_steps = sem("s_steps")
        yT_done = sem("yT_done")
        gate_steps = sem("gate_steps")
        sq_done = sem("sq_done")
        yhi_done = sem("yhi_done")
        ylo_done = sem("ylo_done")
        stat_mm = sem("stat_mm")
        ms_done = sem("ms_done")
        rstd_done = sem("rstd_done")
        out_mm = sem("out_mm")
        h_steps = sem("h_steps")

        def val(G, per, add):
            reg, off = G
            return off * per + add if reg is None else reg * (2 * per) + (off * per + add)

        def nxt(G, n=1):
            return (G[0], G[1] + n)

        def gidx(G):
            return val(G, 1, 0)

        def wait(eng, s, G, per, add):
            if G[0] is None and G[1] * per + add <= 0:
                return
            eng.wait_ge(s, val(G, per, add))

        def pick(ap, G):
            return ap[:, bass.ds(gidx(G), 1)] if G[0] is not None else ap[:, G[1]:G[1] + 1]

        def unit_of(G, i):
            return (nxt(G), i - NU) if i >= NU else (G, i)

        def first(G):
            return G[0] is None and G[1] == 0

        def is_last(G):
            return G[0] is None and G[1] == LASTG

        def steps(G):
            last = is_last(G)
            nolater = G[0] is None and G[1] >= LASTG - 1
            plan = {c: [i for i in PLAN[c] if not (last and i >= NU)] for c in PLAN}
            early = {c: [p for p in EARLY.get(c, []) if not (last and p[0] != "wo")] for c in PLAN}
            late = {c: [p for p in LATE.get(c, []) if not last and not (nolater and p[1] >= CYCLE)] for c in PLAN}
            if last:
                early[1] = [("wo", j) for j in range(4)]
            return plan, early, late

        def groups(eng, body):
            with eng.Fori(0, (GROUPS - 2) // 2) as i:
                body((i, 0))
                body((i, 1))
            body((None, LASTG - 1))
            body((None, LASTG))

        def unit_b(plan, c):
            return plan[c][1] if len(plan[c]) > 1 else None

        def piece_wait(eng, s, G, place, extra):
            wait(eng, s, G, CYCLE, FIRST_PIECES + place + extra)

        block = ctx.enter_context(nc.Block())

        @block.sync
        def _(sp):
            xt = x.rearrange("(i p) d -> p i d", p=P)
            for i in range(NT):
                sp.dma_start(hacc[:, i, :], xt[:, i, :]).then_inc(x_loaded[i], 16)
                if i == 0:
                    sp.dma_start(wb, norm_w.partition_broadcast(P)).then_inc(consts_loaded, 16)
                    sp.dma_start(dtb[:], dt_bias.partition_broadcast(P)).then_inc(consts_loaded, 16)
                    sp.dma_start(alogb[:], a_log.partition_broadcast(P)).then_inc(consts_loaded, 16)
                    sp.dma_start(dall, d_skip.partition_broadcast(P)).then_inc(consts_loaded, 16)
                    sp.dma_start(rows[:, 0, :], conv_w.rearrange("k (n p) -> (k n) p", p=P)).then_inc(consts_loaded, 16)
                    sp.dma_start(rows[0:CT, 1, :], conv_b.rearrange("(n p) -> n p", p=P)).then_inc(consts_loaded, 16)
                    sp.dma_start(rows[CT:CT + 2 * GROUPS, 1, :], y_norm.rearrange("(n p) -> n p", p=P)
                                 ).then_inc(consts_loaded, 16)
                    sp.dma_start(wdt.rearrange("p (k n) -> p k n", k=KD),
                                 w_in[:, DTC:DTC + NH].rearrange("(k p) n -> p k n", p=P)).then_inc(wdt_loaded, 16)

            def column(G, t):
                if t < 2:
                    return val(G, GCH, XBC + t * P)
                if t < 4:
                    return val(G, STATE, XBC + DIN + (t - 2) * GROUPS * STATE)
                return val(G, GCH, (t - 4) * P)

            def load_tile_piece(G, t, half, slot):
                src = w_in[half * 4 * P:(half + 1) * 4 * P, bass.ds(column(G, t), P)].rearrange("(k p) n -> p k n", p=P)
                sp.dma_start(raw[:, slot, :].rearrange("p (k n) -> p k n", k=4), src).then_inc(raw_loaded[slot], 16)

            def load_piece(G, what, place):
                piece_wait(sp, w_ready, G, place, -1)
                if what == "wo":
                    j = place - (0 if is_last(G) else 2)
                    row = val(G, GCH, (j // 2) * P)
                    sp.dma_start(raw[:, place % 2, :], w_out[bass.ds(row, P), (j % 2) * 512:(j % 2) * 512 + 512]
                                 ).then_inc(raw_loaded[place % 2], 16)
                else:
                    load_tile_piece(nxt(G, 2) if place >= CYCLE else nxt(G), what, place % 2, place % 2)

            def load_e(G, c):
                wait(sp, y_mm, G, NT, c - 1)
                src = acum_dram[bass.ds(val(G, NT * R, c * R), R), :].rearrange("r l -> (r l)").partition_broadcast(P)
                sp.dma_start(E[:, c % 2].rearrange("p r l -> p (r l)"), src).then_inc(e_loaded[c % 2], 16)

            for p in range(FIRST_PIECES):
                if p >= 2:
                    sp.wait_ge(w_ready, p - 1)
                load_tile_piece((None, 0), p // 2, p % 2, p % 2)
            G0 = (None, 0)
            for j in range(2):
                sp.wait_ge(acT_sb, j + 1)
                sp.dma_start(acum_dram[j * P:(j + 1) * P, :], acs[:, j, :]).then_inc(acT_stored, 16)
            sp.wait_ge(acT_stored, 32)
            load_e(G0, 0)
            load_e(G0, 1)
            for half in range(2):
                sp.wait_ge(w_ready, FIRST_PIECES + half - 1)
                load_tile_piece((None, 1), 0, half, half)

            def body(G):
                plan, early, late = steps(G)
                last = is_last(G)
                for c in range(1, 9):
                    if c < NT - 1 or not last:
                        load_e(G, c + 1)
                    for what, place in early[c] + late[c]:
                        load_piece(G, what, place)

            groups(sp, body)

        @block.gpsimd
        def _(pool):
            nc.gpsimd.memset(ident[:], 0.0).then_inc(const_steps, 1)
            nc.gpsimd.memset(tri[:], 1.0).then_inc(const_steps, 1)
            nc.gpsimd.memset(ones[:], 1.0).then_inc(const_steps, 1)
            nc.gpsimd.memset(mhalf[:], -0.5).then_inc(const_steps, 1)
            nc.gpsimd.memset(S[:], 0.0).then_inc(const_steps, 1)
            nc.gpsimd.memset(xr[:], 0.0).then_inc(const_steps, 1)
            pool.wait_ge(const_steps, 6)
            nc.gpsimd.affine_select(out=ident[:], in_=ident[:], compare_op=ALU.not_equal, fill=1.0, base=0,
                                    pattern=[[-1, P]], channel_multiplier=1).then_inc(const_steps, 1)
            nc.gpsimd.affine_select(out=tri[:], in_=tri[:], compare_op=ALU.is_ge, fill=0.0, base=0,
                                    pattern=[[1, P]], channel_multiplier=-1).then_inc(const_steps, 1)

            def low(dst, src, hi):
                return nc.gpsimd.tensor_tensor(dst, src, hi.bitcast(F32), ALU.subtract)

            def tile_low(t, half, slot):
                s = (t % 2, slice(half * 4, half * 4 + 4))
                low(wl[:, s[0], s[1], :], raw[:, slot, :].rearrange("p (k n) -> p k n", k=4),
                    wh[:, s[0], s[1], :]).then_inc(w_ready, 1)

            for i in range(NT):
                pool.wait_ge(msx_done, i + 1)
                nc.gpsimd.tensor_tensor(rsx[:, i:i + 1], msx[:, i:i + 1], mhalf[:, i:i + 1], ALU.pow
                                        ).then_inc(rsx_done, 1)
            for p in range(FIRST_PIECES):
                pool.wait_ge(w_hi, p + 1)
                tile_low(p // 2, p % 2, p % 2)

            def piece(G, what, place):
                piece_wait(pool, w_hi, G, place, 1)
                if what == "wo":
                    j = place - (0 if is_last(G) else 2)
                    low(wol[:, j // 2, (j % 2) * 512:(j % 2) * 512 + 512], raw[:, place % 2, :],
                        woh[:, j // 2, (j % 2) * 512:(j % 2) * 512 + 512]).then_inc(w_ready, 1)
                else:
                    tile_low(what, place % 2, place % 2)

            for place in (0, 1):
                piece((None, 0), 0, place)

            def body(G):
                plan, early, late = steps(G)
                for c in range(1, 9):
                    for what, place in early[c]:
                        piece(G, what, place)
                    k = c - 1
                    wait(pool, ms_done, G, NT, k + 1)
                    nc.gpsimd.tensor_tensor(rstd[:, k % 2:k % 2 + 1], ms[:, k % 2:k % 2 + 1], mhalf[:, 0:1], ALU.pow
                                            ).then_inc(rstd_done, 1)
                    for what, place in late[c]:
                        piece(G, what, place)

            groups(pool, body)

        @block.scalar
        def _(act):
            def tile_high(t, half):
                slot = half
                nc.scalar.activation(wh[:, t % 2, half * 4:half * 4 + 4, :],
                                     raw[:, slot, :].rearrange("p (k n) -> p k n", k=4), ACT.Copy).then_inc(w_hi, 1)

            def free_slot(G, t):
                wait(act, proj_done, G, NU, (-1, 0, 2, 4, 6, 8)[t])

            act.wait_ge(const_steps, 8)
            for i in range(NT):
                act.wait_ge(x_loaded[i], 16)
                if i >= 1:
                    act.wait_ge(sumsq_done, i)
                nc.scalar.activation(junk, hacc[:, i, :], ACT.Square, accum_out=ssq[:, i:i + 1]).then_inc(sumsq_done, 1)
            act.wait_ge(wdt_loaded, 16)
            nc.scalar.activation(wdh[:].rearrange("p k n -> p (k n)"), wdt, ACT.Copy).then_inc(wd_hi, 1)
            for i in range(NT):
                for j in range(2):
                    act.wait_ge(xT_done, 2 * i + j + 1)
                    nc.scalar.activation(uTh[:, 4 * j:4 * j + 4, i * P:(i + 1) * P],
                                         tcb_ps[j][:], ACT.Copy).then_inc(uhi_done, 1)
            for p in range(4):
                act.wait_ge(raw_loaded[p % 2], 16 * (p // 2 + 1))
                tile_high(p // 2, p % 2)
            act.wait_ge(dt_steps, 3)
            nc.scalar.activation(tmp[2], tmp[2], ACT.Exp, scale=-1.0).then_inc(dt_act, 1)
            act.wait_ge(dt_steps, 4)
            nc.scalar.activation(tmp[4], tmp[3], ACT.Ln).then_inc(dt_act, 1)
            act.wait_ge(consts_loaded, 16 * 7)
            nc.scalar.activation(alogb[:], alogb[:], ACT.Exp).then_inc(dt_act, 1)
            act.wait_ge(cum_mm, 2)
            flat = "p g c r -> p (g c r)"
            nc.scalar.activation(acum[:].rearrange(flat), y_ps[:, 0, :], ACT.Copy).then_inc(cum_act, 1)
            nc.scalar.activation(eac[:].rearrange(flat), y_ps[:, 0, :], ACT.Exp).then_inc(cum_act, 1)
            nc.scalar.activation(dch[:].rearrange(flat), y_ps[:, 1, :], ACT.Exp).then_inc(cum_act, 1)
            act.wait_ge(dt_steps, 15)
            nc.scalar.activation(dst[:].rearrange(flat), tmp[1], ACT.Exp).then_inc(cum_act, 1)
            for j in range(2):
                act.wait_ge(acT_mm, 2)
                nc.scalar.activation(acs[:, j, :], st_ps[:, 0, j * P:(j + 1) * P], ACT.Copy).then_inc(acT_sb, 1)

            def copy_unit(G, i):
                t, half = UNITS[i]
                wait(act, conv_steps, G, 32, 4 * (i - 1))
                if half == 1:
                    wait(act, raw_copied, G, 8, i)
                    nc.scalar.activation(xr[:, 1, 0:3], xr[:, 0, HALF:HALF + 3], ACT.Copy).then_inc(halo_copied, 1)
                else:
                    wait(act, halo_copied, G, 4, t)
                wait(act, proj_done, G, NU, i + 1)
                nc.scalar.activation(xr[:, half, 3:3 + HALF], proj_ps[i % 2][:], ACT.Copy).then_inc(raw_copied, 1)

            def tanh_unit(G, i, par):
                t, half = UNITS[i]
                cols = slice(half * HALF, half * HALF + HALF)
                if t < 4:
                    wait(act, conv_steps, G, 32, 4 * (i + 1))
                    nc.scalar.activation(xbc[:, par, t, cols], v[:], ACT.Tanh).then_inc(tanh_done, 1)
                else:
                    wait(act, proj_done, G, NU, i + 1)
                    if half == 0:
                        wait(act, gate_steps, G, 24, -12)
                    nc.scalar.activation(zs[:, t - 4, cols], proj_ps[i % 2][:], ACT.Tanh, scale=0.5
                                         ).then_inc(tanh_done, 1)

            def exp_e(G, c):
                wait(act, sub_steps, G, 32, 4 * c + 4)
                e = E[:, c % 2].rearrange("p r l -> p (r l)")
                nc.scalar.activation(e, e, ACT.Exp).then_inc(exp_done, 1)

            def copy_b(G, c):
                wait(act, tcb_done, G, NT, c + 1)
                wait(act, st_mm, G, NT, c)
                nc.scalar.activation(btok[:], tcb_ps[c % 2][:, 2, :], ACT.Copy).then_inc(btok_done, 1)

            def gated(G, k):
                wait(act, gate_steps, G, 24, 3 * k + 3)
                nc.scalar.activation(sq[:], ygf[:], ACT.Square).then_inc(sq_done, 1)
                for t in range(2):
                    nc.scalar.activation(yh[:, t, :], ygf[:, t, :], ACT.Copy, scale=nw[:, bass.ds(val(G, 2, t), 1)]
                                         ).then_inc(yhi_done, 1)

            def piece(G, what, place):
                n = FIRST_PIECES + place
                wait(act, raw_loaded[place % 2], G, 16 * CYCLE // 2, 16 * (n // 2 + 1))
                if what == "wo":
                    j = place - (0 if is_last(G) else 2)
                    nc.scalar.activation(woh[:, j // 2, (j % 2) * 512:(j % 2) * 512 + 512], raw[:, place % 2, :],
                                         ACT.Copy).then_inc(w_hi, 1)
                else:
                    H = nxt(G, 2) if place >= CYCLE else nxt(G)
                    free_slot(H, what)
                    tile_high(what, place % 2)

            G0 = (None, 0)
            act.wait_ge(cum_act, 4)
            for i in range(10):
                t, half = UNITS[i]
                if t < 4:
                    copy_unit(G0, i)
                tanh_unit(G0, i, 0)
                if half == 0 and t < 4:
                    act.wait_ge(proj_done, 2 * t + 2)
                    for q in (0, 1):
                        act.wait_ge(raw_loaded[q], 16 * (t + 3))
                        tile_high(t + 2, q)
                if i == 6:
                    exp_e(G0, 0)
            copy_b(G0, 0)
            exp_e(G0, 1)
            copy_b(G0, 1)
            tanh_unit(G0, 10, 0)
            for place in (0, 1):
                act.wait_ge(raw_loaded[place], 16 * (FIRST_PIECES // 2 + 1))
                act.wait_ge(proj_done, 11)
                tile_high(0, place)

            def body(G):
                plan, early, late = steps(G)
                last = is_last(G)
                prev_b = None
                for c in range(1, 9):
                    k = c - 1
                    if prev_b is not None and prev_b[1] < 8:
                        copy_unit(*prev_b)
                    gated(G, k)
                    if prev_b is not None:
                        tanh_unit(*prev_b, (G[1] + 1) % 2)
                    if c < NT - 1 or not last:
                        exp_e(G, c + 1)
                        if c < 8 or not last:
                            copy_b(G, c + 1)
                    for q in early[c]:
                        piece(G, *q)
                    if plan[c]:
                        A = unit_of(G, plan[c][0])
                        if A[1] < 8:
                            copy_unit(*A)
                        tanh_unit(*A, A[0][1] % 2)
                    for q in late[c]:
                        piece(G, *q)
                    b = unit_b(plan, c)
                    prev_b = unit_of(G, b) if b is not None else None

            groups(act, body)

        @block.vector
        def _(dve):
            vec = nc.vector
            dve.wait_ge(consts_loaded, 16 * 7)
            for i in range(NT):
                dve.wait_ge(sumsq_done, i + 1)
                vec.tensor_scalar(msx[:, i:i + 1], ssq[:, i:i + 1], 1.0 / D, EPS, ALU.mult, ALU.add).then_inc(msx_done, 1)
            dve.wait_ge(rows_T, 1)
            tT = out_ps[1]
            vec.tensor_scalar(cw[:, 0:TAPS, :].rearrange("p k n -> p (k n)"), tT[:, 0:P], 0.5, None, ALU.mult
                              ).then_inc(halved, 1)
            vec.tensor_scalar(cw[:, TAPS, :], tT[:, P:P + CT], 0.5, None, ALU.mult).then_inc(halved, 1)
            vec.tensor_scalar(nw[:], tT[:, P + CT:P + CT + 2 * GROUPS], 0.5, None, ALU.mult).then_inc(halved, 1)
            dh = dall.rearrange("p (n q) -> p n q", q=2)
            for q in range(2):
                half_p = slice(q * HEAD_DIM, (q + 1) * HEAD_DIM)
                vec.tensor_copy(dsk[half_p, :], dh[half_p, :, q]).then_inc(halved, 1)

            def norm_tile(i):
                dve.wait_ge(rsx_done, i + 1)
                if i >= 2:
                    dve.wait_ge(xT_done, 2 * (i - 1))
                vec.scalar_tensor_tensor(xn[:, i % 2, :], hacc[:, i, :], rsx[:, i:i + 1], wb, ALU.mult, ALU.mult
                                         ).then_inc(xn_done, 1)

            norm_tile(0)
            dve.wait_ge(wd_hi, 1)
            vec.tensor_tensor(wdl[:].rearrange("p k n -> p (k n)"), wdt,
                              wdh[:].bitcast(F32).rearrange("p k n -> p (k n)"), ALU.subtract).then_inc(wd_lo, 1)
            for i in range(NT):
                if i + 1 < NT:
                    norm_tile(i + 1)
                for j in range(2):
                    dve.wait_ge(uhi_done, 2 * i + j + 1)
                    cols = slice(i * P, (i + 1) * P)
                    vec.tensor_tensor(uTl[:, 4 * j:4 * j + 4, cols], tcb_ps[j][:],
                                      uTh[:, 4 * j:4 * j + 4, cols].bitcast(F32), ALU.subtract).then_inc(ulo_done, 1)

            count = [0]

            def link(ins):
                count[0] += 1
                ins.then_inc(dt_steps, 1)
                dve.wait_ge(dt_steps, count[0])

            def gcr(ap):
                return ap.rearrange("p (g c r) -> p g c r", g=GROUPS, c=NT)

            dve.wait_ge(dt_mm, 1)
            dtv = out_ps[0][:, 0:NT * NH].rearrange("p (c g r) -> p g c r", c=NT, g=GROUPS)
            b4 = dtb[:].rearrange("p (g r) -> p g r", g=GROUPS)
            for g in range(GROUPS):
                ins = vec.tensor_tensor(gcr(tmp[0])[:, g], dtv[:, g], b4[:, g:g + 1, :].to_broadcast([P, NT, R]), ALU.add)
                if g < GROUPS - 1:
                    ins.then_inc(halved, 1)
            count[0] += 1
            ins.then_inc(dt_steps, 1)
            dve.wait_ge(dt_steps, 1)
            dve.wait_ge(halved, 5 + GROUPS - 1)
            link(vec.tensor_scalar(tmp[1], tmp[0], 0.0, None, ALU.max))
            link(vec.scalar_tensor_tensor(tmp[2], tmp[0], -1.0, tmp[0], ALU.mult, ALU.max))
            dve.wait_ge(dt_act, 1)
            link(vec.tensor_scalar(tmp[3], tmp[2], 1.0, None, ALU.add))
            link(vec.tensor_scalar(tmp[5], tmp[3], -1.0, None, ALU.add))
            link(vec.tensor_scalar(tmp[6], tmp[5], 0.0, None, ALU.is_equal))
            link(vec.tensor_tensor(tmp[5], tmp[5], tmp[6], ALU.add))
            dve.wait_ge(dt_act, 2)
            link(vec.tensor_tensor(tmp[4], tmp[4], tmp[6], ALU.add))
            link(vec.reciprocal(tmp[5], tmp[5]))
            link(vec.tensor_tensor(tmp[4], tmp[4], tmp[5], ALU.mult))
            link(vec.tensor_tensor(tmp[4], tmp[4], tmp[2], ALU.mult))
            dflat = dtT[:].rearrange("p g c r -> p (g c r)")
            link(vec.tensor_tensor(dflat, tmp[4], tmp[1], ALU.add))
            dve.wait_ge(dt_act, 3)
            link(vec.tensor_scalar(alogb[:], alogb[:], -1.0, None, ALU.mult))
            a4 = alogb[:].rearrange("p (g r) -> p g r", g=GROUPS)
            for g in range(GROUPS):
                ins = vec.tensor_tensor(gcr(tmp[7])[:, g], dtT[:, g], a4[:, g:g + 1, :].to_broadcast([P, NT, R]), ALU.mult)
                if g < GROUPS - 1:
                    ins.then_inc(halved, 1)
            dve.wait_ge(halved, 5 + 2 * (GROUPS - 1))
            link(ins)
            dve.wait_ge(cum_act, 3)
            link(vec.tensor_tensor(tmp[1], y_ps[:, 1, :], acum[:].rearrange("p g c r -> p (g c r)"), ALU.subtract))

            def conv_unit(G, i):
                t, half = UNITS[i]
                wait(dve, raw_copied, G, 8, i + 1)
                prev = i - 1 if i else -5
                wait(dve, unit_final, G, NU, prev + 1)
                n = 4 * i
                tile = (G, 2, t) if t < 2 else (G, 1, 2 * GROUPS + (t - 2) * GROUPS)

                def w(k):
                    return cw[:, k, bass.ds(val(*tile), 1)]

                vec.tensor_scalar(v[:], xr[:, half, 3:3 + HALF], w(3), w(4), ALU.mult, ALU.add
                                  ).then_inc(conv_steps, 1)
                for k in (2, 1, 0):
                    wait(dve, conv_steps, G, 32, n + 3 - k)
                    vec.scalar_tensor_tensor(v[:], xr[:, half, k:k + HALF], w(k), v[:], ALU.mult, ALU.add
                                             ).then_inc(conv_steps, 1)

            def final_unit(G, i, par):
                t, half = UNITS[i]
                cols = slice(half * HALF, half * HALF + HALF)
                wait(dve, tanh_done, G, NU, i + 1)
                if t < 4:
                    dst, src = xbc[:, par, t, cols], v[:]
                else:
                    dst, src = zs[:, t - 4, cols], proj_ps[i % 2][:]
                vec.scalar_tensor_tensor(dst, dst, 1.0, src, ALU.add, ALU.mult).then_inc(unit_final, 1)

            def sub_e(G, c):
                wait(dve, e_loaded[c % 2], G, 16 * NT // 2, 16 * (c // 2 + 1))
                a = pick(acum, G) if c < 8 else pick(acum, nxt(G))
                for r in range(R):
                    e = E[:, c % 2, r, :]
                    vec.tensor_scalar(e, e, a[:, 0, c % 8, r:r + 1], 0.0, ALU.subtract, ALU.min).then_inc(sub_steps, 1)

            def spread(tab, G, c):
                H = G if c < 8 else nxt(G)
                return pick(tab, H)[:, 0, c % 8, :].unsqueeze(2).to_broadcast([P, R, HEAD_DIM])

            def heads(ap):
                return ap.rearrange("p (r q) -> p r q", r=R)

            def prep(G, c):
                wait(dve, btok_done, G, NT, c + 1)
                wait(dve, y_mm, G, NT, c - 1)
                tp = tcb_ps[c % 2]
                vec.tensor_tensor(heads(xdt[:, c % 2, :]), heads(tp[:, 0:2, :].rearrange("p t q -> p (t q)")),
                                  spread(dtT, G, c), ALU.mult).then_inc(xdt_steps, 1)
                wait(dve, m_done, G, NT, c)
                vec.tensor_tensor(cbm[:], tp[:, 3, :], tri[:], ALU.mult).then_inc(cbm_done, 1)
                wait(dve, xdt_steps, G, 2 * NT, 2 * c + 1)
                wait(dve, st_mm, G, NT, c)
                vec.tensor_tensor(heads(xds[:]), heads(xdt[:, c % 2, :]), spread(dst, G, c), ALU.mult
                                  ).then_inc(xdt_steps, 1)

            def make_m(G, c):
                wait(dve, exp_done, G, NT, c + 1)
                wait(dve, cbm_done, G, NT, c + 1)
                cb = cbm[:].unsqueeze(1).to_broadcast([P, R, P])
                vec.tensor_tensor(E[:, c % 2], E[:, c % 2], cb, ALU.mult).then_inc(m_done, 1)

            def y_and_state(G, c, last_chunk):
                wait(dve, y_mm, G, NT, c + 1)
                wait(dve, yT_done, G, NT, c)
                vec.tensor_tensor(heads(ysb[:]), heads(y_ps[:, 0, :]), spread(eac, G, c), ALU.mult).then_inc(y_steps, 1)
                wait(dve, y_steps, G, 2 * NT, 2 * c + 1)
                vec.tensor_tensor(ysb[:], ysb[:], y_ps[:, 1, :], ALU.add).then_inc(y_steps, 1)
                new = S[:, (c + 1) % 2, :]
                wait(dve, st_mm, G, NT, c + 1)
                if last_chunk:
                    for j in range(2):
                        vec.memset(new[:, j * P:(j + 1) * P], 0.0).then_inc(s_steps, 1)
                    return
                wait(dve, s_steps, G, 2 * NT, 2 * c)
                vec.tensor_tensor(heads(new), heads(S[:, c % 2, :]), spread(dch, G, c), ALU.mult).then_inc(s_steps, 1)
                wait(dve, s_steps, G, 2 * NT, 2 * c + 1)
                vec.tensor_tensor(new, new, st_ps[:, 0, :], ALU.add).then_inc(s_steps, 1)

            def gate(G, k):
                par = G[1] % 2
                cols = slice(k * P, k * P + P)
                wait(dve, yT_done, G, NT, k + 1)
                for t in range(2):
                    vec.scalar_tensor_tensor(ygf[:, t, :], xbc[:, par, t, cols], dsk[:, bass.ds(val(G, 2, t), 1)],
                                             st_ps[:, 1, t * P:(t + 1) * P], ALU.mult, ALU.add).then_inc(gate_steps, 1)
                wait(dve, gate_steps, G, 24, 3 * k + 2)
                wait(dve, unit_final, G, NU, 10 if k < 4 else 12)
                vec.tensor_tensor(ygf[:], ygf[:], zs[:, :, cols], ALU.mult).then_inc(gate_steps, 1)

            def gated_low(G, k):
                wait(dve, yhi_done, G, 2 * NT, 2 * k + 2)
                for t in range(2):
                    vec.scalar_tensor_tensor(yl[:, t, :], ygf[:, t, :], nw[:, bass.ds(val(G, 2, t), 1)],
                                             yh[:, t, :].bitcast(F32), ALU.mult, ALU.subtract).then_inc(ylo_done, 1)

            def mean_square(G, k):
                wait(dve, stat_mm, G, NT, k + 1)
                vec.tensor_scalar(ms[:, k % 2:k % 2 + 1], out_ps[0][:, 0:1], 1.0 / (4 * GCH), EPS, ALU.mult, ALU.add
                                  ).then_inc(ms_done, 1)

            def add_h(G, k):
                wait(dve, rstd_done, G, NT, k + 1)
                for n, j in enumerate((1, 0)):
                    wait(dve, out_mm, G, 2 * NT, 2 * k + n + 1)
                    h = hacc[:, k, j * 512:(j + 1) * 512]
                    vec.scalar_tensor_tensor(h, out_ps[j][:], rstd[:, k % 2:k % 2 + 1], h, ALU.mult, ALU.add
                                             ).then_inc(h_steps, 1)

            G0 = (None, 0)
            for i in range(10):
                if UNITS[i][0] < 4:
                    conv_unit(G0, i)
                if i == 6:
                    sub_e(G0, 0)
                final_unit(G0, i, 0)
            prep(G0, 0)
            make_m(G0, 0)
            sub_e(G0, 1)
            prep(G0, 1)
            y_and_state(G0, 0, False)
            make_m(G0, 1)
            final_unit(G0, 10, 0)

            def body(G):
                plan, early, late = steps(G)
                last = is_last(G)
                prev_b = None
                for c in range(1, 9):
                    k = c - 1
                    more = c < NT - 1 or not last
                    gate(G, k)
                    if prev_b is not None and prev_b[1] < 8:
                        conv_unit(*prev_b)
                    if more:
                        sub_e(G, c + 1)
                    gated_low(G, k)
                    if prev_b is not None:
                        final_unit(*prev_b, (G[1] + 1) % 2)
                    if more:
                        prep(G, c + 1)
                    if c < NT or not last:
                        y_and_state(G, c, c == NT - 1)
                    if more:
                        make_m(G, c + 1)
                    A = unit_of(G, plan[c][0]) if plan[c] else None
                    if A and A[1] < 8:
                        conv_unit(*A)
                    mean_square(G, k)
                    add_h(G, k)
                    if A:
                        final_unit(*A, A[0][1] % 2)
                    b = unit_b(plan, c)
                    prev_b = unit_of(G, b) if b is not None else None

            groups(dve, body)

        @block.tensor
        def _(pe):
            def mm3(out, ah, al, bh, bl, start, stop):
                nc.tensor.matmul(out, al, bh, start=start, stop=False)
                nc.tensor.matmul(out, ah, bl, start=False, stop=False)
                return nc.tensor.matmul(out, ah, bh, start=False, stop=stop)

            pe.wait_ge(const_steps, 8)
            pe.wait_ge(consts_loaded, 16 * 7)
            nr = CT + 2 * GROUPS
            nc.tensor.transpose(out_ps[1][:, 0:P], rows[:, 0, :], ident[:])
            nc.tensor.transpose(out_ps[1][:, P:P + nr], rows[0:nr, 1, :], ident[0:nr, 0:nr]).then_inc(rows_T, 1)
            for i in range(NT):
                pe.wait_ge(xn_done, i + 1)
                for j in range(2):
                    if i >= 1:
                        pe.wait_ge(ulo_done, 2 * (i - 1) + j + 1)
                    for k in range(4):
                        col = (4 * j + k) * P
                        mm = nc.tensor.transpose(tcb_ps[j][:, k, :], xn[:, i % 2, col:col + P], ident[:])
                    mm.then_inc(xT_done, 1)
            pe.wait_ge(wd_lo, 1)
            for i in range(NT):
                pe.wait_ge(ulo_done, 2 * i + 2)
                for k in range(KD):
                    cols = slice(i * P, (i + 1) * P)
                    mm = mm3(out_ps[0][:, i * NH:(i + 1) * NH], uTh[:, k, cols], uTl[:, k, cols],
                             wdh[:, k, :], wdl[:, k, :], k == 0, k == KD - 1)
            mm.then_inc(dt_mm, 1)

            def unit(G, i):
                t, half = UNITS[i]
                if first(G):
                    pe.wait_ge(w_ready, 2 * t + 2)
                else:
                    wait(pe, w_ready, nxt(G, -1), CYCLE, FIRST_PIECES + TILE_PLACE[t] + 2)
                if i in (0, 1):
                    wait(pe, unit_final, G, NU, i - 1)
                elif i < 10:
                    wait(pe, raw_copied, G, 8, i - 1)
                else:
                    wait(pe, unit_final, G, NU, i - 1)
                cols = slice(half * HALF, half * HALF + HALF)
                for k in range(KD):
                    mm = mm3(proj_ps[i % 2][:], wh[:, t % 2, k, :], wl[:, t % 2, k, :],
                             uTh[:, k, cols], uTl[:, k, cols], k == 0, k == KD - 1)
                mm.then_inc(proj_done, 1)

            def tcb(G, c):
                H, cc = (G, c) if c < 8 else (nxt(G), c - 8)
                par = H[1] % 2
                cols = slice(cc * P, cc * P + P)
                wait(pe, unit_final, H, NU, 7 if cc < 4 else 8)
                wait(pe, xdt_steps, G, 2 * NT, 2 * (c - 1))
                wait(pe, btok_done, G, NT, c - 1)
                out = tcb_ps[c % 2]
                for t in range(3):
                    nc.tensor.transpose(out[:, t, :], xbc[:, par, t, cols], ident[:])
                nc.tensor.matmul(out[:, 3, :], xbc[:, par, 2, cols], xbc[:, par, 3, cols], start=True, stop=True
                                 ).then_inc(tcb_done, 1)

            def scan(G, c):
                H, cc = (G, c) if c < 8 else (nxt(G), c - 8)
                wait(pe, s_steps, G, 2 * NT, 2 * c)
                wait(pe, y_steps, G, 2 * NT, 2 * c)
                nc.tensor.matmul(y_ps[:, 0, :], xbc[:, H[1] % 2, 3, cc * P:cc * P + P], S[:, c % 2, :], start=True, stop=True)
                wait(pe, m_done, G, NT, c + 1)
                for r in range(R):
                    q = slice(r * HEAD_DIM, (r + 1) * HEAD_DIM)
                    mm = nc.tensor.matmul(y_ps[:, 1, q], E[:, c % 2, r, :], xdt[:, c % 2, q], start=True, stop=True)
                mm.then_inc(y_mm, 1)
                wait(pe, xdt_steps, G, 2 * NT, 2 * c + 2)
                wait(pe, btok_done, G, NT, c + 1)
                wait(pe, gate_steps, G, 24, 3 * c)
                nc.tensor.matmul(st_ps[:, 0, :], btok[:], xds[:], start=True, stop=True).then_inc(st_mm, 1)

            def turn_y(G, c):
                wait(pe, y_steps, G, 2 * NT, 2 * c + 2)
                wait(pe, s_steps, G, 2 * NT, 2 * c + 2)
                for t in range(2):
                    mm = nc.tensor.transpose(st_ps[:, 1, t * P:(t + 1) * P], ysb[:, t * P:(t + 1) * P], ident[:])
                mm.then_inc(yT_done, 1)

            def project_out(G, k):
                wait(pe, sq_done, G, NT, k + 1)
                for t in range(2):
                    mm = nc.tensor.matmul(out_ps[0][:, 0:1], sq[:, t, :], ones[:, 0:1], start=(t == 0), stop=(t == 1))
                mm.then_inc(stat_mm, 1)
                wait(pe, ylo_done, G, 2 * NT, 2 * k + 2)
                if k == 0:
                    wait(pe, w_ready, G, CYCLE, FIRST_PIECES + (4 if is_last(G) else 6))
                for j in (1, 0):
                    if j == 0:
                        wait(pe, ms_done, G, NT, k + 1)
                    for t in range(2):
                        cols = slice(j * 512, (j + 1) * 512)
                        mm = mm3(out_ps[j][:], yh[:, t, :], yl[:, t, :], woh[:, t, cols], wol[:, t, cols],
                                 t == 0, t == 1)
                    mm.then_inc(out_mm, 1)

            G0 = (None, 0)
            for i in range(2):
                unit(G0, i)
            pe.wait_ge(dt_steps, 14)
            nc.tensor.matmul(y_ps[:, 0, :], tri[:], tmp[7], start=True, stop=True).then_inc(cum_mm, 1)
            nc.tensor.matmul(y_ps[:, 1, :], ones[:], tmp[7], start=True, stop=True).then_inc(cum_mm, 1)
            pe.wait_ge(cum_act, 1)
            af = acum[:].rearrange("p g c r -> p (g c r)")
            for j in range(2):
                nc.tensor.transpose(st_ps[:, 0, j * P:(j + 1) * P], af[:, j * P:(j + 1) * P], ident[:]).then_inc(acT_mm, 1)
            for i in range(2, 10):
                unit(G0, i)
            tcb(G0, 0)
            unit(G0, 10)
            tcb(G0, 1)
            pe.wait_ge(acT_sb, 2)
            scan(G0, 0)
            turn_y(G0, 0)

            def body(G):
                plan, early, late = steps(G)
                last = is_last(G)
                for c in range(1, 9):
                    if plan[c]:
                        unit(*unit_of(G, plan[c][0]))
                    if c < NT - 1 or not last:
                        tcb(G, c + 1)
                    if c < NT or not last:
                        scan(G, c)
                    if unit_b(plan, c) is not None:
                        unit(*unit_of(G, unit_b(plan, c)))
                    project_out(G, c - 1)
                    if c < NT or not last:
                        turn_y(G, c)

            groups(pe, body)


def routing(nc, hacc, ridx, etab, npairs, wtok, norm_w, w_group, b_group, w_expert, b_expert, u2_dram):
    D = norm_w.shape[0]
    KD = D // P
    NT = hacc.shape[1]
    NL = EG + NE
    NTH = NT * P // P - 1

    with ExitStack() as ctx:
        def sb(name, shape, dt=F32):
            return ctx.enter_context(nc.sbuf_tensor(name, shape, dt))

        def sem(name):
            return ctx.enter_context(nc.semaphore(name))

        def psum(name, shape):
            return ctx.enter_context(nc.psum_tensor(name, shape, F32))

        wb = sb("wb2", [P, D])
        u2 = sb("u2", [P, 2, D])
        uT = sb("u2T", [P, 2, KD, P])
        wr = sb("wr", [P, KD, NL])
        biasb = sb("biasb", [P, NL])
        junk = sb("junk2", [P, D])
        ident = sb("ident2", [P, P])
        ones = sb("ones2", [P, P])
        below = sb("below", [P, P])
        stats = sb("stats", [P, 4, NT])
        mhalf = sb("mhalf2", [P, NT])
        iota_e = sb("iota_e", [P, NE])
        rev_e = sb("rev_e", [P, NE])
        iota_b = sb("iota_b", [P, MAXB])
        iota_p = sb("iota_p", [P, P])
        thr = sb("thr", [P, NTH])
        toki = sb("toki", [P, NT])
        lg = sb("lg", [P, NT, NL])
        el = sb("el", [P, NT, NE])
        ta = sb("ta", [P, NT, NE])
        tb = sb("tb", [P, NT, NE])
        M = sb("M", [P, 2, NT, NE])
        A = sb("A", [P, NT, NE])
        pre = sb("pre", [P, NT + 1, NE])
        gs = sb("gs", [P, NT, EG])
        g1 = sb("g1", [P, NT, EG])
        g2 = sb("g2", [P, NT, EG])
        s8 = sb("s8", [P, 16, NT])
        cmp = sb("cmp", [P, NE * NE])
        extra = sb("extra", [P, NE])
        scan = sb("scan2", [P, 2, 16 + NE])
        start = sb("start", [P, NE])
        hot = sb("hot", [P, 2, P])
        vals = sb("vals", [P, 2, 2, MAXB])
        ef = sb("ef", [P, MAXB])
        nf = sb("nf", [P, 2])

        tp = [psum(f"tp2_{j}", [P, 4, P]) for j in range(4)]
        lg_ps = psum("lg_ps", [P, NT, NL])
        rank_ps = psum("rank_ps", [P, NT, NE])
        cnt_ps = psum("cnt_ps", [P, NE])
        tab_ps = psum("tab_ps", [P, 2, MAXB])

        loaded = sem("loaded2")
        const_steps = sem("const_steps2")
        sumsq = sem("sumsq2")
        ms_done = sem("ms_done2")
        rs_done = sem("rs_done2")
        u_done = sem("u_done2")
        u_stored = [sem(f"u_stored{j}") for j in range(2)]
        turned = sem("turned2")
        uT_done = sem("uT_done2")
        logits = sem("logits")
        steps = sem("steps2")
        act_exp = sem("act_exp2")
        rank_mm = sem("rank_mm")
        hot_done = sem("hot_done")
        tab_mm = sem("tab_mm")

        block = ctx.enter_context(nc.Block())

        @block.sync
        def _(sp):
            sp.dma_start(wb[:], norm_w.partition_broadcast(P)).then_inc(loaded, 16)
            sp.dma_start(wr[:, :, 0:EG], w_group.rearrange("(k p) n -> p k n", p=P)).then_inc(loaded, 16)
            sp.dma_start(wr[:, :, EG:NL], w_expert.rearrange("(k p) n -> p k n", p=P)).then_inc(loaded, 16)
            sp.dma_start(biasb[:, 0:EG], b_group.partition_broadcast(P)).then_inc(loaded, 16)
            sp.dma_start(biasb[:, EG:NL], b_expert.partition_broadcast(P)).then_inc(loaded, 16)
            ud = u2_dram.rearrange("(i p) d -> p i d", p=P)
            for i in range(NT):
                sp.wait_ge(u_done, i + 1)
                sp.dma_start(ud[:, i, :], u2[:, i % 2, :]).then_inc(u_stored[i % 2], 16)
            for j in range(2):
                sp.wait_ge(u_stored[j], 16 * NT // 2)

        @block.gpsimd
        def _(pool):
            g = nc.gpsimd
            g.memset(ident[:], 0.0).then_inc(const_steps, 1)
            g.memset(below[:], 1.0).then_inc(const_steps, 1)
            g.memset(ones[:], 1.0).then_inc(const_steps, 1)
            g.memset(mhalf[:], -0.5).then_inc(const_steps, 1)
            g.memset(pre[:, 0, :], 0.0).then_inc(const_steps, 1)
            g.memset(scan[:], 0.0).then_inc(const_steps, 1)
            exact = dict(allow_small_or_imprecise_dtypes=True)
            g.iota(iota_e[:], pattern=[[1, NE]], base=0, channel_multiplier=0, **exact).then_inc(const_steps, 1)
            g.iota(rev_e[:], pattern=[[-1, NE]], base=NE, channel_multiplier=0, **exact).then_inc(const_steps, 1)
            g.iota(iota_b[:], pattern=[[1, MAXB]], base=0, channel_multiplier=0, **exact).then_inc(const_steps, 1)
            g.iota(iota_p[:], pattern=[[1, P]], base=0, channel_multiplier=0, **exact).then_inc(const_steps, 1)
            g.iota(thr[:], pattern=[[P, NTH]], base=P, channel_multiplier=0, **exact).then_inc(const_steps, 1)
            g.iota(toki[:], pattern=[[P, NT]], base=0, channel_multiplier=1, **exact).then_inc(const_steps, 1)
            pool.wait_ge(const_steps, 12)
            g.affine_select(out=ident[:], in_=ident[:], compare_op=ALU.not_equal, fill=1.0, base=0,
                            pattern=[[-1, P]], channel_multiplier=1).then_inc(const_steps, 1)
            g.affine_select(out=below[:], in_=below[:], compare_op=ALU.is_gt, fill=0.0, base=0,
                            pattern=[[1, P]], channel_multiplier=-1).then_inc(const_steps, 1)
            for i in range(NT):
                pool.wait_ge(ms_done, i + 1)
                g.tensor_tensor(stats[:, 2, i:i + 1], stats[:, 1, i:i + 1], mhalf[:, i:i + 1], ALU.pow
                                ).then_inc(rs_done, 1)

        @block.scalar
        def _(act):
            for i in range(NT):
                if i >= 1:
                    act.wait_ge(sumsq, i)
                nc.scalar.activation(junk[:], hacc[:, i, :], ACT.Square, accum_out=stats[:, 0, i:i + 1]
                                     ).then_inc(sumsq, 1)
            for i in range(NT):
                for j in range(2):
                    act.wait_ge(turned, 2 * i + j + 1)
                    if i >= 2:
                        act.wait_ge(logits, i - 1)
                    nc.scalar.activation(uT[:, i % 2, 4 * j:4 * j + 4, :], tp[2 * (i % 2) + j][:], ACT.Copy
                                         ).then_inc(uT_done, 1)
            act.wait_ge(steps, 7)
            nc.scalar.activation(g2[:], g1[:], ACT.Exp).then_inc(act_exp, 1)
            act.wait_ge(steps, 24)
            nc.scalar.activation(s8[:, 7, :], s8[:, 6, :], ACT.Exp).then_inc(act_exp, 1)

        @block.tensor
        def _(pe):
            pe.wait_ge(const_steps, 14)
            pe.wait_ge(loaded, 16 * 5)

            def logits_of(i):
                pe.wait_ge(uT_done, 2 * i + 2)
                for k in range(KD):
                    mm = nc.tensor.matmul(lg_ps[:, i, :], uT[:, i % 2, k, :], wr[:, k, :], start=(k == 0), stop=(k == KD - 1))
                mm.then_inc(logits, 1)

            for i in range(NT):
                pe.wait_ge(u_done, i + 1)
                if i >= 2:
                    pe.wait_ge(uT_done, 2 * (i - 1))
                for j in range(2):
                    for k in range(4):
                        col = (4 * j + k) * P
                        mm = nc.tensor.transpose(tp[2 * (i % 2) + j][:, k, :], u2[:, i % 2, col:col + P], ident[:])
                    mm.then_inc(turned, 1)
                if i >= 1:
                    logits_of(i - 1)
            logits_of(NT - 1)
            pe.wait_ge(steps, 29 + NT)
            flat = "p i e -> p (i e)"
            nc.tensor.matmul(rank_ps[:].rearrange(flat), below[:], A[:].rearrange(flat), start=True, stop=False)
            nc.tensor.matmul(rank_ps[:].rearrange(flat), ones[:], pre[:, 0:NT, :].rearrange(flat), start=False, stop=True)
            nc.tensor.matmul(cnt_ps[:], ones[:], pre[:, NT, :], start=True, stop=True).then_inc(rank_mm, 1)
            for n in range(2 * NT):
                pe.wait_ge(hot_done, 3 * (n + 1))
                nc.tensor.matmul(tab_ps[:].rearrange("p v b -> p (v b)"), hot[:, n % 2, :],
                                 vals[:, n % 2].rearrange("p v b -> p (v b)"), start=(n == 0), stop=(n == 2 * NT - 1)
                                 ).then_inc(tab_mm, 1)

        @block.vector
        def _(dve):
            vec = nc.vector
            for i in range(NT):
                dve.wait_ge(sumsq, i + 1)
                vec.tensor_scalar(stats[:, 1, i:i + 1], stats[:, 0, i:i + 1], 1.0 / D, EPS, ALU.mult, ALU.add
                                  ).then_inc(ms_done, 1)
            dve.wait_ge(loaded, 16 * 5)
            for i in range(NT):
                dve.wait_ge(rs_done, i + 1)
                if i >= 2:
                    dve.wait_ge(turned, 2 * (i - 1))
                    dve.wait_ge(u_stored[i % 2], 16 * (i // 2))
                vec.scalar_tensor_tensor(u2[:, i % 2, :], hacc[:, i, :], stats[:, 2, i:i + 1], wb[:], ALU.mult, ALU.mult
                                         ).then_inc(u_done, 1)
            count = [0]

            def link(ins):
                count[0] += 1
                ins.then_inc(steps, 1)
                dve.wait_ge(steps, count[0])

            def over(ap, n):
                return ap.unsqueeze(2).to_broadcast([P, NT, n])

            def each(ap, n):
                return ap.unsqueeze(1).to_broadcast([P, NT, n])

            dve.wait_ge(const_steps, 14)
            dve.wait_ge(logits, NT)
            link(vec.tensor_tensor(lg[:], lg_ps[:], each(biasb[:], NL), ALU.add))
            gl = lg[:, :, 0:EG]
            link(vec.tensor_reduce(s8[:, 0, :], gl, AX.X, ALU.max))
            link(vec.tensor_tensor(g1[:], gl, over(s8[:, 0, :], EG), ALU.is_ge))
            link(vec.tensor_tensor(g1[:], g1[:], each(rev_e[:, NE - EG:NE], EG), ALU.mult))
            link(vec.tensor_reduce(s8[:, 1, :], g1[:], AX.X, ALU.max))
            link(vec.tensor_tensor(gs[:], each(rev_e[:, NE - EG:NE], EG), over(s8[:, 1, :], EG), ALU.is_equal))
            link(vec.tensor_tensor(g1[:], gl, over(s8[:, 0, :], EG), ALU.subtract))
            dve.wait_ge(act_exp, 1)
            link(vec.tensor_reduce(s8[:, 2, :], g2[:], AX.X, ALU.add))
            link(vec.reciprocal(s8[:, 3, :], s8[:, 2, :]))
            link(vec.tensor_scalar(g1[:], gs[:], 1e30, -1e30, ALU.mult, ALU.add))
            for g in range(EG):
                q = slice(g * EPG, (g + 1) * EPG)
                link(vec.tensor_tensor(el[:, :, q], lg[:, :, EG + g * EPG:EG + (g + 1) * EPG],
                                       over(gs[:, :, g], EPG), ALU.mult))
            pen = g1[:].rearrange("p i g -> p (i g)").unsqueeze(2).to_broadcast([P, NT * EG, EPG])
            ev = el[:].rearrange("p i (g e) -> p (i g) e", g=EG)
            link(vec.tensor_tensor(ev, ev, pen, ALU.add))

            def top(n, mx, first):
                link(vec.tensor_reduce(s8[:, mx, :], el[:], AX.X, ALU.max))
                link(vec.tensor_tensor(ta[:], el[:], over(s8[:, mx, :], NE), ALU.is_ge))
                link(vec.tensor_tensor(ta[:], ta[:], each(rev_e[:], NE), ALU.mult))
                link(vec.tensor_reduce(s8[:, first, :], ta[:], AX.X, ALU.max))
                link(vec.tensor_tensor(M[:, n], each(rev_e[:], NE), over(s8[:, first, :], NE), ALU.is_equal))

            top(0, 4, 5)
            fl = "p i e -> p (i e)"
            link(vec.scalar_tensor_tensor(el[:].rearrange(fl), M[:, 0].rearrange(fl), -3e30, el[:].rearrange(fl),
                                          ALU.mult, ALU.add))
            link(vec.tensor_reduce(s8[:, 6, :], el[:], AX.X, ALU.max))
            link(vec.tensor_copy(s8[:, 8, :], s8[:, 6, :]))
            link(vec.tensor_tensor(s8[:, 6, :], s8[:, 6, :], s8[:, 4, :], ALU.subtract))
            link(vec.tensor_tensor(ta[:], el[:], over(s8[:, 8, :], NE), ALU.is_ge))
            link(vec.tensor_tensor(ta[:], ta[:], each(rev_e[:], NE), ALU.mult))
            link(vec.tensor_reduce(s8[:, 9, :], ta[:], AX.X, ALU.max))
            link(vec.tensor_tensor(M[:, 1], each(rev_e[:], NE), over(s8[:, 9, :], NE), ALU.is_equal))
            link(vec.tensor_tensor(A[:], M[:, 0], M[:, 1], ALU.add))
            for i in range(NT):
                link(vec.tensor_tensor(pre[:, i + 1, :], pre[:, i, :], A[:, i, :], ALU.add))
            dve.wait_ge(act_exp, 2)
            link(vec.tensor_scalar(s8[:, 10, :], s8[:, 7, :], 1.0, None, ALU.add))
            link(vec.reciprocal(s8[:, 10, :], s8[:, 10, :]))
            link(vec.tensor_tensor(wtok[:, 0, :], s8[:, 3, :], s8[:, 10, :], ALU.mult))
            link(vec.tensor_tensor(wtok[:, 1, :], wtok[:, 0, :], s8[:, 7, :], ALU.mult))
            dve.wait_ge(rank_mm, 1)
            c3 = cmp[:, 0:NE * NTH].rearrange("p (e j) -> p e j", e=NE)
            link(vec.tensor_tensor(c3, cnt_ps[:].unsqueeze(2).to_broadcast([P, NE, NTH]),
                                   thr[:].unsqueeze(1).to_broadcast([P, NE, NTH]), ALU.is_gt))
            link(vec.tensor_reduce(extra[:], c3, AX.X, ALU.add))
            link(vec.tensor_copy(scan[:, 0, 16:16 + NE], extra[:]))
            for n in range(5):
                a, b = scan[:, n % 2, :], scan[:, (n + 1) % 2, :]
                link(vec.tensor_tensor(b[:, 16:16 + NE], a[:, 16:16 + NE], a[:, 16 - (1 << n):16 + NE - (1 << n)], ALU.add))
            incl = scan[:, 1, 16:16 + NE]
            link(vec.tensor_tensor(start[:], incl, extra[:], ALU.subtract))
            link(vec.tensor_copy(ef[:], iota_b[:]))
            c3 = cmp[:, 0:16 * NE].rearrange("p (j e) -> p j e", j=16)
            link(vec.tensor_tensor(c3, incl.unsqueeze(1).to_broadcast([P, 16, NE]),
                                   iota_b[:, 0:16].unsqueeze(2).to_broadcast([P, 16, NE]), ALU.is_le))
            link(vec.tensor_reduce(ef[:, NE:NE + 16], c3, AX.X, ALU.add))
            link(vec.tensor_scalar(ef[:], ef[:], float(NE - 1), None, ALU.min))
            link(vec.tensor_copy(etab[:], ef[:]))
            link(vec.tensor_scalar(cmp[:, 0:8], iota_b[:, 0:8], 2.0, incl[:, NE - 1:NE], ALU.mult, ALU.is_lt))
            link(vec.tensor_reduce(nf[:, 0:1], cmp[:, 0:8], AX.X, ALU.add))
            link(vec.tensor_scalar(npairs[:, 0:1], nf[:, 0:1], float(NE // 2), None, ALU.add))
            link(vec.tensor_scalar(npairs[:, 1:2], nf[:, 0:1], float(NE // 2 - 1), None, ALU.add))
            for k in range(2):
                for table, at in ((rank_ps[:], 0), (each(iota_e[:], NE), 1), (each(start[:], NE), 2)):
                    link(vec.tensor_tensor(tb[:], M[:, k], table, ALU.mult))
                    link(vec.tensor_reduce(s8[:, at, :], tb[:], AX.X, ALU.add))
                c3 = cmp[:, 0:NT * NTH].rearrange("p (i j) -> p i j", i=NT)
                link(vec.tensor_tensor(c3, over(s8[:, 0, :], NTH), each(thr[:], NTH), ALU.is_ge))
                link(vec.tensor_reduce(s8[:, 4, :], c3, AX.X, ALU.add))
                link(vec.scalar_tensor_tensor(s8[:, 11 + 2 * k, :], s8[:, 4, :], -float(P), s8[:, 0, :],
                                              ALU.mult, ALU.add))
                link(vec.tensor_tensor(s8[:, 5, :], s8[:, 2, :], s8[:, 4, :], ALU.add))
                link(vec.tensor_tensor(s8[:, 5, :], s8[:, 5, :], s8[:, 1, :], ALU.subtract))
                link(vec.tensor_scalar(s8[:, 5, :], s8[:, 5, :], float(NE - 1), None, ALU.add))
                link(vec.tensor_scalar(s8[:, 6, :], s8[:, 4, :], 0.0, None, ALU.is_gt))
                link(vec.tensor_tensor(s8[:, 5, :], s8[:, 5, :], s8[:, 6, :], ALU.mult))
                link(vec.tensor_tensor(s8[:, 12 + 2 * k, :], s8[:, 5, :], s8[:, 1, :], ALU.add))
            link(vec.tensor_scalar(stats[:, 0, :], toki[:], -PADROW, None, ALU.add))
            link(vec.tensor_scalar(stats[:, 1, :], toki[:], 2.0, -PADROW, ALU.mult, ALU.add))
            link(vec.tensor_scalar(stats[:, 2, :], toki[:], 2.0, 1.0 - PADROW, ALU.mult, ALU.add))
            for n in range(2 * NT):
                k, i = n // NT, n % NT
                if n >= 2:
                    dve.wait_ge(tab_mm, n - 1)
                vec.tensor_scalar(hot[:, n % 2, :], iota_p[:], s8[:, 11 + 2 * k, i:i + 1], None, ALU.is_equal
                                  ).then_inc(hot_done, 1)
                for q, src in enumerate((0, 1 + k)):
                    vec.tensor_scalar(vals[:, n % 2, q, :], iota_b[:], s8[:, 12 + 2 * k, i:i + 1], stats[:, src, i:i + 1],
                                      ALU.is_equal, ALU.mult).then_inc(hot_done, 1)
            dve.wait_ge(tab_mm, 2 * NT)
            link(vec.tensor_scalar(ridx[:], tab_ps[:], PADROW, None, ALU.add))


def experts(nc, hacc, ridx, etab, npairs, wtok, w_gate, w_up, w_down, u2_dram, y_dram, out):
    _, D, FF = w_gate.shape
    KD = D // P
    KF = FF // P
    NT = hacc.shape[1]
    T = NT * P
    NPC = 12

    with ExitStack() as ctx:
        def sb(name, shape, dt=F32):
            return ctx.enter_context(nc.sbuf_tensor(name, shape, dt))

        def sem(name):
            return ctx.enter_context(nc.semaphore(name))

        def psum(name, shape):
            return ctx.enter_context(nc.psum_tensor(name, shape, F32))

        wg = sb("wg", [P, 2, KD, FF])
        wu = sb("wu", [P, 2, KD, FF])
        wd = sb("wd", [P, 2, KF, D])
        xg = sb("xg", [P, 2, D])
        xT = sb("xT", [P, 2, KD, P])
        hid = sb("hid", [P, FF])
        hT = sb("hT", [P, 2, KF, P])
        yb = sb("yb", [P, 2, D])
        gidx = sb("gidx", [P, 2, 1], I32)
        sidx = sb("sidx", [P, 2, 1], I32)
        zero = sb("zero", [P, 1], I32)
        gtmp = sb("gtmp", [P, 2, 1], I32)
        stmp = sb("stmp", [P, 2, 1], I32)
        ident = sb("ident3", [P, P])
        tp = [psum(f"tp3_{j}", [P, 4, P]) for j in range(2)]
        g_ps = psum("g_ps", [P, FF])
        u_ps = psum("u_ps", [P, FF])
        hT_ps = psum("hT_ps", [P, KF, P])
        y_ps = [psum(f"y3_{j}", [P, 512]) for j in range(2)]
        y2 = wg[:].rearrange("p a k f -> p (a k f)").rearrange("p (s c d) -> p s c d", s=4, c=2)

        w_loaded = [[sem(f"w_loaded{b}_{j}") for j in range(NPC)] for b in range(2)]
        gu_used = sem("gu_used")
        d_used = sem("d_used")
        const_steps = sem("const_steps3")
        gidx_done = sem("gidx_done")
        sidx_done = sem("sidx_done")
        gathered = [sem(f"gathered{b}") for b in range(2)]
        scattered = [sem(f"scattered{b}") for b in range(2)]
        turned = sem("turned3")
        xT_done = sem("xT_done3")
        g_mm = sem("g_mm")
        u_mm = sem("u_mm")
        silu_done = sem("silu_done")
        hid_done = sem("hid_done")
        hT_mm = sem("hT_mm")
        hT_done = sem("hT_done3")
        y_mm = sem("y_mm3")
        y_done = sem("y_done3")
        y2_loaded = [sem(f"y2_loaded{j}") for j in range(4)]
        comb = sem("comb")
        out_stored = sem("out_stored")

        def val(p, b, per, add):
            return (2 * p + b) * per + add if isinstance(p, int) else p * (2 * per) + (b * per + add)

        def wait(eng, s, p, b, per, add):
            if isinstance(p, int) and val(p, b, per, add) <= 0:
                return
            eng.wait_ge(s, val(p, b, per, add))

        def pairs(eng, body):
            n = eng.value_load(npairs[0:1, 0:1], min_val=NE // 2, max_val=NE // 2 + 8)
            body(0)
            with eng.Fori(1, n) as p:
                body(p)
            return n

        def last_pair(eng):
            return eng.value_load(npairs[0:1, 1:2], min_val=NE // 2 - 1, max_val=NE // 2 + 7)

        block = ctx.enter_context(nc.Block())

        @block.sync
        def _(sp):
            def body(p):
                for b in range(2):
                    if isinstance(p, int):
                        e = b
                    else:
                        e = sp.value_load(etab[0:1, bass.ds(p * 2 + b, 1)], min_val=0, max_val=NE - 1)
                    for j in range(NPC):
                        n = j % 4
                        if j < 6:
                            wait(sp, gu_used, p, b, 6, j + 1 - 12)
                        elif j < 8:
                            wait(sp, (g_mm, u_mm)[j % 2], p, b, 1, -1)
                        elif n < 3:
                            wait(sp, d_used, p, b, 3, n + 1 - 6)
                        else:
                            wait(sp, y_mm, p, b, 2, -2)
                        if j < 8:
                            n = j // 2
                            src, dst = ((w_gate, wg), (w_up, wu))[j % 2]
                            src = src[bass.ds(e, 1)].rearrange("e (p k) f -> p (e k) f", p=P)[:, 2 * n:2 * n + 2, :]
                            dst = dst[:, b, 2 * n:2 * n + 2, :]
                        else:
                            src = w_down[bass.ds(e, 1)].rearrange("e (p k) d -> p (e k) d", p=P)[:, n:n + 1, :]
                            dst = wd[:, b, n:n + 1, :]
                        sp.dma_start(dst, src).then_inc(w_loaded[b][j], 16)

            n = pairs(sp, body)
            for b in range(2):
                sp.wait_ge(scattered[b], n * 16)
            yv = y_dram.rearrange("(i p c) d -> p i c d", p=P, c=2)
            ov = out.rearrange("(i p) d -> p i d", p=P)
            for i in range(NT + 3):
                if i < NT:
                    if i >= 4:
                        sp.wait_ge(comb, 2 * (i - 3))
                    sp.dma_start(y2[:, i % 4], yv[:, i]).then_inc(y2_loaded[i % 4], 16)
                if i >= 3:
                    sp.wait_ge(comb, 2 * (i - 2))
                    sp.dma_start(ov[:, i - 3, :], hacc[:, i - 3, :]).then_inc(out_stored, 16)
            sp.wait_ge(out_stored, 16 * NT)

        @block.gpsimd
        def _(pool):
            g = nc.gpsimd
            g.memset(ident[:], 0.0).then_inc(const_steps, 1)
            g.memset(xg[:], 0.0).then_inc(const_steps, 1)
            g.memset(zero[:], 0).then_inc(const_steps, 1)
            pool.wait_ge(const_steps, 3)
            g.affine_select(out=ident[:], in_=ident[:], compare_op=ALU.not_equal, fill=1.0, base=0,
                            pattern=[[-1, P]], channel_multiplier=1).then_inc(const_steps, 1)

            last_token, last_row = pool.to_reg(T - 1), pool.to_reg(2 * T - 1)

            def gather(p, b, ahead):
                par = (b + ahead) % 2
                B = 2 * p + b + ahead if isinstance(p, int) else p * 2 + (b + ahead)
                wait(pool, turned, p, b, 2, 2 * (ahead - 1))
                g.tensor_copy(gtmp[:, par, :], ridx[:, 0, bass.ds(B, 1)]).then_inc(gidx_done, 1)
                wait(pool, gidx_done, p, b, 1, ahead + 1)
                g.tensor_tensor(gidx[:, par, :], gtmp[:, par, :], zero[:], ALU.add).then_inc(const_steps, 1)
                g.drain()
                g.indirect_dma_start(xg[:, par, :], None, u2_dram,
                                     bass.IndirectOffsetOnAxis(gidx[:, par, :].bitcast(U32), 0),
                                     bounds_check=last_token, oob_is_err=False).then_inc(gathered[par], 16)

            def scatter(p, b):
                B = 2 * p + b if isinstance(p, int) else p * 2 + b
                if not (isinstance(p, int) and p == 0):
                    pool.wait_ge(scattered[b], val(p, 0, 8, 0))
                g.tensor_copy(stmp[:, b, :], ridx[:, 1, bass.ds(B, 1)]).then_inc(sidx_done, 1)
                wait(pool, sidx_done, p, b, 1, 1)
                wait(pool, y_done, p, b, 2, 2)
                g.tensor_tensor(sidx[:, b, :], stmp[:, b, :], zero[:], ALU.add).then_inc(const_steps, 1)
                g.drain()
                g.indirect_dma_start(y_dram, bass.IndirectOffsetOnAxis(sidx[:, b, :].bitcast(U32), 0), yb[:, b, :], None,
                                     bounds_check=last_row, oob_is_err=False).then_inc(scattered[b], 16)

            def body(p):
                gather(p, 1, 2)
                scatter(p, 0)
                gather(p, 2, 2)
                scatter(p, 1)

            for ahead in range(3):
                gather(0, 0, ahead)
            n = pairs(pool, body)
            pool.wait_ge(gathered[0], n * 16 + 32)
            pool.wait_ge(gathered[1], n * 16 + 16)

        @block.scalar
        def _(act):
            def turn_x(p, b, ahead):
                par = (b + ahead) % 2
                for j in range(2):
                    wait(act, turned, p, b, 2, 2 * ahead + j + 1)
                    if j == 0:
                        wait(act, u_mm, p, b, 1, ahead - 1)
                    nc.scalar.activation(xT[:, par, 4 * j:4 * j + 4, :], tp[j][:], ACT.Copy).then_inc(xT_done, 1)

            def body(p):
                for b in range(2):
                    wait(act, g_mm, p, b, 1, 1)
                    wait(act, hT_mm, p, b, 1, 0)
                    nc.scalar.activation(hid[:], g_ps[:], ACT.Silu).then_inc(silu_done, 1)
                    turn_x(p, b, 1)

            turn_x(0, 0, 0)
            pairs(act, body)

        @block.tensor
        def _(pe):
            pe.wait_ge(const_steps, 4)

            def turn_x(p, b, ahead):
                par = (b + ahead) % 2
                pe.wait_ge(gathered[par], val(p, 0, 8, 16 + 16 * ((b + ahead) // 2)))
                wait(pe, xT_done, p, b, 2, 2 * ahead)
                xk = xg[:, par, :].rearrange("p (q k) -> p k q", k=KD)
                for j in range(2):
                    for k in range(4):
                        mm = nc.tensor.transpose(tp[j][:, k, :], xk[:, 4 * j + k, :], ident[:])
                    mm.then_inc(turned, 1)

            def loaded(p, b, j):
                pe.wait_ge(w_loaded[b][j], val(p, 0, 8, 16))

            def gate_up(p, b):
                wait(pe, xT_done, p, b, 2, 2)
                wait(pe, silu_done, p, b, 1, 0)
                wait(pe, hid_done, p, b, 1, 0)
                for n in range(4):
                    for w, ps, j in ((wg, g_ps, 2 * n), (wu, u_ps, 2 * n + 1)):
                        loaded(p, b, j)
                        for k in (2 * n, 2 * n + 1):
                            mm = nc.tensor.matmul(ps[:], xT[:, b, k, :], w[:, b, k, :], start=(k == 0), stop=(k == KD - 1))
                        mm.then_inc(gu_used if n < 3 else (g_mm if w is wg else u_mm), 1)

            def turn_hid(p, b):
                wait(pe, hid_done, p, b, 1, 1)
                wait(pe, hT_done, p, b, 1, 0)
                hk = hid[:].rearrange("p (q k) -> p k q", k=KF)
                for k in range(KF):
                    mm = nc.tensor.transpose(hT_ps[:, k, :], hk[:, k, :], ident[:])
                mm.then_inc(hT_mm, 1)

            def down(p, b):
                wait(pe, hT_done, p, b, 1, 1)
                for k in range(KF):
                    loaded(p, b, 8 + k)
                    for j in range(2):
                        if k == 0:
                            wait(pe, y_done, p, b, 2, j - 1)
                        mm = nc.tensor.matmul(y_ps[j][:], hT[:, b, k, :], wd[:, b, k, j * 512:(j + 1) * 512],
                                              start=(k == 0), stop=(k == KF - 1))
                        if k == KF - 1:
                            mm.then_inc(y_mm, 1)
                    if k < KF - 1:
                        mm.then_inc(d_used, 1)

            def body(p):
                for b in range(2):
                    gate_up(p, b)
                    if b == 1:
                        down(p, 0)
                    elif not isinstance(p, int):
                        down(p + (-1), 1)
                    turn_hid(p, b)
                    turn_x(p, b, 1)

            turn_x(0, 0, 0)
            n = pairs(pe, body)
            down(last_pair(pe), 1)

        @block.vector
        def _(dve):
            vec = nc.vector

            def y_out(p, b):
                wait(dve, sidx_done, p, b, 1, 1)
                for j in range(2):
                    wait(dve, y_mm, p, b, 2, j + 1)
                    vec.tensor_copy(yb[:, b, j * 512:(j + 1) * 512], y_ps[j][:]).then_inc(y_done, 1)

            def body(p):
                for b in range(2):
                    wait(dve, silu_done, p, b, 1, 1)
                    wait(dve, u_mm, p, b, 1, 1)
                    vec.tensor_tensor(hid[:], hid[:], u_ps[:], ALU.mult).then_inc(hid_done, 1)
                    if b == 1:
                        y_out(p, 0)
                    elif not isinstance(p, int):
                        q = p + (-1)
                        y_out(q, 1)
                    wait(dve, hT_mm, p, b, 1, 1)
                    wait(dve, y_mm, p, b, 2, -2)
                    vec.tensor_copy(hT[:, b], hT_ps[:]).then_inc(hT_done, 1)

            n = pairs(dve, body)
            y_out(last_pair(dve), 1)
            for i in range(NT):
                dve.wait_ge(y2_loaded[i % 4], 16 * (i // 4 + 1))
                for c in range(2):
                    if c:
                        dve.wait_ge(comb, 2 * i + 1)
                    vec.scalar_tensor_tensor(hacc[:, i, :], y2[:, i % 4, c, :], wtok[:, c, i:i + 1], hacc[:, i, :],
                                             ALU.mult, ALU.add).then_inc(comb, 1)


def layer(nc, x, norm_mix, norm_ffn, ssd_w_in, ssd_conv_w, ssd_conv_b, ssd_dt_bias, ssd_a_log, ssd_d, ssd_norm,
          ssd_w_out, moe_w_group, moe_b_group, moe_w_expert, moe_b_expert, moe_w_gate, moe_w_up, moe_w_down, out):
    T, D = x.shape[1:]
    with ExitStack() as ctx:
        hacc = ctx.enter_context(nc.sbuf_tensor("hacc", [P, T // P, D], F32))
        ridx = ctx.enter_context(nc.sbuf_tensor("ridx", [P, 2, MAXB], I32))
        etab = ctx.enter_context(nc.sbuf_tensor("etab", [P, MAXB], I32))
        npairs = ctx.enter_context(nc.sbuf_tensor("npairs", [P, 2], I32))
        wtok = ctx.enter_context(nc.sbuf_tensor("wtok", [P, 2, T // P], F32))
        acum_dram = nc.dram_tensor("acum_dram", [GROUPS * R * (T // P), P], F32).ap()
        u2_dram = nc.dram_tensor("u2_dram", [T, D], F32).ap()
        y_dram = nc.dram_tensor("y_dram", [2 * T, D], F32).ap()
        mamba(nc, hacc, x[0], norm_mix[0], ssd_w_in[0], ssd_conv_w[0], ssd_conv_b[0], ssd_dt_bias[0], ssd_a_log[0],
              ssd_d[0], ssd_norm[0], ssd_w_out[0], acum_dram)
        routing(nc, hacc, ridx, etab, npairs, wtok, norm_ffn[0], moe_w_group[0], moe_b_group[0], moe_w_expert[0],
                moe_b_expert[0], u2_dram)
        experts(nc, hacc, ridx, etab, npairs, wtok, moe_w_gate[0], moe_w_up[0], moe_w_down[0], u2_dram, y_dram, out[0])


_INS = ["x", "norm_mix", "norm_ffn", "ssd_w_in", "ssd_conv_w", "ssd_conv_b", "ssd_dt_bias", "ssd_a_log", "ssd_d",
        "ssd_norm", "ssd_w_out", "moe_w_group", "moe_b_group", "moe_w_expert", "moe_b_expert", "moe_w_gate",
        "moe_w_up", "moe_w_down"]
_OUTS = [((1, 1024, 1024), "float32")]


def kernel(**inputs):
    import numpy as _np
    import concourse.bacc as _bacc
    from concourse import mybir as _mybir
    from concourse.bass_utils import run_bass_kernel_spmd as _run

    nc = _bacc.Bacc("TRN2", target_bir_lowering=False, num_devices=1)
    arrays, args = {}, []
    for name in _INS:
        a = _np.ascontiguousarray(inputs[name])
        arrays[f"in_{name}_dram"] = a
        args.append(nc.dram_tensor(f"in_{name}_dram", a.shape, _mybir.dt.from_np(a.dtype), kind="ExternalInput").ap())
    for i, (shape, dtype) in enumerate(_OUTS):
        dt = _mybir.dt.from_np(_np.dtype(dtype))
        args.append(nc.dram_tensor(f"out_{i}_dram", shape, dt, kind="ExternalOutput").ap())
    layer(nc, *args)
    r = _run(nc, [arrays], core_ids=[0])
    return r.results[0]["out_0_dram"]
```

```python
from contextlib import ExitStack

import concourse.bass as bass
from concourse import mybir

ALU = mybir.AluOpType
ACT = mybir.ActivationFunctionType
AX = mybir.AxisListType
F32 = mybir.dt.float32
F32R = mybir.dt.float32r
I32 = mybir.dt.int32
U32 = mybir.dt.uint32

P = 128
EPS = 1e-6
HEAD_DIM = 64
GROUPS = 8
R = 4
STATE = 128
TAPS = 4
GCH = R * HEAD_DIM
TILES = 6
HALF = 512
UNITS = [(0, 0), (0, 1), (1, 0), (1, 1), (2, 0), (2, 1), (3, 0), (3, 1), (4, 0), (5, 0), (4, 1), (5, 1)]
NU = len(UNITS)
PLAN = {1: [11, NU + 0], 2: [NU + 1], 3: [NU + 2, NU + 3], 4: [NU + 4], 5: [NU + 5, NU + 6],
        6: [NU + 7], 7: [NU + 8, NU + 9], 8: [NU + 10]}
CYCLE = 16
FIRST_PIECES = 2 * TILES
EARLY = {1: [("wo", 2), ("wo", 3), ("wo", 4), ("wo", 5)], 4: [(3, 10), (3, 11)], 6: [(4, 12), (4, 13)],
         7: [(5, 14), (5, 15)]}
LATE = {1: [(1, 6), (1, 7)], 2: [(2, 8), (2, 9)], 8: [(0, 16), (0, 17)]}
TILE_PLACE = [0, 6, 8, 10, 12, 14]
EG = 4
EPG = 8
NE = EG * EPG
MAXB = 52
PADROW = 8192.0


def bcast(ap, shape):
    return ap.to_broadcast(shape)


def mamba(nc, hacc, x, norm_w, w_in, conv_w, conv_b, dt_bias, a_log, d_skip, y_norm, w_out, acum_dram):
    T, D = x.shape
    KD = D // P
    NT = T // P
    NH = GROUPS * R
    DIN = GROUPS * GCH
    XBC = DIN
    DTC = XBC + DIN + 2 * GROUPS * STATE
    CT = (DIN + 2 * GROUPS * STATE) // P
    LASTG = GROUPS - 1

    with ExitStack() as ctx:
        def sb(name, shape, dt=F32):
            return ctx.enter_context(nc.sbuf_tensor(name, shape, dt))

        def sem(name):
            return ctx.enter_context(nc.semaphore(name))

        uTh = sb("uTh", [P, KD, T], F32R)
        uTl = sb("uTl", [P, KD, T], F32R)
        wh = sb("wh", [P, 2, KD, P], F32R)
        wl = sb("wl", [P, 2, KD, P], F32R)
        raw = sb("raw", [P, 2, 512])
        woh = sb("woh", [P, 2, D], F32R)
        wol = sb("wol", [P, 2, D], F32R)
        xr = sb("xr", [P, 2, 3 + HALF])
        v = sb("v", [P, HALF])
        xbc = sb("xbc", [P, 2, 4, T])
        zs = sb("zs", [P, 2, T])
        E = sb("E", [P, 2, R, P])
        xdt = sb("xdt", [P, 2, GCH])
        xds = sb("xds", [P, 2, GCH])
        btok = sb("btok", [P, 2, P])
        cbm = sb("cbm", [P, P])
        S = sb("S", [P, 2, GCH])
        ysb = sb("ysb", [P, GCH])
        ygf = sb("ygf", [P, 2, P])
        sq = sb("sq", [P, 2, P])
        yh = sb("yh", [P, 2, P], F32R)
        yl = sb("yl", [P, 2, P], F32R)
        ms = sb("ms", [P, 2])
        rstd = sb("rstd", [P, 2])
        dtT = sb("dtT", [P, GROUPS, NT, R])
        acum = sb("acum", [P, GROUPS, NT, R])
        eac = sb("eac", [P, GROUPS, NT, R])
        dst = sb("dst", [P, GROUPS, NT, R])
        dch = sb("dch", [P, GROUPS, NT, R])
        ident = sb("ident", [P, P])
        tri = sb("tri", [P, P])
        ones = sb("ones", [P, P])
        cw = sb("cw", [P, TAPS + 1, CT])
        dsk = sb("dsk", [P, 2 * GROUPS])
        nw = sb("nw", [P, 2 * GROUPS])
        alogb = sb("alogb", [P, NH])
        dtb = sb("dtb", [P, NH])
        ssq = sb("ssq", [P, NT])
        msx = sb("msx", [P, NT])
        rsx = sb("rsx", [P, NT])
        mhalf = sb("mhalf", [P, NT])

        junk, xn, wb = xbc[:, 1, 0, :], xbc[:, 1, 1:3, :], xbc[:, 1, 3, :]
        wdt, dtc = xbc[:, 0, 0, :], xbc[:, 0, 1, :]
        tmp = [zs[:, j // 4, 256 * (j % 4):256 * (j % 4) + 256] for j in range(8)]
        acs, rows, dall = sq, ygf, ysb[:, 0:NH]

        proj_ps = [ctx.enter_context(nc.psum_tensor(f"proj{j}", [P, 512], F32)) for j in range(2)]
        tcb_ps = [ctx.enter_context(nc.psum_tensor(f"tcb{j}", [P, 4, P], F32)) for j in range(2)]
        y_ps = ctx.enter_context(nc.psum_tensor("y_ps", [P, 2, GCH], F32))
        st_ps = ctx.enter_context(nc.psum_tensor("st_ps", [P, 2, GCH], F32))
        out_ps = [ctx.enter_context(nc.psum_tensor(f"out{j}", [P, 512], F32)) for j in range(2)]

        x_loaded = [sem(f"x_loaded{i}") for i in range(NT)]
        consts_loaded = sem("consts_loaded")
        wdt_loaded = sem("wdt_loaded")
        const_steps = sem("const_steps")
        rows_T = sem("rows_T")
        halved = sem("halved")
        sumsq_done = sem("sumsq_done")
        msx_done = sem("msx_done")
        rsx_done = sem("rsx_done")
        xn_done = sem("xn_done")
        xT_done = sem("xT_done")
        uhi_done = sem("uhi_done")
        ulo_done = sem("ulo_done")
        wd_hi = sem("wd_hi")
        wd_lo = sem("wd_lo")
        dt_mm = sem("dt_mm")
        dtc_done = sem("dtc_done")
        dtT_mm = sem("dtT_mm")
        dt_steps = sem("dt_steps")
        dt_act = sem("dt_act")
        cum_mm = sem("cum_mm")
        cum_act = sem("cum_act")
        acT_mm = sem("acT_mm")
        acT_sb = sem("acT_sb")
        acT_stored = sem("acT_stored")
        raw_loaded = [sem(f"raw_loaded{j}") for j in range(2)]
        w_hi = sem("w_hi")
        w_ready = sem("w_ready")
        proj_done = sem("proj_done")
        raw_copied = sem("raw_copied")
        halo_copied = sem("halo_copied")
        conv_steps = sem("conv_steps")
        tanh_done = sem("tanh_done")
        unit_final = sem("unit_final")
        tcb_done = sem("tcb_done")
        btok_done = sem("btok_done")
        xdt_steps = sem("xdt_steps")
        cbm_done = sem("cbm_done")
        e_loaded = [sem(f"e_loaded{j}") for j in range(2)]
        sub_steps = sem("sub_steps")
        exp_done = sem("exp_done")
        m_done = sem("m_done")
        y_mm = sem("y_mm")
        st_mm = sem("st_mm")
        y_steps = sem("y_steps")
        s_steps = sem("s_steps")
        yT_done = sem("yT_done")
        gate_steps = sem("gate_steps")
        sq_done = sem("sq_done")
        yhi_done = sem("yhi_done")
        ylo_done = sem("ylo_done")
        stat_mm = sem("stat_mm")
        ms_done = sem("ms_done")
        rstd_done = sem("rstd_done")
        out_mm = sem("out_mm")
        h_steps = sem("h_steps")

        def val(G, per, add):
            reg, off = G
            return off * per + add if reg is None else reg * (2 * per) + (off * per + add)

        def nxt(G, n=1):
            return (G[0], G[1] + n)

        def gidx(G):
            return val(G, 1, 0)

        def wait(eng, s, G, per, add):
            if G[0] is None and G[1] * per + add <= 0:
                return
            eng.wait_ge(s, val(G, per, add))

        def pick(ap, G):
            return ap[:, bass.ds(gidx(G), 1)] if G[0] is not None else ap[:, G[1]:G[1] + 1]

        def unit_of(G, i):
            return (nxt(G), i - NU) if i >= NU else (G, i)

        def first(G):
            return G[0] is None and G[1] == 0

        def is_last(G):
            return G[0] is None and G[1] == LASTG

        def steps(G):
            last = is_last(G)
            nolater = G[0] is None and G[1] >= LASTG - 1
            plan = {c: [i for i in PLAN[c] if not (last and i >= NU)] for c in PLAN}
            early = {c: [p for p in EARLY.get(c, []) if not (last and p[0] != "wo")] for c in PLAN}
            late = {c: [p for p in LATE.get(c, []) if not last and not (nolater and p[1] >= CYCLE)] for c in PLAN}
            if last:
                early[1] = [("wo", j) for j in range(4)]
            return plan, early, late

        def groups(eng, body):
            with eng.Fori(0, (GROUPS - 2) // 2) as i:
                body((i, 0))
                body((i, 1))
            body((None, LASTG - 1))
            body((None, LASTG))

        def unit_b(plan, c):
            return plan[c][1] if len(plan[c]) > 1 else None

        def piece_wait(eng, s, G, place, extra):
            wait(eng, s, G, CYCLE, FIRST_PIECES + place + extra)

        block = ctx.enter_context(nc.Block())

        @block.sync
        def _(sp):
            xt = x.rearrange("(i p) d -> p i d", p=P)
            for i in range(NT):
                sp.dma_start(hacc[:, i, :], xt[:, i, :]).then_inc(x_loaded[i], 16)
                if i == 0:
                    sp.dma_start(wb, norm_w.partition_broadcast(P)).then_inc(consts_loaded, 16)
                    sp.dma_start(dtb[:], dt_bias.partition_broadcast(P)).then_inc(consts_loaded, 16)
                    sp.dma_start(alogb[:], a_log.partition_broadcast(P)).then_inc(consts_loaded, 16)
                    sp.dma_start(dall, d_skip.partition_broadcast(P)).then_inc(consts_loaded, 16)
                    sp.dma_start(rows[:, 0, :], conv_w.rearrange("k (n p) -> (k n) p", p=P)).then_inc(consts_loaded, 16)
                    sp.dma_start(rows[0:CT, 1, :], conv_b.rearrange("(n p) -> n p", p=P)).then_inc(consts_loaded, 16)
                    sp.dma_start(rows[CT:CT + 2 * GROUPS, 1, :], y_norm.rearrange("(n p) -> n p", p=P)
                                 ).then_inc(consts_loaded, 16)
                    sp.dma_start(wdt.rearrange("p (k n) -> p k n", k=KD),
                                 w_in[:, DTC + NH - P:DTC + NH].rearrange("(k p) n -> p k n", p=P)).then_inc(wdt_loaded, 16)

            def column(G, t):
                if t < 2:
                    return val(G, GCH, XBC + t * P)
                if t < 4:
                    return val(G, STATE, XBC + DIN + (t - 2) * GROUPS * STATE)
                return val(G, GCH, (t - 4) * P)

            def load_tile_piece(G, t, half, slot):
                src = w_in[half * 4 * P:(half + 1) * 4 * P, bass.ds(column(G, t), P)].rearrange("(k p) n -> p k n", p=P)
                sp.dma_start(raw[:, slot, :].rearrange("p (k n) -> p k n", k=4), src).then_inc(raw_loaded[slot], 16)

            def load_piece(G, what, place):
                piece_wait(sp, w_ready, G, place, -1)
                if what == "wo":
                    j = place - (0 if is_last(G) else 2)
                    row = val(G, GCH, (j // 2) * P)
                    sp.dma_start(raw[:, place % 2, :], w_out[bass.ds(row, P), (j % 2) * 512:(j % 2) * 512 + 512]
                                 ).then_inc(raw_loaded[place % 2], 16)
                else:
                    load_tile_piece(nxt(G, 2) if place >= CYCLE else nxt(G), what, place % 2, place % 2)

            def load_e(G, c):
                wait(sp, y_mm, G, NT, c - 1)
                src = acum_dram[bass.ds(val(G, NT * R, c * R), R), :].rearrange("r l -> (r l)").partition_broadcast(P)
                sp.dma_start(E[:, c % 2].rearrange("p r l -> p (r l)"), src).then_inc(e_loaded[c % 2], 16)

            for p in range(FIRST_PIECES):
                if p >= 2:
                    sp.wait_ge(w_ready, p - 1)
                load_tile_piece((None, 0), p // 2, p % 2, p % 2)
            G0 = (None, 0)
            for j in range(2):
                sp.wait_ge(acT_sb, j + 1)
                sp.dma_start(acum_dram[j * P:(j + 1) * P, :], acs[:, j, :]).then_inc(acT_stored, 16)
            sp.wait_ge(acT_stored, 32)
            load_e(G0, 0)
            load_e(G0, 1)
            for half in range(2):
                sp.wait_ge(w_ready, FIRST_PIECES + half - 1)
                load_tile_piece((None, 1), 0, half, half)

            def body(G):
                plan, early, late = steps(G)
                last = is_last(G)
                for c in range(1, 9):
                    if c < NT - 1 or not last:
                        load_e(G, c + 1)
                    for what, place in early[c] + late[c]:
                        load_piece(G, what, place)

            groups(sp, body)

        @block.gpsimd
        def _(pool):
            nc.gpsimd.memset(ident[:], 0.0).then_inc(const_steps, 1)
            nc.gpsimd.memset(tri[:], 1.0).then_inc(const_steps, 1)
            nc.gpsimd.memset(ones[:], 1.0).then_inc(const_steps, 1)
            nc.gpsimd.memset(mhalf[:], -0.5).then_inc(const_steps, 1)
            nc.gpsimd.memset(S[:], 0.0).then_inc(const_steps, 1)
            nc.gpsimd.memset(xr[:], 0.0).then_inc(const_steps, 1)
            pool.wait_ge(const_steps, 6)
            nc.gpsimd.affine_select(out=ident[:], in_=ident[:], compare_op=ALU.not_equal, fill=1.0, base=0,
                                    pattern=[[-1, P]], channel_multiplier=1).then_inc(const_steps, 1)
            nc.gpsimd.affine_select(out=tri[:], in_=tri[:], compare_op=ALU.is_ge, fill=0.0, base=0,
                                    pattern=[[1, P]], channel_multiplier=-1).then_inc(const_steps, 1)

            def low(dst, src, hi):
                return nc.gpsimd.tensor_tensor(dst, src, hi.bitcast(F32), ALU.subtract)

            def tile_low(t, half, slot):
                s = (t % 2, slice(half * 4, half * 4 + 4))
                low(wl[:, s[0], s[1], :], raw[:, slot, :].rearrange("p (k n) -> p k n", k=4),
                    wh[:, s[0], s[1], :]).then_inc(w_ready, 1)

            for i in range(NT):
                pool.wait_ge(msx_done, i + 1)
                nc.gpsimd.tensor_tensor(rsx[:, i:i + 1], msx[:, i:i + 1], mhalf[:, i:i + 1], ALU.pow
                                        ).then_inc(rsx_done, 1)
            for p in range(FIRST_PIECES):
                pool.wait_ge(w_hi, p + 1)
                tile_low(p // 2, p % 2, p % 2)

            def piece(G, what, place):
                piece_wait(pool, w_hi, G, place, 1)
                if what == "wo":
                    j = place - (0 if is_last(G) else 2)
                    low(wol[:, j // 2, (j % 2) * 512:(j % 2) * 512 + 512], raw[:, place % 2, :],
                        woh[:, j // 2, (j % 2) * 512:(j % 2) * 512 + 512]).then_inc(w_ready, 1)
                else:
                    tile_low(what, place % 2, place % 2)

            for place in (0, 1):
                piece((None, 0), 0, place)

            def body(G):
                plan, early, late = steps(G)
                for c in range(1, 9):
                    for what, place in early[c]:
                        piece(G, what, place)
                    k = c - 1
                    wait(pool, ms_done, G, NT, k + 1)
                    nc.gpsimd.tensor_tensor(rstd[:, k % 2:k % 2 + 1], ms[:, k % 2:k % 2 + 1], mhalf[:, 0:1], ALU.pow
                                            ).then_inc(rstd_done, 1)
                    for what, place in late[c]:
                        piece(G, what, place)

            groups(pool, body)

        @block.scalar
        def _(act):
            def tile_high(t, half):
                slot = half
                nc.scalar.activation(wh[:, t % 2, half * 4:half * 4 + 4, :],
                                     raw[:, slot, :].rearrange("p (k n) -> p k n", k=4), ACT.Copy).then_inc(w_hi, 1)

            def free_slot(G, t):
                wait(act, proj_done, G, NU, (-1, 0, 2, 4, 6, 8)[t])

            act.wait_ge(const_steps, 8)
            for i in range(NT):
                act.wait_ge(x_loaded[i], 16)
                if i >= 1:
                    act.wait_ge(sumsq_done, i)
                nc.scalar.activation(junk, hacc[:, i, :], ACT.Square, accum_out=ssq[:, i:i + 1]).then_inc(sumsq_done, 1)
            act.wait_ge(wdt_loaded, 16)
            nc.scalar.activation(wh[:, 1], wdt.rearrange("p (k n) -> p k n", k=KD), ACT.Copy).then_inc(wd_hi, 1)
            for i in range(NT):
                for j in range(2):
                    act.wait_ge(xT_done, 2 * i + j + 1)
                    nc.scalar.activation(uTh[:, 4 * j:4 * j + 4, i * P:(i + 1) * P],
                                         tcb_ps[j][:], ACT.Copy).then_inc(uhi_done, 1)
                if i == 0:
                    for p in range(2):
                        act.wait_ge(raw_loaded[p], 16)
                        tile_high(0, p)

            def copy_unit(G, i):
                t, half = UNITS[i]
                wait(act, conv_steps, G, 32, 4 * (i - 1))
                if half == 1:
                    wait(act, raw_copied, G, 8, i)
                    nc.scalar.activation(xr[:, 1, 0:3], xr[:, 0, HALF:HALF + 3], ACT.Copy).then_inc(halo_copied, 1)
                else:
                    wait(act, halo_copied, G, 4, t)
                wait(act, proj_done, G, NU, i + 1)
                nc.scalar.activation(xr[:, half, 3:3 + HALF], proj_ps[i % 2][:], ACT.Copy).then_inc(raw_copied, 1)

            def tanh_unit(G, i, par):
                t, half = UNITS[i]
                cols = slice(half * HALF, half * HALF + HALF)
                if t < 4:
                    wait(act, conv_steps, G, 32, 4 * (i + 1))
                    nc.scalar.activation(xbc[:, par, t, cols], v[:], ACT.Tanh).then_inc(tanh_done, 1)
                else:
                    wait(act, proj_done, G, NU, i + 1)
                    if half == 0:
                        wait(act, gate_steps, G, 24, -12)
                    nc.scalar.activation(zs[:, t - 4, cols], proj_ps[i % 2][:], ACT.Tanh, scale=0.5
                                         ).then_inc(tanh_done, 1)

            def exp_e(G, c):
                wait(act, sub_steps, G, 32, 4 * c + 4)
                e = E[:, c % 2].rearrange("p r l -> p (r l)")
                nc.scalar.activation(e, e, ACT.Exp).then_inc(exp_done, 1)

            def copy_b(G, c):
                wait(act, tcb_done, G, NT, c + 1)
                wait(act, st_mm, G, NT, c - 1)
                nc.scalar.activation(btok[:, c % 2, :], tcb_ps[c % 2][:, 2, :], ACT.Copy).then_inc(btok_done, 1)

            def gated(G, k):
                wait(act, gate_steps, G, 24, 3 * k + 3)
                nc.scalar.activation(sq[:], ygf[:], ACT.Square).then_inc(sq_done, 1)
                for t in range(2):
                    nc.scalar.activation(yh[:, t, :], ygf[:, t, :], ACT.Copy, scale=nw[:, bass.ds(val(G, 2, t), 1)]
                                         ).then_inc(yhi_done, 1)

            def piece(G, what, place):
                n = FIRST_PIECES + place
                wait(act, raw_loaded[place % 2], G, 16 * CYCLE // 2, 16 * (n // 2 + 1))
                if what == "wo":
                    j = place - (0 if is_last(G) else 2)
                    nc.scalar.activation(woh[:, j // 2, (j % 2) * 512:(j % 2) * 512 + 512], raw[:, place % 2, :],
                                         ACT.Copy).then_inc(w_hi, 1)
                else:
                    H = nxt(G, 2) if place >= CYCLE else nxt(G)
                    free_slot(H, what)
                    tile_high(what, place % 2)

            def step_sizes():
                act.wait_ge(dt_steps, 3)
                nc.scalar.activation(tmp[2], tmp[2], ACT.Exp, scale=-1.0).then_inc(dt_act, 1)
                act.wait_ge(consts_loaded, 16 * 7)
                nc.scalar.activation(alogb[:], alogb[:], ACT.Exp).then_inc(dt_act, 1)
                act.wait_ge(dt_steps, 4)
                nc.scalar.activation(tmp[4], tmp[3], ACT.Ln).then_inc(dt_act, 1)

            def decays():
                flat = "p g c r -> p (g c r)"
                act.wait_ge(cum_mm, 2)
                nc.scalar.activation(acum[:].rearrange(flat), y_ps[:, 0, :], ACT.Copy).then_inc(cum_act, 1)
                nc.scalar.activation(eac[:].rearrange(flat), y_ps[:, 0, :], ACT.Exp).then_inc(cum_act, 1)
                nc.scalar.activation(dch[:].rearrange(flat), y_ps[:, 1, :], ACT.Exp).then_inc(cum_act, 1)

            def row_sums():
                flat = "p g c r -> p (g c r)"
                for j in range(2):
                    act.wait_ge(acT_mm, 2)
                    nc.scalar.activation(acs[:, j, :], st_ps[:, 0, j * P:(j + 1) * P], ACT.Copy).then_inc(acT_sb, 1)
                act.wait_ge(dt_steps, 15)
                nc.scalar.activation(dst[:].rearrange(flat), tmp[1], ACT.Exp).then_inc(cum_act, 1)

            G0 = (None, 0)
            for i in range(10):
                t, half = UNITS[i]
                if i == 8:
                    act.wait_ge(cum_act, 4)
                if t < 4:
                    copy_unit(G0, i)
                if i == 0:
                    for j in range(2):
                        act.wait_ge(dt_mm, j + 1)
                        nc.scalar.activation(dtc[:, j * HALF:(j + 1) * HALF], out_ps[j][:], ACT.Copy).then_inc(dtc_done, 1)
                    for p in range(2):
                        act.wait_ge(raw_loaded[p], 32)
                        tile_high(1, p)
                if i == 1:
                    step_sizes()
                if i == 2:
                    decays()
                if i == 3:
                    row_sums()
                tanh_unit(G0, i, 0)
                if half == 0 and t < 4:
                    act.wait_ge(proj_done, 2 * t + 2)
                    for q in (0, 1):
                        act.wait_ge(raw_loaded[q], 16 * (t + 3))
                        tile_high(t + 2, q)
                if i == 6:
                    exp_e(G0, 0)
            copy_b(G0, 0)
            exp_e(G0, 1)
            copy_b(G0, 1)
            tanh_unit(G0, 10, 0)
            for place in (0, 1):
                act.wait_ge(raw_loaded[place], 16 * (FIRST_PIECES // 2 + 1))
                act.wait_ge(proj_done, 11)
                tile_high(0, place)

            def body(G):
                plan, early, late = steps(G)
                last = is_last(G)
                prev_b = None
                for c in range(1, 9):
                    k = c - 1
                    if prev_b is not None and prev_b[1] < 8:
                        copy_unit(*prev_b)
                    gated(G, k)
                    if prev_b is not None:
                        tanh_unit(*prev_b, (G[1] + 1) % 2)
                    if c < NT - 1 or not last:
                        exp_e(G, c + 1)
                    A = unit_of(G, plan[c][0]) if plan[c] else None
                    if A and A[1] < 8:
                        copy_unit(*A)
                    if c == 1:
                        for q in early[c][:2]:
                            piece(G, *q)
                    if c < NT - 1 or not last:
                        copy_b(G, c + 1)
                    for q in early[c][2 if c == 1 else 0:]:
                        piece(G, *q)
                    if A:
                        tanh_unit(*A, A[0][1] % 2)
                    for q in late[c]:
                        piece(G, *q)
                    b = unit_b(plan, c)
                    prev_b = unit_of(G, b) if b is not None else None

            groups(act, body)

        @block.vector
        def _(dve):
            vec = nc.vector
            dve.wait_ge(consts_loaded, 16 * 7)
            def mean_square_x(i):
                dve.wait_ge(sumsq_done, i + 1)
                vec.tensor_scalar(msx[:, i:i + 1], ssq[:, i:i + 1], 1.0 / D, EPS, ALU.mult, ALU.add).then_inc(msx_done, 1)

            mean_square_x(0)
            dve.wait_ge(rows_T, 1)
            tT = out_ps[1]
            vec.tensor_scalar(cw[:, 0:TAPS, :].rearrange("p k n -> p (k n)"), tT[:, 0:P], 0.5, None, ALU.mult
                              ).then_inc(halved, 1)
            vec.tensor_scalar(cw[:, TAPS, :], tT[:, P:P + CT], 0.5, None, ALU.mult).then_inc(halved, 1)
            vec.tensor_scalar(nw[:], tT[:, P + CT:P + CT + 2 * GROUPS], 0.5, None, ALU.mult).then_inc(halved, 1)
            dh = dall.rearrange("p (n q) -> p n q", q=2)
            for q in range(2):
                half_p = slice(q * HEAD_DIM, (q + 1) * HEAD_DIM)
                vec.tensor_copy(dsk[half_p, :], dh[half_p, :, q]).then_inc(halved, 1)

            def norm_tile(i):
                dve.wait_ge(rsx_done, i + 1)
                if i >= 2:
                    dve.wait_ge(xT_done, 2 * (i - 1))
                vec.scalar_tensor_tensor(xn[:, i % 2, :], hacc[:, i, :], rsx[:, i:i + 1], wb, ALU.mult, ALU.mult
                                         ).then_inc(xn_done, 1)

            norm_tile(0)
            mean_square_x(1)
            for i in range(NT):
                if i + 1 < NT:
                    norm_tile(i + 1)
                if i + 2 < NT:
                    mean_square_x(i + 2)
                if i == NT // 2:
                    dve.wait_ge(wd_hi, 1)
                    vec.tensor_tensor(wl[:, 1], wdt.rearrange("p (k n) -> p k n", k=KD), wh[:, 1].bitcast(F32), ALU.subtract
                                      ).then_inc(wd_lo, 1)
                for j in range(2):
                    dve.wait_ge(uhi_done, 2 * i + j + 1)
                    cols = slice(i * P, (i + 1) * P)
                    vec.tensor_tensor(uTl[:, 4 * j:4 * j + 4, cols], tcb_ps[j][:],
                                      uTh[:, 4 * j:4 * j + 4, cols].bitcast(F32), ALU.subtract).then_inc(ulo_done, 1)

            count = [0]

            def link(ins):
                count[0] += 1
                ins.then_inc(dt_steps, 1)
                dve.wait_ge(dt_steps, count[0])

            def gcr(ap):
                return ap.rearrange("p (g c r) -> p g c r", g=GROUPS, c=NT)

            def step_sizes():
                dve.wait_ge(dtT_mm, 2)
                b4 = dtb[:].rearrange("p (g r) -> p g r", g=GROUPS)
                for c in range(NT):
                    ins = vec.tensor_tensor(gcr(tmp[0])[:, :, c], tcb_ps[c // 4][:, c % 4, P - NH:P].rearrange("p (g r) -> p g r", g=GROUPS),
                                            b4, ALU.add)
                    if c < NT - 1:
                        ins.then_inc(halved, 1)
                count[0] += 1
                ins.then_inc(dt_steps, 1)
                dve.wait_ge(dt_steps, 1)
                dve.wait_ge(halved, 5 + NT - 1)
                link(vec.tensor_scalar(tmp[1], tmp[0], 0.0, None, ALU.max))
                link(vec.scalar_tensor_tensor(tmp[2], tmp[0], -1.0, tmp[0], ALU.mult, ALU.max))
                dve.wait_ge(dt_act, 1)
                link(vec.tensor_scalar(tmp[3], tmp[2], 1.0, None, ALU.add))
                link(vec.tensor_scalar(tmp[5], tmp[3], -1.0, None, ALU.add))
                link(vec.tensor_scalar(tmp[6], tmp[5], 0.0, None, ALU.is_equal))
                link(vec.tensor_tensor(tmp[5], tmp[5], tmp[6], ALU.add))
                link(vec.reciprocal(tmp[5], tmp[5]))
                dve.wait_ge(dt_act, 3)
                link(vec.tensor_tensor(tmp[4], tmp[4], tmp[6], ALU.add))
                link(vec.tensor_tensor(tmp[4], tmp[4], tmp[5], ALU.mult))
                link(vec.tensor_tensor(tmp[4], tmp[4], tmp[2], ALU.mult))
                dflat = dtT[:].rearrange("p g c r -> p (g c r)")
                link(vec.tensor_tensor(dflat, tmp[4], tmp[1], ALU.add))
                link(vec.tensor_scalar(alogb[:], alogb[:], -1.0, None, ALU.mult))
                a4 = alogb[:].rearrange("p (g r) -> p g r", g=GROUPS)
                for g in range(GROUPS):
                    ins = vec.tensor_tensor(gcr(tmp[7])[:, g], dtT[:, g], a4[:, g:g + 1, :].to_broadcast([P, NT, R]), ALU.mult)
                    if g < GROUPS - 1:
                        ins.then_inc(halved, 1)
                dve.wait_ge(halved, 5 + NT - 1 + GROUPS - 1)
                link(ins)

            def decay_to_end():
                dve.wait_ge(cum_act, 3)
                link(vec.tensor_tensor(tmp[1], y_ps[:, 1, :], acum[:].rearrange("p g c r -> p (g c r)"), ALU.subtract))

            def conv_unit(G, i):
                t, half = UNITS[i]
                wait(dve, raw_copied, G, 8, i + 1)
                prev = i - 1 if i else -5
                wait(dve, unit_final, G, NU, prev + 1)
                n = 4 * i
                tile = (G, 2, t) if t < 2 else (G, 1, 2 * GROUPS + (t - 2) * GROUPS)

                def w(k):
                    return cw[:, k, bass.ds(val(*tile), 1)]

                vec.tensor_scalar(v[:], xr[:, half, 3:3 + HALF], w(3), w(4), ALU.mult, ALU.add
                                  ).then_inc(conv_steps, 1)
                for k in (2, 1, 0):
                    wait(dve, conv_steps, G, 32, n + 3 - k)
                    vec.scalar_tensor_tensor(v[:], xr[:, half, k:k + HALF], w(k), v[:], ALU.mult, ALU.add
                                             ).then_inc(conv_steps, 1)

            def final_unit(G, i, par):
                t, half = UNITS[i]
                cols = slice(half * HALF, half * HALF + HALF)
                wait(dve, tanh_done, G, NU, i + 1)
                if t < 4:
                    dst, src = xbc[:, par, t, cols], v[:]
                else:
                    dst, src = zs[:, t - 4, cols], proj_ps[i % 2][:]
                vec.scalar_tensor_tensor(dst, dst, 1.0, src, ALU.add, ALU.mult).then_inc(unit_final, 1)

            def sub_e(G, c):
                wait(dve, e_loaded[c % 2], G, 16 * NT // 2, 16 * (c // 2 + 1))
                a = pick(acum, G) if c < 8 else pick(acum, nxt(G))
                for r in range(R):
                    e = E[:, c % 2, r, :]
                    vec.tensor_scalar(e, e, a[:, 0, c % 8, r:r + 1], 0.0, ALU.subtract, ALU.min).then_inc(sub_steps, 1)

            def spread(tab, G, c):
                H = G if c < 8 else nxt(G)
                return pick(tab, H)[:, 0, c % 8, :].unsqueeze(2).to_broadcast([P, R, HEAD_DIM])

            def heads(ap):
                return ap.rearrange("p (r q) -> p r q", r=R)

            def prep(G, c):
                wait(dve, btok_done, G, NT, c + 1)
                wait(dve, y_mm, G, NT, c - 1)
                tp = tcb_ps[c % 2]
                vec.tensor_tensor(heads(xdt[:, c % 2, :]), heads(tp[:, 0:2, :].rearrange("p t q -> p (t q)")),
                                  spread(dtT, G, c), ALU.mult).then_inc(xdt_steps, 1)
                wait(dve, m_done, G, NT, c)
                vec.tensor_tensor(cbm[:], tp[:, 3, :], tri[:], ALU.mult).then_inc(cbm_done, 1)
                wait(dve, xdt_steps, G, 2 * NT, 2 * c + 1)
                wait(dve, st_mm, G, NT, c - 1)
                vec.tensor_tensor(heads(xds[:, c % 2, :]), heads(xdt[:, c % 2, :]), spread(dst, G, c), ALU.mult
                                  ).then_inc(xdt_steps, 1)

            def make_m(G, c):
                wait(dve, exp_done, G, NT, c + 1)
                wait(dve, cbm_done, G, NT, c + 1)
                cb = cbm[:].unsqueeze(1).to_broadcast([P, R, P])
                vec.tensor_tensor(E[:, c % 2], E[:, c % 2], cb, ALU.mult).then_inc(m_done, 1)

            def y_and_state(G, c, last_chunk):
                wait(dve, y_mm, G, NT, c + 1)
                wait(dve, yT_done, G, NT, c)
                vec.tensor_tensor(heads(ysb[:]), heads(y_ps[:, 0, :]), spread(eac, G, c), ALU.mult).then_inc(y_steps, 1)
                wait(dve, y_steps, G, 2 * NT, 2 * c + 1)
                vec.tensor_tensor(ysb[:], ysb[:], y_ps[:, 1, :], ALU.add).then_inc(y_steps, 1)
                new = S[:, (c + 1) % 2, :]
                wait(dve, st_mm, G, NT, c + 1)
                if last_chunk:
                    for j in range(2):
                        vec.memset(new[:, j * P:(j + 1) * P], 0.0).then_inc(s_steps, 1)
                    return
                wait(dve, s_steps, G, 2 * NT, 2 * c)
                vec.tensor_tensor(heads(new), heads(S[:, c % 2, :]), spread(dch, G, c), ALU.mult).then_inc(s_steps, 1)
                wait(dve, s_steps, G, 2 * NT, 2 * c + 1)
                vec.tensor_tensor(new, new, st_ps[:, 0, :], ALU.add).then_inc(s_steps, 1)

            def gate(G, k):
                par = G[1] % 2
                cols = slice(k * P, k * P + P)
                wait(dve, yT_done, G, NT, k + 1)
                for t in range(2):
                    vec.scalar_tensor_tensor(ygf[:, t, :], xbc[:, par, t, cols], dsk[:, bass.ds(val(G, 2, t), 1)],
                                             st_ps[:, 1, t * P:(t + 1) * P], ALU.mult, ALU.add).then_inc(gate_steps, 1)
                wait(dve, gate_steps, G, 24, 3 * k + 2)
                wait(dve, unit_final, G, NU, 10 if k < 4 else 12)
                vec.tensor_tensor(ygf[:], ygf[:], zs[:, :, cols], ALU.mult).then_inc(gate_steps, 1)

            def gated_low(G, k):
                wait(dve, yhi_done, G, 2 * NT, 2 * k + 2)
                for t in range(2):
                    vec.scalar_tensor_tensor(yl[:, t, :], ygf[:, t, :], nw[:, bass.ds(val(G, 2, t), 1)],
                                             yh[:, t, :].bitcast(F32), ALU.mult, ALU.subtract).then_inc(ylo_done, 1)

            def mean_square(G, k):
                wait(dve, stat_mm, G, NT, k + 1)
                vec.tensor_scalar(ms[:, k % 2:k % 2 + 1], out_ps[0][:, 0:1], 1.0 / (4 * GCH), EPS, ALU.mult, ALU.add
                                  ).then_inc(ms_done, 1)

            def add_h(G, k, n):
                j = 1 - n
                wait(dve, rstd_done, G, NT, k + 1)
                wait(dve, out_mm, G, 2 * NT, 2 * k + n + 1)
                h = hacc[:, k, j * 512:(j + 1) * 512]
                vec.scalar_tensor_tensor(h, out_ps[j][:], rstd[:, k % 2:k % 2 + 1], h, ALU.mult, ALU.add
                                         ).then_inc(h_steps, 1)

            G0 = (None, 0)
            for i in range(10):
                if UNITS[i][0] < 4:
                    conv_unit(G0, i)
                if i == 6:
                    sub_e(G0, 0)
                final_unit(G0, i, 0)
                if i == 0:
                    step_sizes()
                if i == 2:
                    decay_to_end()
            prep(G0, 0)
            make_m(G0, 0)
            sub_e(G0, 1)
            prep(G0, 1)
            y_and_state(G0, 0, False)
            make_m(G0, 1)
            final_unit(G0, 10, 0)

            def body(G):
                plan, early, late = steps(G)
                last = is_last(G)
                prev_b = None
                for c in range(1, 9):
                    k = c - 1
                    more = c < NT - 1 or not last
                    gate(G, k)
                    if prev_b is not None and prev_b[1] < 8:
                        conv_unit(*prev_b)
                    if more:
                        sub_e(G, c + 1)
                    gated_low(G, k)
                    if prev_b is not None:
                        final_unit(*prev_b, (G[1] + 1) % 2)
                    if more:
                        prep(G, c + 1)
                    mean_square(G, k)
                    if c < NT or not last:
                        y_and_state(G, c, c == NT - 1)
                    if more:
                        make_m(G, c + 1)
                    A = unit_of(G, plan[c][0]) if plan[c] else None
                    if A and A[1] < 8:
                        conv_unit(*A)
                    add_h(G, k, 0)
                    if A:
                        final_unit(*A, A[0][1] % 2)
                    add_h(G, k, 1)
                    b = unit_b(plan, c)
                    prev_b = unit_of(G, b) if b is not None else None

            groups(dve, body)

        @block.tensor
        def _(pe):
            def mm3(out, ah, al, bh, bl, start, stop):
                nc.tensor.matmul(out, al, bh, start=start, stop=False)
                nc.tensor.matmul(out, ah, bl, start=False, stop=False)
                return nc.tensor.matmul(out, ah, bh, start=False, stop=stop)

            pe.wait_ge(const_steps, 8)
            pe.wait_ge(consts_loaded, 16 * 7)
            nr = CT + 2 * GROUPS
            nc.tensor.transpose(out_ps[1][:, 0:P], rows[:, 0, :], ident[:])
            nc.tensor.transpose(out_ps[1][:, P:P + nr], rows[0:nr, 1, :], ident[0:nr, 0:nr]).then_inc(rows_T, 1)
            def unit(G, i, ks=range(KD)):
                t, half = UNITS[i]
                if first(G):
                    pe.wait_ge(w_ready, 2 * t + 2)
                else:
                    wait(pe, w_ready, nxt(G, -1), CYCLE, FIRST_PIECES + TILE_PLACE[t] + 2)
                if i in (0, 1):
                    wait(pe, unit_final, G, NU, i - 1)
                elif i < 10:
                    wait(pe, raw_copied, G, 8, i - 1)
                else:
                    wait(pe, unit_final, G, NU, i - 1)
                cols = slice(half * HALF, half * HALF + HALF)
                for k in ks:
                    mm = mm3(proj_ps[i % 2][:], wh[:, t % 2, k, :], wl[:, t % 2, k, :],
                             uTh[:, k, cols], uTl[:, k, cols], k == 0, k == KD - 1)
                if ks[-1] == KD - 1:
                    mm.then_inc(proj_done, 1)

            def tcb(G, c):
                H, cc = (G, c) if c < 8 else (nxt(G), c - 8)
                par = H[1] % 2
                cols = slice(cc * P, cc * P + P)
                wait(pe, unit_final, H, NU, 7 if cc < 4 else 8)
                wait(pe, xdt_steps, G, 2 * NT, 2 * (c - 1))
                wait(pe, btok_done, G, NT, c - 1)
                out = tcb_ps[c % 2]
                for t in range(3):
                    nc.tensor.transpose(out[:, t, :], xbc[:, par, t, cols], ident[:])
                nc.tensor.matmul(out[:, 3, :], xbc[:, par, 2, cols], xbc[:, par, 3, cols], start=True, stop=True
                                 ).then_inc(tcb_done, 1)

            def scan(G, c):
                H, cc = (G, c) if c < 8 else (nxt(G), c - 8)
                wait(pe, s_steps, G, 2 * NT, 2 * c)
                wait(pe, y_steps, G, 2 * NT, 2 * c)
                nc.tensor.matmul(y_ps[:, 0, :], xbc[:, H[1] % 2, 3, cc * P:cc * P + P], S[:, c % 2, :], start=True, stop=True)
                wait(pe, m_done, G, NT, c + 1)
                for r in range(R):
                    q = slice(r * HEAD_DIM, (r + 1) * HEAD_DIM)
                    mm = nc.tensor.matmul(y_ps[:, 1, q], E[:, c % 2, r, :], xdt[:, c % 2, q], start=True, stop=True)
                mm.then_inc(y_mm, 1)
                wait(pe, xdt_steps, G, 2 * NT, 2 * c + 2)
                wait(pe, btok_done, G, NT, c + 1)
                wait(pe, gate_steps, G, 24, 3 * c)
                nc.tensor.matmul(st_ps[:, 0, :], btok[:, c % 2, :], xds[:, c % 2, :], start=True, stop=True).then_inc(st_mm, 1)

            def turn_y(G, c):
                wait(pe, y_steps, G, 2 * NT, 2 * c + 2)
                wait(pe, s_steps, G, 2 * NT, 2 * c + 2)
                for t in range(2):
                    mm = nc.tensor.transpose(st_ps[:, 1, t * P:(t + 1) * P], ysb[:, t * P:(t + 1) * P], ident[:])
                mm.then_inc(yT_done, 1)

            def sum_squares(G, k):
                wait(pe, sq_done, G, NT, k + 1)
                for t in range(2):
                    mm = nc.tensor.matmul(out_ps[0][:, 0:1], sq[:, t, :], ones[:, 0:1], start=(t == 0), stop=(t == 1))
                mm.then_inc(stat_mm, 1)

            def project_out(G, k):
                wait(pe, ylo_done, G, 2 * NT, 2 * k + 2)
                if k == 0:
                    wait(pe, w_ready, G, CYCLE, FIRST_PIECES + (4 if is_last(G) else 6))
                for j in (1, 0):
                    if j == 0:
                        wait(pe, ms_done, G, NT, k + 1)
                    for t in range(2):
                        cols = slice(j * 512, (j + 1) * 512)
                        mm = mm3(out_ps[j][:], yh[:, t, :], yl[:, t, :], woh[:, t, cols], wol[:, t, cols],
                                 t == 0, t == 1)
                    mm.then_inc(out_mm, 1)

            G0 = (None, 0)
            for i in range(NT):
                pe.wait_ge(xn_done, i + 1)
                for j in range(2):
                    if i >= 1:
                        pe.wait_ge(ulo_done, 2 * (i - 1) + j + 1)
                    for k in range(4):
                        col = (4 * j + k) * P
                        mm = nc.tensor.transpose(tcb_ps[j][:, k, :], xn[:, i % 2, col:col + P], ident[:])
                    mm.then_inc(xT_done, 1)
                if i >= NT // 2:
                    unit(G0, 0, range(2 * i - NT, 2 * i - NT + 2))
            pe.wait_ge(wd_lo, 1)
            pe.wait_ge(halved, 3)
            for j in range(2):
                pe.wait_ge(ulo_done, NT * (j + 1))
                for k in range(KD):
                    mm = mm3(out_ps[j][:], wh[:, 1, k, :], wl[:, 1, k, :], uTh[:, k, j * HALF:(j + 1) * HALF],
                             uTl[:, k, j * HALF:(j + 1) * HALF], k == 0, k == KD - 1)
                mm.then_inc(dt_mm, 1)
            for c in range(NT):
                pe.wait_ge(dtc_done, c // 4 + 1)
                mm = nc.tensor.transpose(tcb_ps[c // 4][:, c % 4, :], dtc[:, c * P:(c + 1) * P], ident[:])
                if c % 4 == 3:
                    mm.then_inc(dtT_mm, 1)
            unit(G0, 1)
            unit(G0, 2)
            pe.wait_ge(dt_steps, 14)
            nc.tensor.matmul(y_ps[:, 0, :], tri[:], tmp[7], start=True, stop=True).then_inc(cum_mm, 1)
            nc.tensor.matmul(y_ps[:, 1, :], ones[:], tmp[7], start=True, stop=True).then_inc(cum_mm, 1)
            unit(G0, 3)
            pe.wait_ge(cum_act, 1)
            af = acum[:].rearrange("p g c r -> p (g c r)")
            for j in range(2):
                nc.tensor.transpose(st_ps[:, 0, j * P:(j + 1) * P], af[:, j * P:(j + 1) * P], ident[:]).then_inc(acT_mm, 1)
            for i in range(4, 10):
                unit(G0, i)
            tcb(G0, 0)
            unit(G0, 10)
            tcb(G0, 1)
            pe.wait_ge(acT_sb, 2)
            scan(G0, 0)
            turn_y(G0, 0)

            def body(G):
                plan, early, late = steps(G)
                last = is_last(G)
                for c in range(1, 9):
                    if plan[c]:
                        unit(*unit_of(G, plan[c][0]))
                    if c < NT - 1 or not last:
                        tcb(G, c + 1)
                    sum_squares(G, c - 1)
                    if c < NT or not last:
                        scan(G, c)
                    b = unit_b(plan, c)
                    if b is not None and c == 1:
                        unit(*unit_of(G, b))
                    project_out(G, c - 1)
                    if b is not None and c > 1:
                        unit(*unit_of(G, b))
                    if c < NT or not last:
                        turn_y(G, c)

            groups(pe, body)


def routing(nc, hacc, ridx, etab, npairs, wtok, weights, norm_w, w_group, b_group, w_expert, b_expert, u2_dram):
    D = norm_w.shape[0]
    KD = D // P
    NT = hacc.shape[1]
    NL = EG + NE
    NTH = NT * P // P - 1

    with ExitStack() as ctx:
        def sb(name, shape, dt=F32):
            return ctx.enter_context(nc.sbuf_tensor(name, shape, dt))

        def sem(name):
            return ctx.enter_context(nc.semaphore(name))

        def psum(name, shape):
            return ctx.enter_context(nc.psum_tensor(name, shape, F32))

        wb = sb("wb2", [P, D])
        u2 = sb("u2", [P, 2, D])
        uT = sb("u2T", [P, 2, KD, P])
        wr = sb("wr", [P, KD, NL])
        biasb = sb("biasb", [P, NL])
        junk = sb("junk2", [P, D])
        ident = sb("ident2", [P, P])
        ones = sb("ones2", [P, P])
        below = sb("below", [P, P])
        stats = sb("stats", [P, 4, NT])
        mhalf = sb("mhalf2", [P, NT])
        iota_e = sb("iota_e", [P, NE])
        rev_e = sb("rev_e", [P, NE])
        iota_b = sb("iota_b", [P, MAXB])
        iota_p = sb("iota_p", [P, P])
        thr = sb("thr", [P, NTH])
        toki = sb("toki", [P, NT])
        lg = sb("lg", [P, NT, NL])
        el = sb("el", [P, NT, NE])
        ta = sb("ta", [P, NT, NE])
        tb = sb("tb", [P, NT, NE])
        M = sb("M", [P, 2, NT, NE])
        A = sb("A", [P, NT, NE])
        pre = sb("pre", [P, NT + 1, NE])
        gs = sb("gs", [P, NT, EG])
        g1 = sb("g1", [P, NT, EG])
        g2 = sb("g2", [P, NT, EG])
        s8 = sb("s8", [P, 16, NT])
        cmp = sb("cmp", [P, NE * NE])
        extra = sb("extra", [P, NE])
        scan = sb("scan2", [P, 2, 16 + NE])
        start = sb("start", [P, NE])
        hot = sb("hot", [P, 2, P])
        vals = sb("vals", [P, 2, 2, MAXB])
        ef = sb("ef", [P, MAXB])
        nf = sb("nf", [P, 2])

        tp = [psum(f"tp2_{j}", [P, 4, P]) for j in range(4)]
        lg_ps = psum("lg_ps", [P, NT, NL])
        rank_ps = psum("rank_ps", [P, NT, NE])
        cnt_ps = psum("cnt_ps", [P, NE])
        tab_ps = psum("tab_ps", [P, 2, MAXB])

        loaded = sem("loaded2")
        const_steps = sem("const_steps2")
        sumsq = sem("sumsq2")
        ms_done = sem("ms_done2")
        rs_done = sem("rs_done2")
        u_done = sem("u_done2")
        u_stored = [sem(f"u_stored{j}") for j in range(2)]
        turned = sem("turned2")
        uT_done = sem("uT_done2")
        logits = sem("logits")
        steps = sem("steps2")
        act_exp = sem("act_exp2")
        rank_mm = sem("rank_mm")
        hot_done = sem("hot_done")
        tab_mm = sem("tab_mm")

        block = ctx.enter_context(nc.Block())

        @block.sync
        def _(sp):
            sp.dma_start(wb[:], norm_w.partition_broadcast(P)).then_inc(loaded, 16)
            sp.dma_start(wr[:, :, 0:EG], w_group.rearrange("(k p) n -> p k n", p=P)).then_inc(loaded, 16)
            sp.dma_start(wr[:, :, EG:NL], w_expert.rearrange("(k p) n -> p k n", p=P)).then_inc(loaded, 16)
            sp.dma_start(biasb[:, 0:EG], b_group.partition_broadcast(P)).then_inc(loaded, 16)
            sp.dma_start(biasb[:, EG:NL], b_expert.partition_broadcast(P)).then_inc(loaded, 16)
            for j in range(NPC):
                weights.load(sp, 0, 0, j)
            ud = u2_dram.rearrange("(i p) d -> p i d", p=P)
            for i in range(NT):
                sp.wait_ge(u_done, i + 1)
                sp.dma_start(ud[:, i, :], u2[:, i % 2, :]).then_inc(u_stored[i % 2], 16)
            for j in range(8):
                weights.load(sp, 1, 1, j)
            for j in range(2):
                sp.wait_ge(u_stored[j], 16 * NT // 2)

        @block.gpsimd
        def _(pool):
            g = nc.gpsimd
            g.memset(ident[:], 0.0).then_inc(const_steps, 1)
            g.memset(below[:], 1.0).then_inc(const_steps, 1)
            g.memset(ones[:], 1.0).then_inc(const_steps, 1)
            g.memset(mhalf[:], -0.5).then_inc(const_steps, 1)
            g.memset(pre[:, 0, :], 0.0).then_inc(const_steps, 1)
            g.memset(scan[:], 0.0).then_inc(const_steps, 1)
            exact = dict(allow_small_or_imprecise_dtypes=True)
            g.iota(iota_e[:], pattern=[[1, NE]], base=0, channel_multiplier=0, **exact).then_inc(const_steps, 1)
            g.iota(rev_e[:], pattern=[[-1, NE]], base=NE, channel_multiplier=0, **exact).then_inc(const_steps, 1)
            g.iota(iota_b[:], pattern=[[1, MAXB]], base=0, channel_multiplier=0, **exact).then_inc(const_steps, 1)
            g.iota(iota_p[:], pattern=[[1, P]], base=0, channel_multiplier=0, **exact).then_inc(const_steps, 1)
            g.iota(thr[:], pattern=[[P, NTH]], base=P, channel_multiplier=0, **exact).then_inc(const_steps, 1)
            g.iota(toki[:], pattern=[[P, NT]], base=0, channel_multiplier=1, **exact).then_inc(const_steps, 1)
            pool.wait_ge(const_steps, 12)
            g.affine_select(out=ident[:], in_=ident[:], compare_op=ALU.not_equal, fill=1.0, base=0,
                            pattern=[[-1, P]], channel_multiplier=1).then_inc(const_steps, 1)
            g.affine_select(out=below[:], in_=below[:], compare_op=ALU.is_gt, fill=0.0, base=0,
                            pattern=[[1, P]], channel_multiplier=-1).then_inc(const_steps, 1)
            for i in range(NT):
                pool.wait_ge(ms_done, i + 1)
                g.tensor_tensor(stats[:, 2, i:i + 1], stats[:, 1, i:i + 1], mhalf[:, i:i + 1], ALU.pow
                                ).then_inc(rs_done, 1)

        @block.scalar
        def _(act):
            for i in range(NT):
                if i >= 1:
                    act.wait_ge(sumsq, i)
                nc.scalar.activation(junk[:], hacc[:, i, :], ACT.Square, accum_out=stats[:, 0, i:i + 1]
                                     ).then_inc(sumsq, 1)
            for i in range(NT):
                for j in range(2):
                    act.wait_ge(turned, 2 * i + j + 1)
                    if i >= 2:
                        act.wait_ge(logits, i - 1)
                    nc.scalar.activation(uT[:, i % 2, 4 * j:4 * j + 4, :], tp[2 * (i % 2) + j][:], ACT.Copy
                                         ).then_inc(uT_done, 1)
            act.wait_ge(steps, 7)
            nc.scalar.activation(g2[:], g1[:], ACT.Exp).then_inc(act_exp, 1)
            act.wait_ge(steps, 24)
            nc.scalar.activation(s8[:, 7, :], s8[:, 6, :], ACT.Exp).then_inc(act_exp, 1)

        @block.tensor
        def _(pe):
            pe.wait_ge(const_steps, 14)
            pe.wait_ge(loaded, 16 * 5)

            def logits_of(i):
                pe.wait_ge(uT_done, 2 * i + 2)
                for k in range(KD):
                    mm = nc.tensor.matmul(lg_ps[:, i, :], uT[:, i % 2, k, :], wr[:, k, :], start=(k == 0), stop=(k == KD - 1))
                mm.then_inc(logits, 1)

            for i in range(NT):
                pe.wait_ge(u_done, i + 1)
                if i >= 2:
                    pe.wait_ge(uT_done, 2 * (i - 1))
                for j in range(2):
                    for k in range(4):
                        col = (4 * j + k) * P
                        mm = nc.tensor.transpose(tp[2 * (i % 2) + j][:, k, :], u2[:, i % 2, col:col + P], ident[:])
                    mm.then_inc(turned, 1)
                if i >= 1:
                    logits_of(i - 1)
            logits_of(NT - 1)
            pe.wait_ge(steps, 29 + NT)
            flat = "p i e -> p (i e)"
            nc.tensor.matmul(rank_ps[:].rearrange(flat), below[:], A[:].rearrange(flat), start=True, stop=False)
            nc.tensor.matmul(rank_ps[:].rearrange(flat), ones[:], pre[:, 0:NT, :].rearrange(flat), start=False, stop=True)
            nc.tensor.matmul(cnt_ps[:], ones[:], pre[:, NT, :], start=True, stop=True).then_inc(rank_mm, 1)
            for n in range(2 * NT):
                pe.wait_ge(hot_done, 3 * (n + 1))
                nc.tensor.matmul(tab_ps[:].rearrange("p v b -> p (v b)"), hot[:, n % 2, :],
                                 vals[:, n % 2].rearrange("p v b -> p (v b)"), start=(n == 0), stop=(n == 2 * NT - 1)
                                 ).then_inc(tab_mm, 1)

        @block.vector
        def _(dve):
            vec = nc.vector
            for i in range(NT):
                dve.wait_ge(sumsq, i + 1)
                vec.tensor_scalar(stats[:, 1, i:i + 1], stats[:, 0, i:i + 1], 1.0 / D, EPS, ALU.mult, ALU.add
                                  ).then_inc(ms_done, 1)
            dve.wait_ge(loaded, 16 * 5)
            for i in range(NT):
                dve.wait_ge(rs_done, i + 1)
                if i >= 2:
                    dve.wait_ge(turned, 2 * (i - 1))
                    dve.wait_ge(u_stored[i % 2], 16 * (i // 2))
                vec.scalar_tensor_tensor(u2[:, i % 2, :], hacc[:, i, :], stats[:, 2, i:i + 1], wb[:], ALU.mult, ALU.mult
                                         ).then_inc(u_done, 1)
            count = [0]

            def link(ins):
                count[0] += 1
                ins.then_inc(steps, 1)
                dve.wait_ge(steps, count[0])

            def over(ap, n):
                return ap.unsqueeze(2).to_broadcast([P, NT, n])

            def each(ap, n):
                return ap.unsqueeze(1).to_broadcast([P, NT, n])

            dve.wait_ge(const_steps, 14)
            dve.wait_ge(logits, NT)
            link(vec.tensor_tensor(lg[:], lg_ps[:], each(biasb[:], NL), ALU.add))
            gl = lg[:, :, 0:EG]
            link(vec.tensor_reduce(s8[:, 0, :], gl, AX.X, ALU.max))
            link(vec.tensor_tensor(g1[:], gl, over(s8[:, 0, :], EG), ALU.is_ge))
            link(vec.tensor_tensor(g1[:], g1[:], each(rev_e[:, NE - EG:NE], EG), ALU.mult))
            link(vec.tensor_reduce(s8[:, 1, :], g1[:], AX.X, ALU.max))
            link(vec.tensor_tensor(gs[:], each(rev_e[:, NE - EG:NE], EG), over(s8[:, 1, :], EG), ALU.is_equal))
            link(vec.tensor_tensor(g1[:], gl, over(s8[:, 0, :], EG), ALU.subtract))
            dve.wait_ge(act_exp, 1)
            link(vec.tensor_reduce(s8[:, 2, :], g2[:], AX.X, ALU.add))
            link(vec.reciprocal(s8[:, 3, :], s8[:, 2, :]))
            link(vec.tensor_scalar(g1[:], gs[:], 1e30, -1e30, ALU.mult, ALU.add))
            for g in range(EG):
                q = slice(g * EPG, (g + 1) * EPG)
                link(vec.tensor_tensor(el[:, :, q], lg[:, :, EG + g * EPG:EG + (g + 1) * EPG],
                                       over(gs[:, :, g], EPG), ALU.mult))
            pen = g1[:].rearrange("p i g -> p (i g)").unsqueeze(2).to_broadcast([P, NT * EG, EPG])
            ev = el[:].rearrange("p i (g e) -> p (i g) e", g=EG)
            link(vec.tensor_tensor(ev, ev, pen, ALU.add))

            def top(n, mx, first):
                link(vec.tensor_reduce(s8[:, mx, :], el[:], AX.X, ALU.max))
                link(vec.tensor_tensor(ta[:], el[:], over(s8[:, mx, :], NE), ALU.is_ge))
                link(vec.tensor_tensor(ta[:], ta[:], each(rev_e[:], NE), ALU.mult))
                link(vec.tensor_reduce(s8[:, first, :], ta[:], AX.X, ALU.max))
                link(vec.tensor_tensor(M[:, n], each(rev_e[:], NE), over(s8[:, first, :], NE), ALU.is_equal))

            top(0, 4, 5)
            fl = "p i e -> p (i e)"
            link(vec.scalar_tensor_tensor(el[:].rearrange(fl), M[:, 0].rearrange(fl), -3e30, el[:].rearrange(fl),
                                          ALU.mult, ALU.add))
            link(vec.tensor_reduce(s8[:, 6, :], el[:], AX.X, ALU.max))
            link(vec.tensor_copy(s8[:, 8, :], s8[:, 6, :]))
            link(vec.tensor_tensor(s8[:, 6, :], s8[:, 6, :], s8[:, 4, :], ALU.subtract))
            link(vec.tensor_tensor(ta[:], el[:], over(s8[:, 8, :], NE), ALU.is_ge))
            link(vec.tensor_tensor(ta[:], ta[:], each(rev_e[:], NE), ALU.mult))
            link(vec.tensor_reduce(s8[:, 9, :], ta[:], AX.X, ALU.max))
            link(vec.tensor_tensor(M[:, 1], each(rev_e[:], NE), over(s8[:, 9, :], NE), ALU.is_equal))
            link(vec.tensor_tensor(A[:], M[:, 0], M[:, 1], ALU.add))
            for i in range(NT):
                link(vec.tensor_tensor(pre[:, i + 1, :], pre[:, i, :], A[:, i, :], ALU.add))
            dve.wait_ge(act_exp, 2)
            link(vec.tensor_scalar(s8[:, 10, :], s8[:, 7, :], 1.0, None, ALU.add))
            link(vec.reciprocal(s8[:, 10, :], s8[:, 10, :]))
            link(vec.tensor_tensor(wtok[:, 0, :], s8[:, 3, :], s8[:, 10, :], ALU.mult))
            link(vec.tensor_tensor(wtok[:, 1, :], wtok[:, 0, :], s8[:, 7, :], ALU.mult))
            dve.wait_ge(rank_mm, 1)
            c3 = cmp[:, 0:NE * NTH].rearrange("p (e j) -> p e j", e=NE)
            link(vec.tensor_tensor(c3, cnt_ps[:].unsqueeze(2).to_broadcast([P, NE, NTH]),
                                   thr[:].unsqueeze(1).to_broadcast([P, NE, NTH]), ALU.is_gt))
            link(vec.tensor_reduce(extra[:], c3, AX.X, ALU.add))
            link(vec.tensor_copy(scan[:, 0, 16:16 + NE], extra[:]))
            for n in range(5):
                a, b = scan[:, n % 2, :], scan[:, (n + 1) % 2, :]
                link(vec.tensor_tensor(b[:, 16:16 + NE], a[:, 16:16 + NE], a[:, 16 - (1 << n):16 + NE - (1 << n)], ALU.add))
            incl = scan[:, 1, 16:16 + NE]
            link(vec.tensor_tensor(start[:], incl, extra[:], ALU.subtract))
            link(vec.tensor_copy(ef[:], iota_b[:]))
            c3 = cmp[:, 0:16 * NE].rearrange("p (j e) -> p j e", j=16)
            link(vec.tensor_tensor(c3, incl.unsqueeze(1).to_broadcast([P, 16, NE]),
                                   iota_b[:, 0:16].unsqueeze(2).to_broadcast([P, 16, NE]), ALU.is_le))
            link(vec.tensor_reduce(ef[:, NE:NE + 16], c3, AX.X, ALU.add))
            link(vec.tensor_scalar(ef[:], ef[:], float(NE - 1), None, ALU.min))
            link(vec.tensor_copy(etab[:], ef[:]))
            link(vec.tensor_scalar(cmp[:, 0:8], iota_b[:, 0:8], 2.0, incl[:, NE - 1:NE], ALU.mult, ALU.is_lt))
            link(vec.tensor_reduce(nf[:, 0:1], cmp[:, 0:8], AX.X, ALU.add))
            for k in range(3):
                link(vec.tensor_scalar(npairs[:, k:k + 1], nf[:, 0:1], float(NE // 2 - 1 - k), None, ALU.add))
            for k in range(2):
                for table, at in ((rank_ps[:], 0), (each(iota_e[:], NE), 1), (each(start[:], NE), 2)):
                    link(vec.tensor_tensor(tb[:], M[:, k], table, ALU.mult))
                    link(vec.tensor_reduce(s8[:, at, :], tb[:], AX.X, ALU.add))
                c3 = cmp[:, 0:NT * NTH].rearrange("p (i j) -> p i j", i=NT)
                link(vec.tensor_tensor(c3, over(s8[:, 0, :], NTH), each(thr[:], NTH), ALU.is_ge))
                link(vec.tensor_reduce(s8[:, 4, :], c3, AX.X, ALU.add))
                link(vec.scalar_tensor_tensor(s8[:, 11 + 2 * k, :], s8[:, 4, :], -float(P), s8[:, 0, :],
                                              ALU.mult, ALU.add))
                link(vec.tensor_tensor(s8[:, 5, :], s8[:, 2, :], s8[:, 4, :], ALU.add))
                link(vec.tensor_tensor(s8[:, 5, :], s8[:, 5, :], s8[:, 1, :], ALU.subtract))
                link(vec.tensor_scalar(s8[:, 5, :], s8[:, 5, :], float(NE - 1), None, ALU.add))
                link(vec.tensor_scalar(s8[:, 6, :], s8[:, 4, :], 0.0, None, ALU.is_gt))
                link(vec.tensor_tensor(s8[:, 5, :], s8[:, 5, :], s8[:, 6, :], ALU.mult))
                link(vec.tensor_tensor(s8[:, 12 + 2 * k, :], s8[:, 5, :], s8[:, 1, :], ALU.add))
            link(vec.tensor_scalar(stats[:, 0, :], toki[:], -PADROW, None, ALU.add))
            link(vec.tensor_scalar(stats[:, 1, :], toki[:], 2.0, -PADROW, ALU.mult, ALU.add))
            link(vec.tensor_scalar(stats[:, 2, :], toki[:], 2.0, 1.0 - PADROW, ALU.mult, ALU.add))
            for n in range(2 * NT):
                k, i = n // NT, n % NT
                if n >= 2:
                    dve.wait_ge(tab_mm, n - 1)
                vec.tensor_scalar(hot[:, n % 2, :], iota_p[:], s8[:, 11 + 2 * k, i:i + 1], None, ALU.is_equal
                                  ).then_inc(hot_done, 1)
                for q, src in enumerate((0, 1 + k)):
                    vec.tensor_scalar(vals[:, n % 2, q, :], iota_b[:], s8[:, 12 + 2 * k, i:i + 1], stats[:, src, i:i + 1],
                                      ALU.is_equal, ALU.mult).then_inc(hot_done, 1)
            dve.wait_ge(tab_mm, 2 * NT)
            link(vec.tensor_scalar(ridx[:], tab_ps[:], PADROW, None, ALU.add))


NPC = 12


class Weights:

    def __init__(self, nc, ctx, w_gate, w_up, w_down):
        _, D, FF = w_gate.shape
        self.src = w_gate, w_up, w_down
        self.gu = [ctx.enter_context(nc.sbuf_tensor(f"w_gu{b}", [P, 2, D // P, FF], F32)) for b in range(2)]
        self.d = [ctx.enter_context(nc.sbuf_tensor(f"w_d{b}", [P, FF // P, D], F32)) for b in range(2)]
        self.loaded = [[ctx.enter_context(nc.semaphore(f"w_loaded{b}_{j}")) for j in range(NPC)] for b in range(2)]

    def load(self, sp, e, b, j):
        if j < 8:
            n = j // 2
            src = self.src[j % 2][bass.ds(e, 1)].rearrange("e (p k) f -> p (e k) f", p=P)[:, 2 * n:2 * n + 2, :]
            dst = self.gu[b][:, j % 2, 2 * n:2 * n + 2, :]
        else:
            n = j - 8
            src = self.src[2][bass.ds(e, 1)].rearrange("e (p k) d -> p (e k) d", p=P)[:, n:n + 1, :]
            dst = self.d[b][:, n:n + 1, :]
        sp.dma_start(dst, src).then_inc(self.loaded[b][j], 16)

    def gate_up(self, b, j):
        n = j // 2
        return self.gu[b][:, j % 2, 2 * n:2 * n + 2, :].rearrange("p k f -> p (k f)")


def experts(nc, hacc, ridx, etab, npairs, wtok, weights, u2_dram, y_dram, out):
    _, D, FF = weights.src[0].shape
    KD = D // P
    KF = FF // P
    NT = hacc.shape[1]
    T = NT * P
    RING = 4

    with ExitStack() as ctx:
        def sb(name, shape, dt=F32):
            return ctx.enter_context(nc.sbuf_tensor(name, shape, dt))

        def sem(name):
            return ctx.enter_context(nc.semaphore(name))

        def psum(name, shape):
            return ctx.enter_context(nc.psum_tensor(name, shape, F32))

        wh = sb("gu_hi", [P, RING, 2 * FF], F32R)
        wl = sb("gu_lo", [P, RING, 2 * FF], F32R)
        xg = sb("xg", [P, 2, D])
        xTh = sb("xTh", [P, 2, KD, P], F32R)
        xTl = sb("xTl", [P, 2, KD, P], F32R)
        hid = sb("hid", [P, FF])
        hT = sb("hT", [P, 2, KF, P])
        yb = sb("yb", [P, 2, D])
        gidx = sb("gidx", [P, 2, 1], I32)
        sidx = sb("sidx", [P, 2, 1], I32)
        zero = sb("zero", [P, 1], I32)
        gtmp = sb("gtmp", [P, 2, 1], I32)
        stmp = sb("stmp", [P, 2, 1], I32)
        ident = sb("ident3", [P, P])
        tp = [psum(f"tp3_{j}", [P, 4, P]) for j in range(2)]
        g_ps = psum("g_ps", [P, FF])
        u_ps = psum("u_ps", [P, FF])
        hT_ps = psum("hT_ps", [P, KF, P])
        y_ps = [psum(f"y3_{j}", [P, 512]) for j in range(2)]
        y2 = [weights.gu[j // 2][:].rearrange("p a k f -> p (a k f)")[:, (j % 2) * 2 * D:(j % 2 + 1) * 2 * D]
              .rearrange("p (c d) -> p c d", c=2) for j in range(4)]

        w_hi = sem("w_hi3")
        w_lo = sem("w_lo3")
        w_used = sem("w_used3")
        d_used = sem("d_used")
        const_steps = sem("const_steps3")
        gidx_done = sem("gidx_done")
        sidx_done = sem("sidx_done")
        gathered = [sem(f"gathered{b}") for b in range(2)]
        scattered = [sem(f"scattered{b}") for b in range(2)]
        turned = sem("turned3")
        xT_hi = sem("xT_hi3")
        xT_lo = sem("xT_lo3")
        silu_done = sem("silu_done")
        hid_done = sem("hid_done")
        hT_mm = sem("hT_mm")
        hT_done = sem("hT_done3")
        y_mm = sem("y_mm3")
        y_done = sem("y_done3")
        y2_loaded = [sem(f"y2_loaded{j}") for j in range(4)]
        comb = sem("comb")
        out_stored = sem("out_stored")

        def val(p, b, per, add):
            reg, off = p
            add += (2 * off + b) * per
            return add if reg is None else reg * (2 * per) + add

        FIRST = (None, 0)

        def shifted(p, n):
            return p[0], p[1] + n

        def wait(eng, s, p, b, per, add):
            if p[0] is None and val(p, b, per, add) <= 0:
                return
            eng.wait_ge(s, val(p, b, per, add))

        def pairs(eng, body, peeled=1):
            def less(k):
                return eng.value_load(npairs[0:1, k - 1:k], min_val=NE // 2 - k, max_val=NE // 2 + 8 - k)

            for n in range(peeled):
                body((None, n), False)
            with eng.Fori(peeled, less(1)) as p:
                body((p, 0), False)
            last = (less(1 + peeled), peeled)
            body(last, True)
            return last

        block = ctx.enter_context(nc.Block())

        @block.sync
        def _(sp):
            def body(p, last):
                if p[0] is None and p[1] == 0:
                    return
                for b in range(2):
                    e = sp.value_load(etab[0:1, bass.ds(val(p, b, 1, 0), 1)], min_val=0, max_val=NE - 1)
                    for j in range(8):
                        wait(sp, w_lo, p, b, 8, j + 1 - 16)
                        weights.load(sp, e, b, j)
                    load_down(p, b - 1)

            def load_down(p, b):
                e = sp.value_load(etab[0:1, bass.ds(val(p, b, 1, 0), 1)], min_val=0, max_val=NE - 1)
                for k in range(KF):
                    if k < KF - 1:
                        wait(sp, d_used, p, b, 3, k + 1 - 6)
                    else:
                        wait(sp, y_mm, p, b, 2, -2)
                    weights.load(sp, e, b % 2, 8 + k)

            last = pairs(sp, body, peeled=2)
            load_down(last, 1)
            for b in range(2):
                sp.wait_ge(scattered[b], val(last, 0, 8, 16))
            yv = y_dram.rearrange("(i p c) d -> p i c d", p=P, c=2)
            ov = out.rearrange("(i p) d -> p i d", p=P)
            for i in range(NT + 3):
                if i < NT:
                    if i >= 4:
                        sp.wait_ge(comb, 2 * (i - 3))
                    sp.dma_start(y2[i % 4], yv[:, i]).then_inc(y2_loaded[i % 4], 16)
                if i >= 3:
                    sp.wait_ge(comb, 2 * (i - 2))
                    sp.dma_start(ov[:, i - 3, :], hacc[:, i - 3, :]).then_inc(out_stored, 16)
            sp.wait_ge(out_stored, 16 * NT)

        @block.gpsimd
        def _(pool):
            g = nc.gpsimd
            g.memset(ident[:], 0.0).then_inc(const_steps, 1)
            g.memset(xg[:], 0.0).then_inc(const_steps, 1)
            g.memset(zero[:], 0).then_inc(const_steps, 1)
            pool.wait_ge(const_steps, 3)
            g.affine_select(out=ident[:], in_=ident[:], compare_op=ALU.not_equal, fill=1.0, base=0,
                            pattern=[[-1, P]], channel_multiplier=1).then_inc(const_steps, 1)

            last_token, last_row = pool.to_reg(T - 1), pool.to_reg(2 * T - 1)

            def gather(p, b, ahead):
                par = (b + ahead) % 2
                wait(pool, turned, p, b, 2, 2 * (ahead - 1))
                g.tensor_copy(gtmp[:, par, :], ridx[:, 0, bass.ds(val(p, b, 1, ahead), 1)]).then_inc(gidx_done, 1)
                wait(pool, gidx_done, p, b, 1, ahead + 1)
                g.tensor_tensor(gidx[:, par, :], gtmp[:, par, :], zero[:], ALU.add).then_inc(const_steps, 1)
                g.drain()
                g.indirect_dma_start(xg[:, par, :], None, u2_dram,
                                     bass.IndirectOffsetOnAxis(gidx[:, par, :].bitcast(U32), 0),
                                     bounds_check=last_token, oob_is_err=False).then_inc(gathered[par], 16)

            def scatter(p, b):
                wait(pool, scattered[b], p, 0, 8, 0)
                g.tensor_copy(stmp[:, b, :], ridx[:, 1, bass.ds(val(p, b, 1, 0), 1)]).then_inc(sidx_done, 1)
                wait(pool, sidx_done, p, b, 1, 1)
                wait(pool, y_done, p, b, 2, 2)
                g.tensor_tensor(sidx[:, b, :], stmp[:, b, :], zero[:], ALU.add).then_inc(const_steps, 1)
                g.drain()
                g.indirect_dma_start(y_dram, bass.IndirectOffsetOnAxis(sidx[:, b, :].bitcast(U32), 0), yb[:, b, :], None,
                                     bounds_check=last_row, oob_is_err=False).then_inc(scattered[b], 16)

            def body(p, last):
                for b in range(2):
                    if not last:
                        gather(p, b, 3)
                    if b == 1:
                        scatter(p, 0)
                    elif p[0] is not None:
                        scatter(shifted(p, -1), 1)

            for ahead in range(3):
                gather(FIRST, 0, ahead)
            last = pairs(pool, body)
            scatter(last, 1)
            pool.wait_ge(gathered[0], val(last, 0, 8, 32))

        @block.scalar
        def _(act):
            def turn_x(p, b, ahead):
                par = (b + ahead) % 2
                for j in range(2):
                    wait(act, turned, p, b, 2, 2 * ahead + j + 1)
                    nc.scalar.activation(xTh[:, par, 4 * j:4 * j + 4, :], tp[j][:], ACT.Copy).then_inc(xT_hi, 1)

            def split(p, b, j):
                act.wait_ge(weights.loaded[b][j], val(p, 0, 8, 16))
                wait(act, w_used, p, b, 8, j + 1 - RING)
                nc.scalar.activation(wh[:, j % RING, :], weights.gate_up(b, j), ACT.Copy).then_inc(w_hi, 1)

            def body(p, last):
                for b in range(2):
                    for j in range(RING, 8):
                        split(p, b, j)
                    if b == 0 or not last:
                        for j in range(RING):
                            split(*((p, 1) if b == 0 else (shifted(p, 1), 0)), j)
                        turn_x(p, b, 1)
                    wait(act, w_used, p, b, 8, 7)
                    wait(act, hT_mm, p, b, 1, 0)
                    nc.scalar.activation(hid[:], g_ps[:], ACT.Silu).then_inc(silu_done, 1)

            for j in range(RING):
                split(FIRST, 0, j)
            turn_x(FIRST, 0, 0)
            pairs(act, body)

        @block.tensor
        def _(pe):
            pe.wait_ge(const_steps, 4)

            def turn_x(p, b, ahead):
                par = (b + ahead) % 2
                pe.wait_ge(gathered[par], val(p, 0, 8, 16 + 16 * ((b + ahead) // 2)))
                wait(pe, xT_lo, p, b, 2, 2 * ahead)
                xk = xg[:, par, :].rearrange("p (q k) -> p k q", k=KD)
                for j in range(2):
                    for k in range(4):
                        mm = nc.tensor.transpose(tp[j][:, k, :], xk[:, 4 * j + k, :], ident[:])
                    mm.then_inc(turned, 1)

            def gate_up(p, b):
                wait(pe, xT_lo, p, b, 2, 2)
                wait(pe, hid_done, p, b, 1, 0)
                for j in range(8):
                    ps = (g_ps, u_ps)[j % 2]
                    wait(pe, w_lo, p, b, 8, j + 1)
                    for i in range(2):
                        k = j // 2 * 2 + i
                        f = slice(i * FF, (i + 1) * FF)
                        nc.tensor.matmul(ps[:], xTl[:, b, k, :], wh[:, j % RING, f], start=(k == 0), stop=False)
                        nc.tensor.matmul(ps[:], xTh[:, b, k, :], wl[:, j % RING, f], start=False, stop=False)
                        mm = nc.tensor.matmul(ps[:], xTh[:, b, k, :], wh[:, j % RING, f], start=False, stop=(k == KD - 1))
                    mm.then_inc(w_used, 1)

            def turn_hid(p, b):
                wait(pe, hid_done, p, b, 1, 1)
                wait(pe, hT_done, p, b, 1, 0)
                hk = hid[:].rearrange("p (q k) -> p k q", k=KF)
                for k in range(KF):
                    mm = nc.tensor.transpose(hT_ps[:, k, :], hk[:, k, :], ident[:])
                mm.then_inc(hT_mm, 1)

            def down(p, b):
                wait(pe, hT_done, p, b, 1, 1)
                for k in range(KF):
                    pe.wait_ge(weights.loaded[b][8 + k], val(p, 0, 8, 16))
                    for j in range(2):
                        if k == 0:
                            wait(pe, y_done, p, b, 2, j - 1)
                        mm = nc.tensor.matmul(y_ps[j][:], hT[:, b, k, :], weights.d[b][:, k, j * 512:(j + 1) * 512],
                                              start=(k == 0), stop=(k == KF - 1))
                        if k == KF - 1:
                            mm.then_inc(y_mm, 1)
                    if k < KF - 1:
                        mm.then_inc(d_used, 1)

            def body(p, last):
                for b in range(2):
                    gate_up(p, b)
                    if b == 0 or not last:
                        turn_x(p, b, 1)
                    if b == 1:
                        down(p, 0)
                    elif not p[0] is None:
                        down(shifted(p, -1), 1)
                    turn_hid(p, b)

            turn_x(FIRST, 0, 0)
            down(pairs(pe, body), 1)

        @block.vector
        def _(dve):
            vec = nc.vector

            def turn_x(p, b, ahead):
                par = (b + ahead) % 2
                for j in range(2):
                    wait(dve, xT_hi, p, b, 2, 2 * ahead + j + 1)
                    vec.tensor_tensor(xTl[:, par, 4 * j:4 * j + 4, :], tp[j][:], xTh[:, par, 4 * j:4 * j + 4, :].bitcast(F32),
                                      ALU.subtract).then_inc(xT_lo, 1)

            def split(p, b, j):
                wait(dve, w_hi, p, b, 8, j + 1)
                vec.tensor_tensor(wl[:, j % RING, :], weights.gate_up(b, j), wh[:, j % RING, :].bitcast(F32), ALU.subtract
                                  ).then_inc(w_lo, 1)

            def y_out(p, b):
                wait(dve, sidx_done, p, b, 1, 1)
                for j in range(2):
                    wait(dve, y_mm, p, b, 2, j + 1)
                    vec.tensor_copy(yb[:, b, j * 512:(j + 1) * 512], y_ps[j][:]).then_inc(y_done, 1)

            def body(p, last):
                for b in range(2):
                    for j in range(RING, 8):
                        split(p, b, j)
                    if b == 0 or not last:
                        for j in range(RING):
                            split(*((p, 1) if b == 0 else (shifted(p, 1), 0)), j)
                        turn_x(p, b, 1)
                    wait(dve, silu_done, p, b, 1, 1)
                    wait(dve, w_used, p, b, 8, 8)
                    vec.tensor_tensor(hid[:], hid[:], u_ps[:], ALU.mult).then_inc(hid_done, 1)
                    if b == 1:
                        y_out(p, 0)
                    elif not p[0] is None:
                        y_out(shifted(p, -1), 1)
                    wait(dve, hT_mm, p, b, 1, 1)
                    wait(dve, y_mm, p, b, 2, -2)
                    vec.tensor_copy(hT[:, b], hT_ps[:]).then_inc(hT_done, 1)

            for j in range(RING):
                split(FIRST, 0, j)
            turn_x(FIRST, 0, 0)
            y_out(pairs(dve, body), 1)
            for i in range(NT):
                dve.wait_ge(y2_loaded[i % 4], 16 * (i // 4 + 1))
                for c in range(2):
                    if c:
                        dve.wait_ge(comb, 2 * i + 1)
                    vec.scalar_tensor_tensor(hacc[:, i, :], y2[i % 4][:, c, :], wtok[:, c, i:i + 1], hacc[:, i, :],
                                             ALU.mult, ALU.add).then_inc(comb, 1)


def layer(nc, x, norm_mix, norm_ffn, ssd_w_in, ssd_conv_w, ssd_conv_b, ssd_dt_bias, ssd_a_log, ssd_d, ssd_norm,
          ssd_w_out, moe_w_group, moe_b_group, moe_w_expert, moe_b_expert, moe_w_gate, moe_w_up, moe_w_down, out):
    T, D = x.shape[1:]
    with ExitStack() as ctx:
        hacc = ctx.enter_context(nc.sbuf_tensor("hacc", [P, T // P, D], F32))
        ridx = ctx.enter_context(nc.sbuf_tensor("ridx", [P, 2, MAXB], I32))
        etab = ctx.enter_context(nc.sbuf_tensor("etab", [P, MAXB], I32))
        npairs = ctx.enter_context(nc.sbuf_tensor("npairs", [P, 3], I32))
        wtok = ctx.enter_context(nc.sbuf_tensor("wtok", [P, 2, T // P], F32))
        acum_dram = nc.dram_tensor("acum_dram", [GROUPS * R * (T // P), P], F32).ap()
        u2_dram = nc.dram_tensor("u2_dram", [T, D], F32).ap()
        y_dram = nc.dram_tensor("y_dram", [2 * T, D], F32).ap()
        mamba(nc, hacc, x[0], norm_mix[0], ssd_w_in[0], ssd_conv_w[0], ssd_conv_b[0], ssd_dt_bias[0], ssd_a_log[0],
              ssd_d[0], ssd_norm[0], ssd_w_out[0], acum_dram)
        weights = Weights(nc, ctx, moe_w_gate[0], moe_w_up[0], moe_w_down[0])
        routing(nc, hacc, ridx, etab, npairs, wtok, weights, norm_ffn[0], moe_w_group[0], moe_b_group[0], moe_w_expert[0],
                moe_b_expert[0], u2_dram)
        experts(nc, hacc, ridx, etab, npairs, wtok, weights, u2_dram, y_dram, out[0])


_INS = ["x", "norm_mix", "norm_ffn", "ssd_w_in", "ssd_conv_w", "ssd_conv_b", "ssd_dt_bias", "ssd_a_log", "ssd_d",
        "ssd_norm", "ssd_w_out", "moe_w_group", "moe_b_group", "moe_w_expert", "moe_b_expert", "moe_w_gate",
        "moe_w_up", "moe_w_down"]
_OUTS = [((1, 1024, 1024), "float32")]


def kernel(**inputs):
    import numpy as _np
    import concourse.bacc as _bacc
    from concourse import mybir as _mybir
    from concourse.bass_utils import run_bass_kernel_spmd as _run

    nc = _bacc.Bacc("TRN2", target_bir_lowering=False, num_devices=1)
    arrays, args = {}, []
    for name in _INS:
        a = _np.ascontiguousarray(inputs[name])
        arrays[f"in_{name}_dram"] = a
        args.append(nc.dram_tensor(f"in_{name}_dram", a.shape, _mybir.dt.from_np(a.dtype), kind="ExternalInput").ap())
    for i, (shape, dtype) in enumerate(_OUTS):
        dt = _mybir.dt.from_np(_np.dtype(dtype))
        args.append(nc.dram_tensor(f"out_{i}_dram", shape, dt, kind="ExternalOutput").ap())
    layer(nc, *args)
    r = _run(nc, [arrays], core_ids=[0])
    return r.results[0]["out_0_dram"]
```

```python
from contextlib import ExitStack

import concourse.bass as bass
from concourse import mybir

ALU = mybir.AluOpType
ACT = mybir.ActivationFunctionType
AX = mybir.AxisListType
F32 = mybir.dt.float32
F32R = mybir.dt.float32r
I32 = mybir.dt.int32
U32 = mybir.dt.uint32

P = 128
EPS = 1e-6
HEAD_DIM = 64
GROUPS = 8
R = 4
STATE = 128
TAPS = 4
GCH = R * HEAD_DIM
TILES = 6
HALF = 512
UNITS = [(0, 0), (0, 1), (1, 0), (1, 1), (2, 0), (2, 1), (3, 0), (3, 1), (4, 0), (5, 0), (4, 1), (5, 1)]
NU = len(UNITS)
PLAN = {1: [11, NU + 0], 2: [NU + 1], 3: [NU + 2, NU + 3], 4: [NU + 4], 5: [NU + 5, NU + 6],
        6: [NU + 7], 7: [NU + 8, NU + 9], 8: [NU + 10]}
CYCLE = 16
FIRST_PIECES = 2 * TILES
EARLY = {1: [("wo", 2), ("wo", 3), ("wo", 4), ("wo", 5)], 4: [(3, 10), (3, 11)], 6: [(4, 12), (4, 13)],
         7: [(5, 14), (5, 15)]}
LATE = {1: [(1, 6), (1, 7)], 2: [(2, 8), (2, 9)], 8: [(0, 16), (0, 17)]}
TILE_PLACE = [0, 6, 8, 10, 12, 14]
EG = 4
EPG = 8
NE = EG * EPG
MAXB = 52
PADROW = 8192.0


def bcast(ap, shape):
    return ap.to_broadcast(shape)


NPC = 12


class Weights:

    def __init__(self, nc, ctx, w_gate, w_up, w_down):
        _, D, FF = w_gate.shape
        self.src = w_gate, w_up, w_down
        self.shape = [P, 2, D // P, FF]
        with ExitStack() as place:
            self.gu = [place.enter_context(nc.sbuf_tensor(f"w_gu{b}", self.shape, F32)) for b in range(2)]
        self.loaded = [[ctx.enter_context(nc.semaphore(f"w_loaded{b}_{j}")) for j in range(NPC)] for b in range(2)]

    def keep(self, nc, ctx):
        _, FF, D = self.src[2].shape
        for b in range(2):
            ctx.enter_context(nc.sbuf_tensor(f"place_gu{b}", self.shape, F32))
        self.d = [ctx.enter_context(nc.sbuf_tensor(f"w_d{b}", [P, FF // P, D], F32)) for b in range(2)]

    def load(self, sp, e, b, j):
        if j < 8:
            n = j // 2
            src = self.src[j % 2][bass.ds(e, 1)].rearrange("e (p k) f -> p (e k) f", p=P)[:, 2 * n:2 * n + 2, :]
            dst = self.gu[b][:, j % 2, 2 * n:2 * n + 2, :]
        else:
            n = j - 8
            src = self.src[2][bass.ds(e, 1)].rearrange("e (p k) d -> p (e k) d", p=P)[:, n:n + 1, :]
            dst = self.d[b][:, n:n + 1, :]
        sp.dma_start(dst, src).then_inc(self.loaded[b][j], 16)

    def gate_up(self, b, j):
        n = j // 2
        return self.gu[b][:, j % 2, 2 * n:2 * n + 2, :].rearrange("p k f -> p (k f)")


def mamba(nc, hacc, lg, weights, x, norm_w, w_in, conv_w, conv_b, dt_bias, a_log, d_skip, y_norm, w_out, acum_dram,
          norm2_w, w_group, w_expert, u2_dram):
    T, D = x.shape
    KD = D // P
    NT = T // P
    NH = GROUPS * R
    DIN = GROUPS * GCH
    XBC = DIN
    DTC = XBC + DIN + 2 * GROUPS * STATE
    CT = (DIN + 2 * GROUPS * STATE) // P
    LASTG = GROUPS - 1

    with ExitStack() as ctx:
        def sb(name, shape, dt=F32):
            return ctx.enter_context(nc.sbuf_tensor(name, shape, dt))

        def sem(name):
            return ctx.enter_context(nc.semaphore(name))

        uTh = sb("uTh", [P, KD, T], F32R)
        uTl = sb("uTl", [P, KD, T], F32R)
        wh = sb("wh", [P, 2, KD, P], F32R)
        wl = sb("wl", [P, 2, KD, P], F32R)
        raw = sb("raw", [P, 2, 512])
        woh = sb("woh", [P, 2, D], F32R)
        wol = sb("wol", [P, 2, D], F32R)
        xr = sb("xr", [P, 2, 3 + HALF])
        v = sb("v", [P, HALF])
        xbc = sb("xbc", [P, 2, 4, T])
        zs = sb("zs", [P, 2, T])
        E = sb("E", [P, 2, R, P])
        xdt = sb("xdt", [P, 2, GCH])
        xds = sb("xds", [P, 2, GCH])
        btok = sb("btok", [P, 2, P])
        cbm = sb("cbm", [P, P])
        S = sb("S", [P, 2, GCH])
        ysb = sb("ysb", [P, GCH])
        ygf = sb("ygf", [P, 2, P])
        sq = sb("sq", [P, 2, P])
        yh = sb("yh", [P, 2, P], F32R)
        yl = sb("yl", [P, 2, P], F32R)
        ms = sb("ms", [P, 2])
        rstd = sb("rstd", [P, 2])
        dtT = sb("dtT", [P, GROUPS, NT, R])
        acum = sb("acum", [P, GROUPS, NT, R])
        eac = sb("eac", [P, GROUPS, NT, R])
        dst = sb("dst", [P, GROUPS, NT, R])
        dch = sb("dch", [P, GROUPS, NT, R])
        ident = sb("ident", [P, P])
        tri = sb("tri", [P, P])
        ones = sb("ones", [P, P])
        cw = sb("cw", [P, TAPS + 1, CT])
        dsk = sb("dsk", [P, 2 * GROUPS])
        nw = sb("nw", [P, 2 * GROUPS])
        alogb = sb("alogb", [P, NH])
        dtb = sb("dtb", [P, NH])
        ssq = sb("ssq", [P, NT])
        msx = sb("msx", [P, NT])
        rsx = sb("rsx", [P, NT])
        mhalf = sb("mhalf", [P, NT])

        junk, xn, wb = xbc[:, 1, 0, :], xbc[:, 1, 1:3, :], xbc[:, 1, 3, :]
        wdt, dtc = xbc[:, 0, 0, :], xbc[:, 0, 1, :]
        tmp = [zs[:, j // 4, 256 * (j % 4):256 * (j % 4) + 256] for j in range(8)]
        acs, rows, dall = sq, ygf, ysb[:, 0:NH]

        NL = EG + NE
        u2, u2T, wb2 = xbc[:, 0, 0:2, :], xbc[:, 0, 2, :].rearrange("p (k l) -> p k l", k=KD), xbc[:, 0, 3, :]
        wr = xr[:, 0, 0:KD * NL].rearrange("p (k n) -> p k n", k=KD)
        junk2 = raw[:].rearrange("p s n -> p (s n)")

        proj_ps = [ctx.enter_context(nc.psum_tensor(f"proj{j}", [P, 512], F32)) for j in range(2)]
        tcb_ps = [ctx.enter_context(nc.psum_tensor(f"tcb{j}", [P, 4, P], F32)) for j in range(2)]
        y_ps = ctx.enter_context(nc.psum_tensor("y_ps", [P, 2, GCH], F32))
        st_ps = ctx.enter_context(nc.psum_tensor("st_ps", [P, 2, GCH], F32))
        out_ps = [ctx.enter_context(nc.psum_tensor(f"out{j}", [P, 512], F32)) for j in range(2)]

        x_loaded = [sem(f"x_loaded{i}") for i in range(NT)]
        consts_loaded = sem("consts_loaded")
        wdt_loaded = sem("wdt_loaded")
        const_steps = sem("const_steps")
        rows_T = sem("rows_T")
        halved = sem("halved")
        sumsq_done = sem("sumsq_done")
        msx_done = sem("msx_done")
        rsx_done = sem("rsx_done")
        xn_done = sem("xn_done")
        xT_done = sem("xT_done")
        uhi_done = sem("uhi_done")
        ulo_done = sem("ulo_done")
        wd_hi = sem("wd_hi")
        wd_lo = sem("wd_lo")
        dt_mm = sem("dt_mm")
        dtc_done = sem("dtc_done")
        dtT_mm = sem("dtT_mm")
        dt_steps = sem("dt_steps")
        dt_act = sem("dt_act")
        cum_mm = sem("cum_mm")
        cum_act = sem("cum_act")
        acT_mm = sem("acT_mm")
        acT_sb = sem("acT_sb")
        acT_stored = sem("acT_stored")
        raw_loaded = [sem(f"raw_loaded{j}") for j in range(2)]
        w_hi = sem("w_hi")
        w_ready = sem("w_ready")
        proj_done = sem("proj_done")
        raw_copied = sem("raw_copied")
        halo_copied = sem("halo_copied")
        conv_steps = sem("conv_steps")
        tanh_done = sem("tanh_done")
        unit_final = sem("unit_final")
        tcb_done = sem("tcb_done")
        btok_done = sem("btok_done")
        xdt_steps = sem("xdt_steps")
        cbm_done = sem("cbm_done")
        e_loaded = [sem(f"e_loaded{j}") for j in range(2)]
        sub_steps = sem("sub_steps")
        exp_done = sem("exp_done")
        m_done = sem("m_done")
        y_mm = sem("y_mm")
        st_mm = sem("st_mm")
        y_steps = sem("y_steps")
        s_steps = sem("s_steps")
        yT_done = sem("yT_done")
        gate_steps = sem("gate_steps")
        sq_done = sem("sq_done")
        yhi_done = sem("yhi_done")
        ylo_done = sem("ylo_done")
        stat_mm = sem("stat_mm")
        ms_done = sem("ms_done")
        rstd_done = sem("rstd_done")
        out_mm = sem("out_mm")
        h_steps = sem("h_steps")
        router_loaded = sem("router_loaded")
        sumsq2_done = sem("sumsq2_done")
        ms2_done = sem("ms2_done")
        rs2_done = sem("rs2_done")
        u2_done = sem("u2_done")
        u2_stored = [sem(f"u2_stored{j}") for j in range(2)]
        u2T_mm = sem("u2T_mm")
        u2T_done = sem("u2T_done")
        lg_mm = sem("lg_mm")
        lg_done = sem("lg_done")

        def val(G, per, add):
            reg, off = G
            return off * per + add if reg is None else reg * (2 * per) + (off * per + add)

        def nxt(G, n=1):
            return (G[0], G[1] + n)

        def gidx(G):
            return val(G, 1, 0)

        def wait(eng, s, G, per, add):
            if G[0] is None and G[1] * per + add <= 0:
                return
            eng.wait_ge(s, val(G, per, add))

        def pick(ap, G):
            return ap[:, bass.ds(gidx(G), 1)] if G[0] is not None else ap[:, G[1]:G[1] + 1]

        def unit_of(G, i):
            return (nxt(G), i - NU) if i >= NU else (G, i)

        def first(G):
            return G[0] is None and G[1] == 0

        def is_last(G):
            return G[0] is None and G[1] == LASTG

        def steps(G):
            last = is_last(G)
            nolater = G[0] is None and G[1] >= LASTG - 1
            plan = {c: [i for i in PLAN[c] if not (last and i >= NU)] for c in PLAN}
            early = {c: [p for p in EARLY.get(c, []) if not (last and p[0] != "wo")] for c in PLAN}
            late = {c: [p for p in LATE.get(c, []) if not last and not (nolater and p[1] >= CYCLE)] for c in PLAN}
            if last:
                early[1] = [("wo", j) for j in range(4)]
            return plan, early, late

        def groups(eng, body):
            with eng.Fori(0, (GROUPS - 2) // 2) as i:
                body((i, 0))
                body((i, 1))
            body((None, LASTG - 1))
            body((None, LASTG))

        def unit_b(plan, c):
            return plan[c][1] if len(plan[c]) > 1 else None

        def piece_wait(eng, s, G, place, extra):
            wait(eng, s, G, CYCLE, FIRST_PIECES + place + extra)

        block = ctx.enter_context(nc.Block())

        MORE = (9, 10)

        def router_tile(last, c, lag):
            k = c - lag
            return k if last and 0 <= k < NT else None

        @block.sync
        def _(sp):
            xt = x.rearrange("(i p) d -> p i d", p=P)
            for i in range(NT):
                sp.dma_start(hacc[:, i, :], xt[:, i, :]).then_inc(x_loaded[i], 16)
                if i == 0:
                    sp.dma_start(wb, norm_w.partition_broadcast(P)).then_inc(consts_loaded, 16)
                    sp.dma_start(dtb[:], dt_bias.partition_broadcast(P)).then_inc(consts_loaded, 16)
                    sp.dma_start(alogb[:], a_log.partition_broadcast(P)).then_inc(consts_loaded, 16)
                    sp.dma_start(dall, d_skip.partition_broadcast(P)).then_inc(consts_loaded, 16)
                    sp.dma_start(rows[:, 0, :], conv_w.rearrange("k (n p) -> (k n) p", p=P)).then_inc(consts_loaded, 16)
                    sp.dma_start(rows[0:CT, 1, :], conv_b.rearrange("(n p) -> n p", p=P)).then_inc(consts_loaded, 16)
                    sp.dma_start(rows[CT:CT + 2 * GROUPS, 1, :], y_norm.rearrange("(n p) -> n p", p=P)
                                 ).then_inc(consts_loaded, 16)
                    sp.dma_start(wdt.rearrange("p (k n) -> p k n", k=KD),
                                 w_in[:, DTC + NH - P:DTC + NH].rearrange("(k p) n -> p k n", p=P)).then_inc(wdt_loaded, 16)

            def column(G, t):
                if t < 2:
                    return val(G, GCH, XBC + t * P)
                if t < 4:
                    return val(G, STATE, XBC + DIN + (t - 2) * GROUPS * STATE)
                return val(G, GCH, (t - 4) * P)

            def load_tile_piece(G, t, half, slot):
                src = w_in[half * 4 * P:(half + 1) * 4 * P, bass.ds(column(G, t), P)].rearrange("(k p) n -> p k n", p=P)
                sp.dma_start(raw[:, slot, :].rearrange("p (k n) -> p k n", k=4), src).then_inc(raw_loaded[slot], 16)

            def load_piece(G, what, place):
                piece_wait(sp, w_ready, G, place, -1)
                if what == "wo":
                    j = place - (0 if is_last(G) else 2)
                    row = val(G, GCH, (j // 2) * P)
                    sp.dma_start(raw[:, place % 2, :], w_out[bass.ds(row, P), (j % 2) * 512:(j % 2) * 512 + 512]
                                 ).then_inc(raw_loaded[place % 2], 16)
                else:
                    load_tile_piece(nxt(G, 2) if place >= CYCLE else nxt(G), what, place % 2, place % 2)

            def load_e(G, c):
                wait(sp, y_mm, G, NT, c - 1)
                src = acum_dram[bass.ds(val(G, NT * R, c * R), R), :].rearrange("r l -> (r l)").partition_broadcast(P)
                sp.dma_start(E[:, c % 2].rearrange("p r l -> p (r l)"), src).then_inc(e_loaded[c % 2], 16)

            for p in range(FIRST_PIECES):
                if p >= 2:
                    sp.wait_ge(w_ready, p - 1)
                load_tile_piece((None, 0), p // 2, p % 2, p % 2)
            G0 = (None, 0)
            for j in range(2):
                sp.wait_ge(acT_sb, j + 1)
                sp.dma_start(acum_dram[j * P:(j + 1) * P, :], acs[:, j, :]).then_inc(acT_stored, 16)
            sp.wait_ge(acT_stored, 32)
            load_e(G0, 0)
            load_e(G0, 1)
            for half in range(2):
                sp.wait_ge(w_ready, FIRST_PIECES + half - 1)
                load_tile_piece((None, 1), 0, half, half)

            def body(G):
                plan, early, late = steps(G)
                last = is_last(G)
                for c in range(1, 9):
                    if c < NT - 1 or not last:
                        load_e(G, c + 1)
                    for what, place in early[c] + late[c]:
                        load_piece(G, what, place)
                    if last and c == 1:
                        wait(sp, gate_steps, G, 24, 1)
                        wait(sp, conv_steps, G, 32, 32)
                        sp.dma_start(wb2, norm2_w.partition_broadcast(P)).then_inc(router_loaded, 16)
                        sp.dma_start(wr[:, :, 0:EG], w_group.rearrange("(k p) n -> p k n", p=P)).then_inc(router_loaded, 16)
                        sp.dma_start(wr[:, :, EG:NL], w_expert.rearrange("(k p) n -> p k n", p=P)).then_inc(router_loaded, 16)
                    if last and c >= 2:
                        load_first_experts(c)
                    store_u2(router_tile(last, c, 3))

            def load_first_experts(c):
                if c == 2:
                    wait(sp, proj_done, (None, LASTG), NU, NU)
                for n in range(3 * (c - 2), min(3 * (c - 1), 16)):
                    weights.load(sp, n // 8, n // 8, n % 8)

            def store_u2(k):
                if k is not None:
                    sp.wait_ge(u2_done, k + 1)
                    sp.dma_start(u2_dram[k * P:(k + 1) * P, :], u2[:, k % 2, :]).then_inc(u2_stored[k % 2], 16)

            groups(sp, body)
            for c in MORE:
                store_u2(router_tile(True, c, 3))
            for j in range(2):
                sp.wait_ge(u2_stored[j], 16 * NT // 2)

        @block.gpsimd
        def _(pool):
            nc.gpsimd.memset(ident[:], 0.0).then_inc(const_steps, 1)
            nc.gpsimd.memset(tri[:], 1.0).then_inc(const_steps, 1)
            nc.gpsimd.memset(ones[:], 1.0).then_inc(const_steps, 1)
            nc.gpsimd.memset(mhalf[:], -0.5).then_inc(const_steps, 1)
            nc.gpsimd.memset(S[:], 0.0).then_inc(const_steps, 1)
            nc.gpsimd.memset(xr[:], 0.0).then_inc(const_steps, 1)
            pool.wait_ge(const_steps, 6)
            nc.gpsimd.affine_select(out=ident[:], in_=ident[:], compare_op=ALU.not_equal, fill=1.0, base=0,
                                    pattern=[[-1, P]], channel_multiplier=1).then_inc(const_steps, 1)
            nc.gpsimd.affine_select(out=tri[:], in_=tri[:], compare_op=ALU.is_ge, fill=0.0, base=0,
                                    pattern=[[1, P]], channel_multiplier=-1).then_inc(const_steps, 1)

            def low(dst, src, hi):
                return nc.gpsimd.tensor_tensor(dst, src, hi.bitcast(F32), ALU.subtract)

            def tile_low(t, half, slot):
                s = (t % 2, slice(half * 4, half * 4 + 4))
                low(wl[:, s[0], s[1], :], raw[:, slot, :].rearrange("p (k n) -> p k n", k=4),
                    wh[:, s[0], s[1], :]).then_inc(w_ready, 1)

            for i in range(NT):
                pool.wait_ge(msx_done, i + 1)
                nc.gpsimd.tensor_tensor(rsx[:, i:i + 1], msx[:, i:i + 1], mhalf[:, i:i + 1], ALU.pow
                                        ).then_inc(rsx_done, 1)
            for p in range(FIRST_PIECES):
                pool.wait_ge(w_hi, p + 1)
                tile_low(p // 2, p % 2, p % 2)

            def piece(G, what, place):
                piece_wait(pool, w_hi, G, place, 1)
                if what == "wo":
                    j = place - (0 if is_last(G) else 2)
                    low(wol[:, j // 2, (j % 2) * 512:(j % 2) * 512 + 512], raw[:, place % 2, :],
                        woh[:, j // 2, (j % 2) * 512:(j % 2) * 512 + 512]).then_inc(w_ready, 1)
                else:
                    tile_low(what, place % 2, place % 2)

            for place in (0, 1):
                piece((None, 0), 0, place)

            def body(G):
                plan, early, late = steps(G)
                last = is_last(G)
                for c in range(1, 9):
                    for what, place in early[c]:
                        piece(G, what, place)
                    k = c - 1
                    wait(pool, ms_done, G, NT, k + 1)
                    nc.gpsimd.tensor_tensor(rstd[:, k % 2:k % 2 + 1], ms[:, k % 2:k % 2 + 1], mhalf[:, 0:1], ALU.pow
                                            ).then_inc(rstd_done, 1)
                    for what, place in late[c]:
                        piece(G, what, place)
                    root_h(router_tile(last, c, 2))

            def root_h(k):
                if k is not None:
                    pool.wait_ge(ms2_done, k + 1)
                    nc.gpsimd.tensor_tensor(rsx[:, k:k + 1], msx[:, k:k + 1], mhalf[:, k:k + 1], ALU.pow).then_inc(rs2_done, 1)

            groups(pool, body)
            root_h(NT - 1)

        @block.scalar
        def _(act):
            def tile_high(t, half):
                slot = half
                nc.scalar.activation(wh[:, t % 2, half * 4:half * 4 + 4, :],
                                     raw[:, slot, :].rearrange("p (k n) -> p k n", k=4), ACT.Copy).then_inc(w_hi, 1)

            def free_slot(G, t):
                wait(act, proj_done, G, NU, (-1, 0, 2, 4, 6, 8)[t])

            act.wait_ge(const_steps, 8)
            def square_x(i):
                act.wait_ge(x_loaded[i], 16)
                if i >= 1:
                    act.wait_ge(sumsq_done, i)
                nc.scalar.activation(junk, hacc[:, i, :], ACT.Square, accum_out=ssq[:, i:i + 1]).then_inc(sumsq_done, 1)

            square_x(0)
            square_x(1)
            for i in range(NT):
                if i + 2 < NT:
                    square_x(i + 2)
                for j in range(2):
                    act.wait_ge(xT_done, 2 * i + j + 1)
                    nc.scalar.activation(uTh[:, 4 * j:4 * j + 4, i * P:(i + 1) * P],
                                         tcb_ps[j][:], ACT.Copy).then_inc(uhi_done, 1)
                if i == 1:
                    for p in range(2):
                        act.wait_ge(raw_loaded[p], 16)
                        tile_high(0, p)
                if i == 2:
                    act.wait_ge(wdt_loaded, 16)
                    nc.scalar.activation(wh[:, 1], wdt.rearrange("p (k n) -> p k n", k=KD), ACT.Copy).then_inc(wd_hi, 1)

            def copy_unit(G, i):
                t, half = UNITS[i]
                wait(act, conv_steps, G, 32, 4 * (i - 1))
                if half == 1:
                    wait(act, raw_copied, G, 8, i)
                    nc.scalar.activation(xr[:, 1, 0:3], xr[:, 0, HALF:HALF + 3], ACT.Copy).then_inc(halo_copied, 1)
                else:
                    wait(act, halo_copied, G, 4, t)
                wait(act, proj_done, G, NU, i + 1)
                nc.scalar.activation(xr[:, half, 3:3 + HALF], proj_ps[i % 2][:], ACT.Copy).then_inc(raw_copied, 1)

            def tanh_unit(G, i, par):
                t, half = UNITS[i]
                cols = slice(half * HALF, half * HALF + HALF)
                if t < 4:
                    wait(act, conv_steps, G, 32, 4 * (i + 1))
                    nc.scalar.activation(xbc[:, par, t, cols], v[:], ACT.Tanh).then_inc(tanh_done, 1)
                else:
                    wait(act, proj_done, G, NU, i + 1)
                    if half == 0:
                        wait(act, gate_steps, G, 24, -12)
                    nc.scalar.activation(zs[:, t - 4, cols], proj_ps[i % 2][:], ACT.Tanh, scale=0.5
                                         ).then_inc(tanh_done, 1)

            def exp_e(G, c):
                wait(act, sub_steps, G, 32, 4 * c + 4)
                e = E[:, c % 2].rearrange("p r l -> p (r l)")
                nc.scalar.activation(e, e, ACT.Exp).then_inc(exp_done, 1)

            def copy_b(G, c):
                wait(act, tcb_done, G, NT, c + 1)
                wait(act, st_mm, G, NT, c - 1)
                nc.scalar.activation(btok[:, c % 2, :], tcb_ps[c % 2][:, 2, :], ACT.Copy).then_inc(btok_done, 1)

            def gated(G, k):
                wait(act, gate_steps, G, 24, 3 * k + 3)
                nc.scalar.activation(sq[:], ygf[:], ACT.Square).then_inc(sq_done, 1)
                for t in range(2):
                    nc.scalar.activation(yh[:, t, :], ygf[:, t, :], ACT.Copy, scale=nw[:, bass.ds(val(G, 2, t), 1)]
                                         ).then_inc(yhi_done, 1)

            def piece(G, what, place):
                n = FIRST_PIECES + place
                wait(act, raw_loaded[place % 2], G, 16 * CYCLE // 2, 16 * (n // 2 + 1))
                if what == "wo":
                    j = place - (0 if is_last(G) else 2)
                    nc.scalar.activation(woh[:, j // 2, (j % 2) * 512:(j % 2) * 512 + 512], raw[:, place % 2, :],
                                         ACT.Copy).then_inc(w_hi, 1)
                else:
                    H = nxt(G, 2) if place >= CYCLE else nxt(G)
                    free_slot(H, what)
                    tile_high(what, place % 2)

            def step_sizes():
                act.wait_ge(dt_steps, 3)
                nc.scalar.activation(tmp[2], tmp[2], ACT.Exp, scale=-1.0).then_inc(dt_act, 1)
                act.wait_ge(consts_loaded, 16 * 7)
                nc.scalar.activation(alogb[:], alogb[:], ACT.Exp).then_inc(dt_act, 1)
                act.wait_ge(dt_steps, 4)
                nc.scalar.activation(tmp[4], tmp[3], ACT.Ln).then_inc(dt_act, 1)

            def decays():
                flat = "p g c r -> p (g c r)"
                act.wait_ge(cum_mm, 2)
                nc.scalar.activation(acum[:].rearrange(flat), y_ps[:, 0, :], ACT.Copy).then_inc(cum_act, 1)
                nc.scalar.activation(eac[:].rearrange(flat), y_ps[:, 0, :], ACT.Exp).then_inc(cum_act, 1)
                nc.scalar.activation(dch[:].rearrange(flat), y_ps[:, 1, :], ACT.Exp).then_inc(cum_act, 1)

            def row_sums():
                flat = "p g c r -> p (g c r)"
                for j in range(2):
                    act.wait_ge(acT_mm, 2)
                    nc.scalar.activation(acs[:, j, :], st_ps[:, 0, j * P:(j + 1) * P], ACT.Copy).then_inc(acT_sb, 1)
                act.wait_ge(dt_steps, 15)
                nc.scalar.activation(dst[:].rearrange(flat), tmp[1], ACT.Exp).then_inc(cum_act, 1)

            G0 = (None, 0)
            for i in range(10):
                t, half = UNITS[i]
                if i == 8:
                    act.wait_ge(cum_act, 4)
                if t < 4:
                    copy_unit(G0, i)
                if i == 0:
                    for j in range(2):
                        act.wait_ge(dt_mm, j + 1)
                        nc.scalar.activation(dtc[:, j * HALF:(j + 1) * HALF], out_ps[j][:], ACT.Copy).then_inc(dtc_done, 1)
                    for p in range(2):
                        act.wait_ge(raw_loaded[p], 32)
                        tile_high(1, p)
                if i == 1:
                    step_sizes()
                if i == 2:
                    decays()
                if i == 3:
                    row_sums()
                tanh_unit(G0, i, 0)
                if half == 0 and t < 4:
                    act.wait_ge(proj_done, 2 * t + 2)
                    for q in (0, 1):
                        act.wait_ge(raw_loaded[q], 16 * (t + 3))
                        tile_high(t + 2, q)
                if i == 6:
                    exp_e(G0, 0)
            copy_b(G0, 0)
            exp_e(G0, 1)
            copy_b(G0, 1)
            tanh_unit(G0, 10, 0)
            for place in (0, 1):
                act.wait_ge(raw_loaded[place], 16 * (FIRST_PIECES // 2 + 1))
                act.wait_ge(proj_done, 11)
                tile_high(0, place)

            def body(G):
                plan, early, late = steps(G)
                last = is_last(G)
                prev_b = None
                for c in range(1, 9):
                    k = c - 1
                    if prev_b is not None and prev_b[1] < 8:
                        copy_unit(*prev_b)
                    turned_h(router_tile(last, c, 3), 0)
                    gated(G, k)
                    square_h(router_tile(last, c, 2))
                    if prev_b is not None:
                        tanh_unit(*prev_b, (G[1] + 1) % 2)
                    if c < NT - 1 or not last:
                        exp_e(G, c + 1)
                    A = unit_of(G, plan[c][0]) if plan[c] else None
                    if A and A[1] < 8:
                        copy_unit(*A)
                    if c == 1:
                        for q in early[c][:2]:
                            piece(G, *q)
                    if c < NT - 1 or not last:
                        copy_b(G, c + 1)
                    for q in early[c][2 if c == 1 else 0:]:
                        piece(G, *q)
                    if A:
                        tanh_unit(*A, A[0][1] % 2)
                    for q in late[c]:
                        piece(G, *q)
                    turned_h(router_tile(last, c, 3), 1)
                    b = unit_b(plan, c)
                    prev_b = unit_of(G, b) if b is not None else None

            def square_h(k):
                if k is None:
                    return
                wait(act, h_steps, (None, LASTG), 2 * NT, 2 * k + 2)
                if k == 0:
                    wait(act, w_ready, (None, LASTG), CYCLE, FIRST_PIECES + 4)
                else:
                    act.wait_ge(sumsq2_done, k)
                nc.scalar.activation(junk2, hacc[:, k, :], ACT.Square, accum_out=ssq[:, k:k + 1]).then_inc(sumsq2_done, 1)

            def turned_h(k, j):
                if k is None:
                    return
                act.wait_ge(u2T_mm, 2 * k + j + 1)
                if k and j == 0:
                    act.wait_ge(lg_mm, k)
                nc.scalar.activation(u2T[:, 4 * j:4 * j + 4, :], proj_ps[0][:].rearrange("p (k l) -> p k l", k=4), ACT.Copy
                                     ).then_inc(u2T_done, 1)

            groups(act, body)
            for c in MORE:
                square_h(router_tile(True, c, 2))
                for j in range(2):
                    turned_h(router_tile(True, c, 3), j)

        @block.vector
        def _(dve):
            vec = nc.vector
            dve.wait_ge(consts_loaded, 16 * 7)
            def mean_square_x(i):
                dve.wait_ge(sumsq_done, i + 1)
                vec.tensor_scalar(msx[:, i:i + 1], ssq[:, i:i + 1], 1.0 / D, EPS, ALU.mult, ALU.add).then_inc(msx_done, 1)

            mean_square_x(0)
            dve.wait_ge(rows_T, 1)
            tT = out_ps[1]
            vec.tensor_scalar(cw[:, 0:TAPS, :].rearrange("p k n -> p (k n)"), tT[:, 0:P], 0.5, None, ALU.mult
                              ).then_inc(halved, 1)
            vec.tensor_scalar(cw[:, TAPS, :], tT[:, P:P + CT], 0.5, None, ALU.mult).then_inc(halved, 1)
            vec.tensor_scalar(nw[:], tT[:, P + CT:P + CT + 2 * GROUPS], 0.5, None, ALU.mult).then_inc(halved, 1)
            dh = dall.rearrange("p (n q) -> p n q", q=2)
            for q in range(2):
                half_p = slice(q * HEAD_DIM, (q + 1) * HEAD_DIM)
                vec.tensor_copy(dsk[half_p, :], dh[half_p, :, q]).then_inc(halved, 1)

            def norm_tile(i):
                dve.wait_ge(rsx_done, i + 1)
                if i >= 2:
                    dve.wait_ge(xT_done, 2 * (i - 1))
                vec.scalar_tensor_tensor(xn[:, i % 2, :], hacc[:, i, :], rsx[:, i:i + 1], wb, ALU.mult, ALU.mult
                                         ).then_inc(xn_done, 1)

            norm_tile(0)
            mean_square_x(1)
            for i in range(NT):
                if i + 1 < NT:
                    norm_tile(i + 1)
                if i + 2 < NT:
                    mean_square_x(i + 2)
                if i == NT // 2:
                    dve.wait_ge(wd_hi, 1)
                    vec.tensor_tensor(wl[:, 1], wdt.rearrange("p (k n) -> p k n", k=KD), wh[:, 1].bitcast(F32), ALU.subtract
                                      ).then_inc(wd_lo, 1)
                for j in range(2):
                    dve.wait_ge(uhi_done, 2 * i + j + 1)
                    cols = slice(i * P, (i + 1) * P)
                    vec.tensor_tensor(uTl[:, 4 * j:4 * j + 4, cols], tcb_ps[j][:],
                                      uTh[:, 4 * j:4 * j + 4, cols].bitcast(F32), ALU.subtract).then_inc(ulo_done, 1)

            count = [0]

            def link(ins):
                count[0] += 1
                ins.then_inc(dt_steps, 1)
                dve.wait_ge(dt_steps, count[0])

            def gcr(ap):
                return ap.rearrange("p (g c r) -> p g c r", g=GROUPS, c=NT)

            def step_sizes():
                dve.wait_ge(dtT_mm, 2)
                b4 = dtb[:].rearrange("p (g r) -> p g r", g=GROUPS)
                for c in range(NT):
                    ins = vec.tensor_tensor(gcr(tmp[0])[:, :, c], tcb_ps[c // 4][:, c % 4, P - NH:P].rearrange("p (g r) -> p g r", g=GROUPS),
                                            b4, ALU.add)
                    if c < NT - 1:
                        ins.then_inc(halved, 1)
                count[0] += 1
                ins.then_inc(dt_steps, 1)
                dve.wait_ge(dt_steps, 1)
                dve.wait_ge(halved, 5 + NT - 1)
                link(vec.tensor_scalar(tmp[1], tmp[0], 0.0, None, ALU.max))
                link(vec.scalar_tensor_tensor(tmp[2], tmp[0], -1.0, tmp[0], ALU.mult, ALU.max))
                dve.wait_ge(dt_act, 1)
                link(vec.tensor_scalar(tmp[3], tmp[2], 1.0, None, ALU.add))
                link(vec.tensor_scalar(tmp[5], tmp[3], -1.0, None, ALU.add))
                link(vec.tensor_scalar(tmp[6], tmp[5], 0.0, None, ALU.is_equal))
                link(vec.tensor_tensor(tmp[5], tmp[5], tmp[6], ALU.add))
                link(vec.reciprocal(tmp[5], tmp[5]))
                dve.wait_ge(dt_act, 3)
                link(vec.tensor_tensor(tmp[4], tmp[4], tmp[6], ALU.add))
                link(vec.tensor_tensor(tmp[4], tmp[4], tmp[5], ALU.mult))
                link(vec.tensor_tensor(tmp[4], tmp[4], tmp[2], ALU.mult))
                dflat = dtT[:].rearrange("p g c r -> p (g c r)")
                link(vec.tensor_tensor(dflat, tmp[4], tmp[1], ALU.add))
                link(vec.tensor_scalar(alogb[:], alogb[:], -1.0, None, ALU.mult))
                a4 = alogb[:].rearrange("p (g r) -> p g r", g=GROUPS)
                for g in range(GROUPS):
                    ins = vec.tensor_tensor(gcr(tmp[7])[:, g], dtT[:, g], a4[:, g:g + 1, :].to_broadcast([P, NT, R]), ALU.mult)
                    if g < GROUPS - 1:
                        ins.then_inc(halved, 1)
                dve.wait_ge(halved, 5 + NT - 1 + GROUPS - 1)
                link(ins)

            def decay_to_end():
                dve.wait_ge(cum_act, 3)
                link(vec.tensor_tensor(tmp[1], y_ps[:, 1, :], acum[:].rearrange("p g c r -> p (g c r)"), ALU.subtract))

            def conv_unit(G, i):
                t, half = UNITS[i]
                wait(dve, raw_copied, G, 8, i + 1)
                prev = i - 1 if i else -5
                wait(dve, unit_final, G, NU, prev + 1)
                n = 4 * i
                tile = (G, 2, t) if t < 2 else (G, 1, 2 * GROUPS + (t - 2) * GROUPS)

                def w(k):
                    return cw[:, k, bass.ds(val(*tile), 1)]

                vec.tensor_scalar(v[:], xr[:, half, 3:3 + HALF], w(3), w(4), ALU.mult, ALU.add
                                  ).then_inc(conv_steps, 1)
                for k in (2, 1, 0):
                    wait(dve, conv_steps, G, 32, n + 3 - k)
                    vec.scalar_tensor_tensor(v[:], xr[:, half, k:k + HALF], w(k), v[:], ALU.mult, ALU.add
                                             ).then_inc(conv_steps, 1)

            def final_unit(G, i, par):
                t, half = UNITS[i]
                cols = slice(half * HALF, half * HALF + HALF)
                wait(dve, tanh_done, G, NU, i + 1)
                if t < 4:
                    dst, src = xbc[:, par, t, cols], v[:]
                else:
                    dst, src = zs[:, t - 4, cols], proj_ps[i % 2][:]
                vec.scalar_tensor_tensor(dst, dst, 1.0, src, ALU.add, ALU.mult).then_inc(unit_final, 1)

            def sub_e(G, c):
                wait(dve, e_loaded[c % 2], G, 16 * NT // 2, 16 * (c // 2 + 1))
                a = pick(acum, G) if c < 8 else pick(acum, nxt(G))
                for r in range(R):
                    e = E[:, c % 2, r, :]
                    vec.tensor_scalar(e, e, a[:, 0, c % 8, r:r + 1], 0.0, ALU.subtract, ALU.min).then_inc(sub_steps, 1)

            def spread(tab, G, c):
                H = G if c < 8 else nxt(G)
                return pick(tab, H)[:, 0, c % 8, :].unsqueeze(2).to_broadcast([P, R, HEAD_DIM])

            def heads(ap):
                return ap.rearrange("p (r q) -> p r q", r=R)

            def prep(G, c):
                wait(dve, btok_done, G, NT, c + 1)
                wait(dve, y_mm, G, NT, c - 1)
                tp = tcb_ps[c % 2]
                vec.tensor_tensor(heads(xdt[:, c % 2, :]), heads(tp[:, 0:2, :].rearrange("p t q -> p (t q)")),
                                  spread(dtT, G, c), ALU.mult).then_inc(xdt_steps, 1)
                wait(dve, m_done, G, NT, c)
                vec.tensor_tensor(cbm[:], tp[:, 3, :], tri[:], ALU.mult).then_inc(cbm_done, 1)
                wait(dve, xdt_steps, G, 2 * NT, 2 * c + 1)
                wait(dve, st_mm, G, NT, c - 1)
                vec.tensor_tensor(heads(xds[:, c % 2, :]), heads(xdt[:, c % 2, :]), spread(dst, G, c), ALU.mult
                                  ).then_inc(xdt_steps, 1)

            def make_m(G, c):
                wait(dve, exp_done, G, NT, c + 1)
                wait(dve, cbm_done, G, NT, c + 1)
                cb = cbm[:].unsqueeze(1).to_broadcast([P, R, P])
                vec.tensor_tensor(E[:, c % 2], E[:, c % 2], cb, ALU.mult).then_inc(m_done, 1)

            def y_and_state(G, c, last_chunk):
                wait(dve, y_mm, G, NT, c + 1)
                wait(dve, yT_done, G, NT, c)
                vec.tensor_tensor(heads(ysb[:]), heads(y_ps[:, 0, :]), spread(eac, G, c), ALU.mult).then_inc(y_steps, 1)
                wait(dve, y_steps, G, 2 * NT, 2 * c + 1)
                vec.tensor_tensor(ysb[:], ysb[:], y_ps[:, 1, :], ALU.add).then_inc(y_steps, 1)
                new = S[:, (c + 1) % 2, :]
                wait(dve, st_mm, G, NT, c + 1)
                if last_chunk:
                    for j in range(2):
                        vec.memset(new[:, j * P:(j + 1) * P], 0.0).then_inc(s_steps, 1)
                    return
                wait(dve, s_steps, G, 2 * NT, 2 * c)
                vec.tensor_tensor(heads(new), heads(S[:, c % 2, :]), spread(dch, G, c), ALU.mult).then_inc(s_steps, 1)
                wait(dve, s_steps, G, 2 * NT, 2 * c + 1)
                vec.tensor_tensor(new, new, st_ps[:, 0, :], ALU.add).then_inc(s_steps, 1)

            def gate(G, k):
                par = G[1] % 2
                cols = slice(k * P, k * P + P)
                wait(dve, yT_done, G, NT, k + 1)
                for t in range(2):
                    vec.scalar_tensor_tensor(ygf[:, t, :], xbc[:, par, t, cols], dsk[:, bass.ds(val(G, 2, t), 1)],
                                             st_ps[:, 1, t * P:(t + 1) * P], ALU.mult, ALU.add).then_inc(gate_steps, 1)
                wait(dve, gate_steps, G, 24, 3 * k + 2)
                wait(dve, unit_final, G, NU, 10 if k < 4 else 12)
                vec.tensor_tensor(ygf[:], ygf[:], zs[:, :, cols], ALU.mult).then_inc(gate_steps, 1)

            def gated_low(G, k):
                wait(dve, yhi_done, G, 2 * NT, 2 * k + 2)
                for t in range(2):
                    vec.scalar_tensor_tensor(yl[:, t, :], ygf[:, t, :], nw[:, bass.ds(val(G, 2, t), 1)],
                                             yh[:, t, :].bitcast(F32), ALU.mult, ALU.subtract).then_inc(ylo_done, 1)

            def mean_square(G, k):
                wait(dve, stat_mm, G, NT, k + 1)
                vec.tensor_scalar(ms[:, k % 2:k % 2 + 1], out_ps[0][:, 0:1], 1.0 / (4 * GCH), EPS, ALU.mult, ALU.add
                                  ).then_inc(ms_done, 1)

            def add_h(G, k, n):
                j = 1 - n
                wait(dve, rstd_done, G, NT, k + 1)
                wait(dve, out_mm, G, 2 * NT, 2 * k + n + 1)
                h = hacc[:, k, j * 512:(j + 1) * 512]
                vec.scalar_tensor_tensor(h, out_ps[j][:], rstd[:, k % 2:k % 2 + 1], h, ALU.mult, ALU.add
                                         ).then_inc(h_steps, 1)

            G0 = (None, 0)
            for i in range(10):
                if UNITS[i][0] < 4:
                    conv_unit(G0, i)
                if i == 6:
                    sub_e(G0, 0)
                final_unit(G0, i, 0)
                if i == 0:
                    step_sizes()
                if i == 2:
                    decay_to_end()
            prep(G0, 0)
            make_m(G0, 0)
            sub_e(G0, 1)
            prep(G0, 1)
            y_and_state(G0, 0, False)
            make_m(G0, 1)
            final_unit(G0, 10, 0)

            def body(G):
                plan, early, late = steps(G)
                last = is_last(G)
                prev_b = None
                for c in range(1, 9):
                    k = c - 1
                    more = c < NT - 1 or not last
                    gate(G, k)
                    if prev_b is not None and prev_b[1] < 8:
                        conv_unit(*prev_b)
                    if more:
                        sub_e(G, c + 1)
                    gated_low(G, k)
                    if prev_b is not None:
                        final_unit(*prev_b, (G[1] + 1) % 2)
                    mean_square_h(router_tile(last, c, 2))
                    if more:
                        prep(G, c + 1)
                    mean_square(G, k)
                    if c < NT or not last:
                        y_and_state(G, c, c == NT - 1)
                    if more:
                        make_m(G, c + 1)
                    A = unit_of(G, plan[c][0]) if plan[c] else None
                    if A and A[1] < 8:
                        conv_unit(*A)
                    add_h(G, k, 0)
                    if A:
                        final_unit(*A, A[0][1] % 2)
                    norm_h(router_tile(last, c, 2))
                    add_h(G, k, 1)
                    b = unit_b(plan, c)
                    prev_b = unit_of(G, b) if b is not None else None

            def mean_square_h(k):
                if k is not None:
                    dve.wait_ge(sumsq2_done, k + 1)
                    vec.tensor_scalar(msx[:, k:k + 1], ssq[:, k:k + 1], 1.0 / D, EPS, ALU.mult, ALU.add).then_inc(ms2_done, 1)

            def norm_h(k):
                if k is None:
                    return
                dve.wait_ge(router_loaded, 48)
                dve.wait_ge(rs2_done, k + 1)
                if k >= 2:
                    dve.wait_ge(u2T_mm, 2 * (k - 1))
                    dve.wait_ge(u2_stored[k % 2], 16 * (k // 2))
                vec.scalar_tensor_tensor(u2[:, k % 2, :], hacc[:, k, :], rsx[:, k:k + 1], wb2, ALU.mult, ALU.mult
                                         ).then_inc(u2_done, 1)

            groups(dve, body)
            mean_square_h(NT - 1)
            norm_h(NT - 1)
            dve.wait_ge(lg_mm, NT)
            vec.tensor_copy(lg[:].rearrange("p i n -> p (i n)"), proj_ps[1][:, 0:NT * NL]).then_inc(lg_done, 1)

        @block.tensor
        def _(pe):
            def mm3(out, ah, al, bh, bl, start, stop):
                nc.tensor.matmul(out, al, bh, start=start, stop=False)
                nc.tensor.matmul(out, ah, bl, start=False, stop=False)
                return nc.tensor.matmul(out, ah, bh, start=False, stop=stop)

            pe.wait_ge(const_steps, 8)
            pe.wait_ge(consts_loaded, 16 * 7)
            nr = CT + 2 * GROUPS
            nc.tensor.transpose(out_ps[1][:, 0:P], rows[:, 0, :], ident[:])
            nc.tensor.transpose(out_ps[1][:, P:P + nr], rows[0:nr, 1, :], ident[0:nr, 0:nr]).then_inc(rows_T, 1)
            def unit(G, i, ks=range(KD)):
                t, half = UNITS[i]
                if first(G):
                    pe.wait_ge(w_ready, 2 * t + 2)
                else:
                    wait(pe, w_ready, nxt(G, -1), CYCLE, FIRST_PIECES + TILE_PLACE[t] + 2)
                if i in (0, 1):
                    wait(pe, unit_final, G, NU, i - 1)
                elif i < 10:
                    wait(pe, raw_copied, G, 8, i - 1)
                else:
                    wait(pe, unit_final, G, NU, i - 1)
                cols = slice(half * HALF, half * HALF + HALF)
                for k in ks:
                    mm = mm3(proj_ps[i % 2][:], wh[:, t % 2, k, :], wl[:, t % 2, k, :],
                             uTh[:, k, cols], uTl[:, k, cols], k == 0, k == KD - 1)
                if ks[-1] == KD - 1:
                    mm.then_inc(proj_done, 1)

            def tcb(G, c):
                H, cc = (G, c) if c < 8 else (nxt(G), c - 8)
                par = H[1] % 2
                cols = slice(cc * P, cc * P + P)
                wait(pe, unit_final, H, NU, 7 if cc < 4 else 8)
                wait(pe, xdt_steps, G, 2 * NT, 2 * (c - 1))
                wait(pe, btok_done, G, NT, c - 1)
                out = tcb_ps[c % 2]
                for t in range(3):
                    nc.tensor.transpose(out[:, t, :], xbc[:, par, t, cols], ident[:])
                nc.tensor.matmul(out[:, 3, :], xbc[:, par, 2, cols], xbc[:, par, 3, cols], start=True, stop=True
                                 ).then_inc(tcb_done, 1)

            def scan(G, c):
                H, cc = (G, c) if c < 8 else (nxt(G), c - 8)
                wait(pe, s_steps, G, 2 * NT, 2 * c)
                wait(pe, y_steps, G, 2 * NT, 2 * c)
                nc.tensor.matmul(y_ps[:, 0, :], xbc[:, H[1] % 2, 3, cc * P:cc * P + P], S[:, c % 2, :], start=True, stop=True)
                wait(pe, m_done, G, NT, c + 1)
                for r in range(R):
                    q = slice(r * HEAD_DIM, (r + 1) * HEAD_DIM)
                    mm = nc.tensor.matmul(y_ps[:, 1, q], E[:, c % 2, r, :], xdt[:, c % 2, q], start=True, stop=True)
                mm.then_inc(y_mm, 1)
                wait(pe, xdt_steps, G, 2 * NT, 2 * c + 2)
                wait(pe, btok_done, G, NT, c + 1)
                wait(pe, gate_steps, G, 24, 3 * c)
                nc.tensor.matmul(st_ps[:, 0, :], btok[:, c % 2, :], xds[:, c % 2, :], start=True, stop=True).then_inc(st_mm, 1)

            def turn_y(G, c):
                wait(pe, y_steps, G, 2 * NT, 2 * c + 2)
                wait(pe, s_steps, G, 2 * NT, 2 * c + 2)
                for t in range(2):
                    mm = nc.tensor.transpose(st_ps[:, 1, t * P:(t + 1) * P], ysb[:, t * P:(t + 1) * P], ident[:])
                mm.then_inc(yT_done, 1)

            def sum_squares(G, k):
                wait(pe, sq_done, G, NT, k + 1)
                for t in range(2):
                    mm = nc.tensor.matmul(out_ps[0][:, 0:1], sq[:, t, :], ones[:, 0:1], start=(t == 0), stop=(t == 1))
                mm.then_inc(stat_mm, 1)

            def project_out(G, k):
                wait(pe, ylo_done, G, 2 * NT, 2 * k + 2)
                if k == 0:
                    wait(pe, w_ready, G, CYCLE, FIRST_PIECES + (4 if is_last(G) else 6))
                for j in (1, 0):
                    if j == 0:
                        wait(pe, ms_done, G, NT, k + 1)
                    for t in range(2):
                        cols = slice(j * 512, (j + 1) * 512)
                        mm = mm3(out_ps[j][:], yh[:, t, :], yl[:, t, :], woh[:, t, cols], wol[:, t, cols],
                                 t == 0, t == 1)
                    mm.then_inc(out_mm, 1)

            G0 = (None, 0)
            for i in range(NT):
                pe.wait_ge(xn_done, i + 1)
                for j in range(2):
                    if i >= 1:
                        pe.wait_ge(ulo_done, 2 * (i - 1) + j + 1)
                    for k in range(4):
                        col = (4 * j + k) * P
                        mm = nc.tensor.transpose(tcb_ps[j][:, k, :], xn[:, i % 2, col:col + P], ident[:])
                    mm.then_inc(xT_done, 1)
                if i >= NT // 2:
                    unit(G0, 0, range(2 * i - NT, 2 * i - NT + 2))
            pe.wait_ge(wd_lo, 1)
            pe.wait_ge(halved, 3)
            for j in range(2):
                pe.wait_ge(ulo_done, NT * (j + 1))
                for k in range(KD):
                    mm = mm3(out_ps[j][:], wh[:, 1, k, :], wl[:, 1, k, :], uTh[:, k, j * HALF:(j + 1) * HALF],
                             uTl[:, k, j * HALF:(j + 1) * HALF], k == 0, k == KD - 1)
                mm.then_inc(dt_mm, 1)
            for c in range(NT):
                pe.wait_ge(dtc_done, c // 4 + 1)
                mm = nc.tensor.transpose(tcb_ps[c // 4][:, c % 4, :], dtc[:, c * P:(c + 1) * P], ident[:])
                if c % 4 == 3:
                    mm.then_inc(dtT_mm, 1)
            unit(G0, 1)
            unit(G0, 2)
            pe.wait_ge(dt_steps, 14)
            nc.tensor.matmul(y_ps[:, 0, :], tri[:], tmp[7], start=True, stop=True).then_inc(cum_mm, 1)
            nc.tensor.matmul(y_ps[:, 1, :], ones[:], tmp[7], start=True, stop=True).then_inc(cum_mm, 1)
            unit(G0, 3)
            pe.wait_ge(cum_act, 1)
            af = acum[:].rearrange("p g c r -> p (g c r)")
            for j in range(2):
                nc.tensor.transpose(st_ps[:, 0, j * P:(j + 1) * P], af[:, j * P:(j + 1) * P], ident[:]).then_inc(acT_mm, 1)
            for i in range(4, 10):
                unit(G0, i)
            tcb(G0, 0)
            unit(G0, 10)
            tcb(G0, 1)
            pe.wait_ge(acT_sb, 2)
            scan(G0, 0)
            turn_y(G0, 0)

            def body(G):
                plan, early, late = steps(G)
                last = is_last(G)
                for c in range(1, 9):
                    if plan[c]:
                        unit(*unit_of(G, plan[c][0]))
                    turn_h(router_tile(last, c, 3), 0)
                    if c < NT - 1 or not last:
                        tcb(G, c + 1)
                    sum_squares(G, c - 1)
                    if c < NT or not last:
                        scan(G, c)
                    b = unit_b(plan, c)
                    if b is not None and c == 1:
                        unit(*unit_of(G, b))
                    turn_h(router_tile(last, c, 3), 1)
                    project_out(G, c - 1)
                    if b is not None and c > 1:
                        unit(*unit_of(G, b))
                    if c < NT or not last:
                        turn_y(G, c)
                    logits(router_tile(last, c, 3))

            def turn_h(k, j):
                if k is None:
                    return
                pe.wait_ge(u2_done, k + 1)
                wait(pe, unit_final, (None, LASTG), NU, NU)
                if k or j:
                    pe.wait_ge(u2T_done, 2 * k + j)
                for q in range(4):
                    col = (4 * j + q) * P
                    mm = nc.tensor.transpose(proj_ps[0][:, q * P:(q + 1) * P], u2[:, k % 2, col:col + P], ident[:])
                mm.then_inc(u2T_mm, 1)

            def logits(k):
                if k is None:
                    return
                pe.wait_ge(u2T_done, 2 * k + 2)
                pe.wait_ge(router_loaded, 48)
                for q in range(KD):
                    mm = nc.tensor.matmul(proj_ps[1][:, k * NL:(k + 1) * NL], u2T[:, q, :], wr[:, q, :],
                                          start=(q == 0), stop=(q == KD - 1))
                mm.then_inc(lg_mm, 1)

            groups(pe, body)
            for c in MORE:
                k = router_tile(True, c, 3)
                for j in range(2):
                    turn_h(k, j)
                logits(k)


def routing(nc, lg, ridx, etab, npairs, wtok, weights, xg, zero, ident, b_group, b_expert):
    NT = lg.shape[1]
    NL = EG + NE
    NTH = NT * P // P - 1

    with ExitStack() as ctx:
        def sb(name, shape, dt=F32):
            return ctx.enter_context(nc.sbuf_tensor(name, shape, dt))

        def sem(name):
            return ctx.enter_context(nc.semaphore(name))

        def psum(name, shape):
            return ctx.enter_context(nc.psum_tensor(name, shape, F32))

        biasb = sb("biasb", [P, NL])
        ones = sb("ones2", [P, P])
        below = sb("below", [P, P])
        stats = sb("stats", [P, 4, NT])
        iota_e = sb("iota_e", [P, NE])
        rev_e = sb("rev_e", [P, NE])
        iota_b = sb("iota_b", [P, MAXB])
        iota_p = sb("iota_p", [P, P])
        thr = sb("thr", [P, NTH])
        toki = sb("toki", [P, NT])
        el = sb("el", [P, NT, NE])
        ta = sb("ta", [P, NT, NE])
        tb = sb("tb", [P, 2, NT, NE])
        M = sb("M", [P, 2, NT, NE])
        A = sb("A", [P, NT, NE])
        pre = sb("pre", [P, NT + 1, NE])
        gs = sb("gs", [P, NT, EG])
        g1 = sb("g1", [P, NT, EG])
        g2 = sb("g2", [P, NT, EG])
        s8 = sb("s8", [P, 16, NT])
        sc = sb("sc", [P, 8, 2, NT])
        cmp = sb("cmp", [P, NE * NE])
        eq = sb("eq", [P, NT, MAXB])
        src = sb("src", [P, 2, NT, 2])
        extra = sb("extra", [P, NE])
        scan = sb("scan2", [P, 2, 16 + NE])
        start = sb("start", [P, NE])
        hot = sb("hot", [P, 2 * NT, P])
        vals = sb("vals", [P, 2 * NT, 2, MAXB])
        ef = sb("ef", [P, MAXB])
        nf = sb("nf", [P, 2])

        rank_ps = psum("rank_ps", [P, NT, NE])
        cnt_ps = psum("cnt_ps", [P, NE])
        tab_ps = psum("tab_ps", [P, 2, MAXB])

        loaded = sem("loaded2")
        const_steps = sem("const_steps2")
        steps = sem("steps2")
        act_exp = sem("act_exp2")
        rank_mm = sem("rank_mm")
        hot_done = sem("hot_done")
        tab_mm = sem("tab_mm")

        block = ctx.enter_context(nc.Block())

        @block.sync
        def _(sp):
            sp.dma_start(biasb[:, 0:EG], b_group.partition_broadcast(P)).then_inc(loaded, 16)
            sp.dma_start(biasb[:, EG:NL], b_expert.partition_broadcast(P)).then_inc(loaded, 16)
            for b in range(2):
                for j in range(8, NPC):
                    weights.load(sp, b, b, j)

        @block.gpsimd
        def _(pool):
            g = nc.gpsimd
            g.memset(below[:], 1.0).then_inc(const_steps, 1)
            g.memset(ones[:], 1.0).then_inc(const_steps, 1)
            g.memset(pre[:, 0, :], 0.0).then_inc(const_steps, 1)
            g.memset(scan[:], 0.0).then_inc(const_steps, 1)
            exact = dict(allow_small_or_imprecise_dtypes=True)
            g.iota(iota_e[:], pattern=[[1, NE]], base=0, channel_multiplier=0, **exact).then_inc(const_steps, 1)
            g.iota(rev_e[:], pattern=[[-1, NE]], base=NE, channel_multiplier=0, **exact).then_inc(const_steps, 1)
            g.iota(iota_b[:], pattern=[[1, MAXB]], base=0, channel_multiplier=0, **exact).then_inc(const_steps, 1)
            g.iota(iota_p[:], pattern=[[1, P]], base=0, channel_multiplier=0, **exact).then_inc(const_steps, 1)
            g.iota(thr[:], pattern=[[P, NTH]], base=P, channel_multiplier=0, **exact).then_inc(const_steps, 1)
            g.iota(toki[:], pattern=[[P, NT]], base=0, channel_multiplier=1, **exact).then_inc(const_steps, 1)
            pool.wait_ge(const_steps, 10)
            g.affine_select(out=below[:], in_=below[:], compare_op=ALU.is_gt, fill=0.0, base=0,
                            pattern=[[1, P]], channel_multiplier=-1).then_inc(const_steps, 1)
            g.memset(ident[:], 0.0).then_inc(const_steps, 1)
            g.memset(xg[:], 0.0).then_inc(const_steps, 1)
            g.memset(zero[:], 0).then_inc(const_steps, 1)
            pool.wait_ge(const_steps, 14)
            g.affine_select(out=ident[:], in_=ident[:], compare_op=ALU.not_equal, fill=1.0, base=0,
                            pattern=[[-1, P]], channel_multiplier=1).then_inc(const_steps, 1)

        @block.scalar
        def _(act):
            act.wait_ge(steps, 7)
            nc.scalar.activation(g2[:], g1[:], ACT.Exp).then_inc(act_exp, 1)
            act.wait_ge(steps, 24)
            nc.scalar.activation(s8[:, 7, :], s8[:, 6, :], ACT.Exp).then_inc(act_exp, 1)

        @block.tensor
        def _(pe):
            pe.wait_ge(const_steps, 11)

            pe.wait_ge(steps, 29 + NT)
            flat = "p i e -> p (i e)"
            nc.tensor.matmul(rank_ps[:].rearrange(flat), below[:], A[:].rearrange(flat), start=True, stop=False)
            nc.tensor.matmul(rank_ps[:].rearrange(flat), ones[:], pre[:, 0:NT, :].rearrange(flat), start=False, stop=True)
            nc.tensor.matmul(cnt_ps[:], ones[:], pre[:, NT, :], start=True, stop=True).then_inc(rank_mm, 1)
            for n in range(2 * NT):
                if n % 4 == 0:
                    pe.wait_ge(hot_done, n // 2 + 2)
                nc.tensor.matmul(tab_ps[:].rearrange("p v b -> p (v b)"), hot[:, n, :],
                                 vals[:, n].rearrange("p v b -> p (v b)"), start=(n == 0), stop=(n == 2 * NT - 1)
                                 ).then_inc(tab_mm, 1)

        @block.vector
        def _(dve):
            vec = nc.vector
            count = [0]

            def link(ins):
                count[0] += 1
                ins.then_inc(steps, 1)
                dve.wait_ge(steps, count[0])

            def over(ap, n):
                return ap.unsqueeze(2).to_broadcast([P, NT, n])

            def each(ap, n):
                return ap.unsqueeze(1).to_broadcast([P, NT, n])

            dve.wait_ge(const_steps, 11)
            dve.wait_ge(loaded, 16 * 2)
            link(vec.tensor_tensor(lg[:], lg[:], each(biasb[:], NL), ALU.add))
            gl = lg[:, :, 0:EG]
            link(vec.tensor_reduce(s8[:, 0, :], gl, AX.X, ALU.max))
            link(vec.tensor_tensor(g1[:], gl, over(s8[:, 0, :], EG), ALU.is_ge))
            link(vec.tensor_tensor(g1[:], g1[:], each(rev_e[:, NE - EG:NE], EG), ALU.mult))
            link(vec.tensor_reduce(s8[:, 1, :], g1[:], AX.X, ALU.max))
            link(vec.tensor_tensor(gs[:], each(rev_e[:, NE - EG:NE], EG), over(s8[:, 1, :], EG), ALU.is_equal))
            link(vec.tensor_tensor(g1[:], gl, over(s8[:, 0, :], EG), ALU.subtract))
            dve.wait_ge(act_exp, 1)
            link(vec.tensor_reduce(s8[:, 2, :], g2[:], AX.X, ALU.add))
            link(vec.reciprocal(s8[:, 3, :], s8[:, 2, :]))
            link(vec.tensor_scalar(g1[:], gs[:], 1e30, -1e30, ALU.mult, ALU.add))
            for g in range(EG):
                q = slice(g * EPG, (g + 1) * EPG)
                link(vec.tensor_tensor(el[:, :, q], lg[:, :, EG + g * EPG:EG + (g + 1) * EPG],
                                       over(gs[:, :, g], EPG), ALU.mult))
            pen = g1[:].rearrange("p i g -> p (i g)").unsqueeze(2).to_broadcast([P, NT * EG, EPG])
            ev = el[:].rearrange("p i (g e) -> p (i g) e", g=EG)
            link(vec.tensor_tensor(ev, ev, pen, ALU.add))

            def top(n, mx, first):
                link(vec.tensor_reduce(s8[:, mx, :], el[:], AX.X, ALU.max))
                link(vec.tensor_tensor(ta[:], el[:], over(s8[:, mx, :], NE), ALU.is_ge))
                link(vec.tensor_tensor(ta[:], ta[:], each(rev_e[:], NE), ALU.mult))
                link(vec.tensor_reduce(s8[:, first, :], ta[:], AX.X, ALU.max))
                link(vec.tensor_tensor(M[:, n], each(rev_e[:], NE), over(s8[:, first, :], NE), ALU.is_equal))

            top(0, 4, 5)
            fl = "p i e -> p (i e)"
            link(vec.scalar_tensor_tensor(el[:].rearrange(fl), M[:, 0].rearrange(fl), -3e30, el[:].rearrange(fl),
                                          ALU.mult, ALU.add))
            link(vec.tensor_reduce(s8[:, 6, :], el[:], AX.X, ALU.max))
            link(vec.tensor_copy(s8[:, 8, :], s8[:, 6, :]))
            link(vec.tensor_tensor(s8[:, 6, :], s8[:, 6, :], s8[:, 4, :], ALU.subtract))
            link(vec.tensor_tensor(ta[:], el[:], over(s8[:, 8, :], NE), ALU.is_ge))
            link(vec.tensor_tensor(ta[:], ta[:], each(rev_e[:], NE), ALU.mult))
            link(vec.tensor_reduce(s8[:, 9, :], ta[:], AX.X, ALU.max))
            link(vec.tensor_tensor(M[:, 1], each(rev_e[:], NE), over(s8[:, 9, :], NE), ALU.is_equal))
            link(vec.tensor_tensor(A[:], M[:, 0], M[:, 1], ALU.add))
            for i in range(NT):
                link(vec.tensor_tensor(pre[:, i + 1, :], pre[:, i, :], A[:, i, :], ALU.add))
            dve.wait_ge(act_exp, 2)
            link(vec.tensor_scalar(s8[:, 10, :], s8[:, 7, :], 1.0, None, ALU.add))
            link(vec.reciprocal(s8[:, 10, :], s8[:, 10, :]))
            link(vec.tensor_tensor(wtok[:, 0, :], s8[:, 3, :], s8[:, 10, :], ALU.mult))
            link(vec.tensor_tensor(wtok[:, 1, :], wtok[:, 0, :], s8[:, 7, :], ALU.mult))
            for k in range(2):
                link(vec.tensor_scalar(src[:, k, :, 0], toki[:], -PADROW, None, ALU.add))
                link(vec.tensor_scalar(src[:, k, :, 1], toki[:], 2.0, k - PADROW, ALU.mult, ALU.add))

            def look_up(table, at):
                link(vec.tensor_tensor(tb[:], M[:], table.unsqueeze(1).to_broadcast([P, 2, NT, NE]), ALU.mult))
                link(vec.tensor_reduce(sc[:, at], tb[:], AX.X, ALU.add))

            look_up(each(iota_e[:], NE), 1)
            dve.wait_ge(rank_mm, 1)
            c3 = cmp[:, 0:NE * NTH].rearrange("p (e j) -> p e j", e=NE)
            link(vec.tensor_tensor(c3, cnt_ps[:].unsqueeze(2).to_broadcast([P, NE, NTH]),
                                   thr[:].unsqueeze(1).to_broadcast([P, NE, NTH]), ALU.is_gt))
            link(vec.tensor_reduce(extra[:], c3, AX.X, ALU.add))
            link(vec.tensor_copy(scan[:, 0, 16:16 + NE], extra[:]))
            for n in range(5):
                a, b = scan[:, n % 2, :], scan[:, (n + 1) % 2, :]
                link(vec.tensor_tensor(b[:, 16:16 + NE], a[:, 16:16 + NE], a[:, 16 - (1 << n):16 + NE - (1 << n)], ALU.add))
            incl = scan[:, 1, 16:16 + NE]
            link(vec.tensor_tensor(start[:], incl, extra[:], ALU.subtract))
            look_up(rank_ps[:], 0)
            look_up(each(start[:], NE), 2)
            rank, expert, first_extra, before, block_of, place = (sc[:, n].rearrange("p c i -> p (c i)") for n in range(6))
            N = 2 * NT
            c3 = cmp[:, 0:N * NTH].rearrange("p (n j) -> p n j", n=N)
            link(vec.tensor_tensor(c3, rank.unsqueeze(2).to_broadcast([P, N, NTH]),
                                   thr[:].unsqueeze(1).to_broadcast([P, N, NTH]), ALU.is_ge))
            link(vec.tensor_reduce(before, c3, AX.X, ALU.add))
            link(vec.scalar_tensor_tensor(place, before, -float(P), rank, ALU.mult, ALU.add))
            link(vec.tensor_tensor(block_of, first_extra, before, ALU.add))
            link(vec.tensor_tensor(block_of, block_of, expert, ALU.subtract))
            link(vec.tensor_scalar(block_of, block_of, float(NE - 1), None, ALU.add))
            link(vec.tensor_scalar(before, before, 0.0, None, ALU.is_gt))
            link(vec.tensor_tensor(block_of, block_of, before, ALU.mult))
            link(vec.tensor_tensor(block_of, block_of, expert, ALU.add))
            for q in range(4):
                n = slice(q * 4, q * 4 + 4)
                vec.tensor_tensor(hot[:, n], iota_p[:].unsqueeze(1).to_broadcast([P, 4, P]),
                                  place[:, n].unsqueeze(2).to_broadcast([P, 4, P]), ALU.is_equal).then_inc(hot_done, 1)
                e = eq[:, (q % 2) * 4:(q % 2) * 4 + 4]
                link(vec.tensor_tensor(e, iota_b[:].unsqueeze(1).to_broadcast([P, 4, MAXB]),
                                       block_of[:, n].unsqueeze(2).to_broadcast([P, 4, MAXB]), ALU.is_equal))
                vec.tensor_tensor(vals[:, n], e.unsqueeze(2).to_broadcast([P, 4, 2, MAXB]),
                                  src[:].rearrange("p c i v -> p (c i) v")[:, n].unsqueeze(3).to_broadcast([P, 4, 2, MAXB]),
                                  ALU.mult).then_inc(hot_done, 1)
            link(vec.tensor_copy(ef[:], iota_b[:]))
            c3 = cmp[:, 0:16 * NE].rearrange("p (j e) -> p j e", j=16)
            link(vec.tensor_tensor(c3, incl.unsqueeze(1).to_broadcast([P, 16, NE]),
                                   iota_b[:, 0:16].unsqueeze(2).to_broadcast([P, 16, NE]), ALU.is_le))
            link(vec.tensor_reduce(ef[:, NE:NE + 16], c3, AX.X, ALU.add))
            link(vec.tensor_scalar(ef[:], ef[:], float(NE - 1), None, ALU.min))
            link(vec.tensor_copy(etab[:], ef[:]))
            link(vec.tensor_scalar(cmp[:, 0:8], iota_b[:, 0:8], 2.0, incl[:, NE - 1:NE], ALU.mult, ALU.is_lt))
            link(vec.tensor_reduce(nf[:, 0:1], cmp[:, 0:8], AX.X, ALU.add))
            for k in range(3):
                link(vec.tensor_scalar(npairs[:, k:k + 1], nf[:, 0:1], float(NE // 2 - 1 - k), None, ALU.add))
            dve.wait_ge(tab_mm, 2 * NT)
            link(vec.tensor_scalar(ridx[:], tab_ps[:], PADROW, None, ALU.add))


def experts(nc, hacc, ridx, etab, npairs, wtok, weights, xg, zero, ident, u2_dram, y_dram, out):
    _, D, FF = weights.src[0].shape
    KD = D // P
    KF = FF // P
    NT = hacc.shape[1]
    T = NT * P
    RING = 4

    with ExitStack() as ctx:
        def sb(name, shape, dt=F32):
            return ctx.enter_context(nc.sbuf_tensor(name, shape, dt))

        def sem(name):
            return ctx.enter_context(nc.semaphore(name))

        def psum(name, shape):
            return ctx.enter_context(nc.psum_tensor(name, shape, F32))

        wh = sb("gu_hi", [P, RING, 2 * FF], F32R)
        wl = sb("gu_lo", [P, RING, 2 * FF], F32R)
        xTh = sb("xTh", [P, 2, KD, P], F32R)
        xTl = sb("xTl", [P, 2, KD, P], F32R)
        hid = sb("hid", [P, FF])
        hT = sb("hT", [P, 2, KF, P])
        yb = sb("yb", [P, 2, D])
        gidx = sb("gidx", [P, 2, 1], I32)
        sidx = sb("sidx", [P, 2, 1], I32)
        gtmp = sb("gtmp", [P, 2, 1], I32)
        stmp = sb("stmp", [P, 2, 1], I32)
        held = sb("held", [P, 2, 1], I32)
        tp = [psum(f"tp3_{j}", [P, 4, P]) for j in range(2)]
        g_ps = psum("g_ps", [P, FF])
        u_ps = psum("u_ps", [P, FF])
        hT_ps = psum("hT_ps", [P, KF, P])
        y_ps = [psum(f"y3_{j}", [P, 512]) for j in range(2)]
        y2 = [weights.gu[j // 2][:].rearrange("p a k f -> p (a k f)")[:, (j % 2) * 2 * D:(j % 2 + 1) * 2 * D]
              .rearrange("p (c d) -> p c d", c=2) for j in range(4)]

        w_hi = sem("w_hi3")
        w_lo = sem("w_lo3")
        w_used = sem("w_used3")
        d_used = sem("d_used")
        gidx_done = sem("gidx_done")
        sidx_done = sem("sidx_done")
        gathered = [sem(f"gathered{b}") for b in range(2)]
        scattered = [sem(f"scattered{b}") for b in range(2)]
        turned = sem("turned3")
        xT_hi = sem("xT_hi3")
        xT_lo = sem("xT_lo3")
        silu_done = sem("silu_done")
        hid_done = sem("hid_done")
        hT_mm = sem("hT_mm")
        hT_done = sem("hT_done3")
        y_mm = sem("y_mm3")
        y_done = sem("y_done3")
        y2_loaded = [sem(f"y2_loaded{j}") for j in range(4)]
        comb = sem("comb")
        out_stored = sem("out_stored")

        def val(p, b, per, add):
            reg, off = p
            add += (2 * off + b) * per
            return add if reg is None else reg * (2 * per) + add

        FIRST = (None, 0)

        def shifted(p, n):
            return p[0], p[1] + n

        def wait(eng, s, p, b, per, add):
            if p[0] is None and val(p, b, per, add) <= 0:
                return
            eng.wait_ge(s, val(p, b, per, add))

        def pairs(eng, body, peeled=1):
            def less(k):
                return eng.value_load(npairs[0:1, k - 1:k], min_val=NE // 2 - k, max_val=NE // 2 + 8 - k)

            for n in range(peeled):
                body((None, n), False)
            with eng.Fori(peeled, less(1)) as p:
                body((p, 0), False)
            last = (less(1 + peeled), peeled)
            body(last, True)
            return last

        block = ctx.enter_context(nc.Block())

        @block.sync
        def _(sp):
            def body(p, last):
                if p[0] is None and p[1] == 0:
                    return
                for b in range(2):
                    e = sp.value_load(etab[0:1, bass.ds(val(p, b, 1, 0), 1)], min_val=0, max_val=NE - 1)
                    for j in range(8):
                        wait(sp, w_lo, p, b, 8, j + 1 - 16)
                        weights.load(sp, e, b, j)
                    if p[0] is not None or b == 1:
                        load_down(p, b - 1)

            def load_down(p, b):
                e = sp.value_load(etab[0:1, bass.ds(val(p, b, 1, 0), 1)], min_val=0, max_val=NE - 1)
                for k in range(KF):
                    if k < KF - 1:
                        wait(sp, d_used, p, b, 3, k + 1 - 6)
                    else:
                        wait(sp, y_mm, p, b, 2, -2)
                    weights.load(sp, e, b % 2, 8 + k)

            last = pairs(sp, body, peeled=2)
            load_down(last, 1)
            for b in range(2):
                sp.wait_ge(scattered[b], val(last, 0, 8, 16))
            yv = y_dram.rearrange("(i p c) d -> p i c d", p=P, c=2)
            ov = out.rearrange("(i p) d -> p i d", p=P)
            for i in range(NT + 3):
                if i < NT:
                    if i >= 4:
                        sp.wait_ge(comb, 2 * (i - 3))
                    sp.dma_start(y2[i % 4], yv[:, i]).then_inc(y2_loaded[i % 4], 16)
                if i >= 3:
                    sp.wait_ge(comb, 2 * (i - 2))
                    sp.dma_start(ov[:, i - 3, :], hacc[:, i - 3, :]).then_inc(out_stored, 16)
            sp.wait_ge(out_stored, 16 * NT)

        @block.gpsimd
        def _(pool):
            g = nc.gpsimd
            last_token, last_row = pool.to_reg(T - 1), pool.to_reg(2 * T - 1)

            def gather(p, b, ahead):
                par = (b + ahead) % 2
                wait(pool, turned, p, b, 2, 2 * (ahead - 1))
                g.tensor_copy(gtmp[:, par, :], ridx[:, 0, bass.ds(val(p, b, 1, ahead), 1)]).then_inc(gidx_done, 1)
                wait(pool, gidx_done, p, b, 3, 3 * ahead + 1)
                g.tensor_tensor(gidx[:, par, :], gtmp[:, par, :], zero[:], ALU.add).then_inc(gidx_done, 1)
                wait(pool, gidx_done, p, b, 3, 3 * ahead + 2)
                g.tensor_tensor(held[:, 0, :], zero[:], zero[:], ALU.add).then_inc(gidx_done, 1)
                g.indirect_dma_start(xg[:, par, :], None, u2_dram,
                                     bass.IndirectOffsetOnAxis(gidx[:, par, :].bitcast(U32), 0),
                                     bounds_check=last_token, oob_is_err=False).then_inc(gathered[par], 16)

            def scatter(p, b):
                wait(pool, scattered[b], p, 0, 8, 0)
                g.tensor_copy(stmp[:, b, :], ridx[:, 1, bass.ds(val(p, b, 1, 0), 1)]).then_inc(sidx_done, 1)
                wait(pool, sidx_done, p, b, 3, 1)
                wait(pool, y_done, p, b, 2, 2)
                g.tensor_tensor(sidx[:, b, :], stmp[:, b, :], zero[:], ALU.add).then_inc(sidx_done, 1)
                wait(pool, sidx_done, p, b, 3, 2)
                g.tensor_tensor(held[:, 1, :], zero[:], zero[:], ALU.add).then_inc(sidx_done, 1)
                g.indirect_dma_start(y_dram, bass.IndirectOffsetOnAxis(sidx[:, b, :].bitcast(U32), 0), yb[:, b, :], None,
                                     bounds_check=last_row, oob_is_err=False).then_inc(scattered[b], 16)

            def body(p, last):
                for b in range(2):
                    if not last:
                        gather(p, b, 3)
                    if b == 1:
                        scatter(p, 0)
                    elif p[0] is not None or p[1]:
                        scatter(shifted(p, -1), 1)

            for ahead in range(3):
                gather(FIRST, 0, ahead)
            last = pairs(pool, body, peeled=2)
            scatter(last, 1)
            pool.wait_ge(gathered[0], val(last, 0, 8, 32))

        @block.scalar
        def _(act):
            def turn_x(p, b, ahead):
                par = (b + ahead) % 2
                for j in range(2):
                    wait(act, turned, p, b, 2, 2 * ahead + j + 1)
                    nc.scalar.activation(xTh[:, par, 4 * j:4 * j + 4, :], tp[j][:], ACT.Copy).then_inc(xT_hi, 1)

            def split(p, b, j):
                act.wait_ge(weights.loaded[b][j], val(p, 0, 8, 16))
                wait(act, w_used, p, b, 8, j + 1 - RING)
                nc.scalar.activation(wh[:, j % RING, :], weights.gate_up(b, j), ACT.Copy).then_inc(w_hi, 1)

            def body(p, last):
                for b in range(2):
                    for j in range(RING, 8):
                        split(p, b, j)
                    if b == 0 or not last:
                        for j in range(RING):
                            split(*((p, 1) if b == 0 else (shifted(p, 1), 0)), j)
                        turn_x(p, b, 1)
                    wait(act, w_used, p, b, 8, 7)
                    wait(act, hT_mm, p, b, 1, 0)
                    nc.scalar.activation(hid[:], g_ps[:], ACT.Silu).then_inc(silu_done, 1)

            for j in range(RING):
                split(FIRST, 0, j)
            turn_x(FIRST, 0, 0)
            pairs(act, body)

        @block.tensor
        def _(pe):
            def turn_x(p, b, ahead):
                par = (b + ahead) % 2
                pe.wait_ge(gathered[par], val(p, 0, 8, 16 + 16 * ((b + ahead) // 2)))
                wait(pe, xT_lo, p, b, 2, 2 * ahead)
                xk = xg[:, par, :].rearrange("p (q k) -> p k q", k=KD)
                for j in range(2):
                    for k in range(4):
                        mm = nc.tensor.transpose(tp[j][:, k, :], xk[:, 4 * j + k, :], ident[:])
                    mm.then_inc(turned, 1)

            def gate_up(p, b):
                wait(pe, xT_lo, p, b, 2, 2)
                wait(pe, hid_done, p, b, 1, 0)
                for j in range(8):
                    ps = (g_ps, u_ps)[j % 2]
                    wait(pe, w_lo, p, b, 8, j + 1)
                    for i in range(2):
                        k = j // 2 * 2 + i
                        f = slice(i * FF, (i + 1) * FF)
                        nc.tensor.matmul(ps[:], xTl[:, b, k, :], wh[:, j % RING, f], start=(k == 0), stop=False)
                        nc.tensor.matmul(ps[:], xTh[:, b, k, :], wl[:, j % RING, f], start=False, stop=False)
                        mm = nc.tensor.matmul(ps[:], xTh[:, b, k, :], wh[:, j % RING, f], start=False, stop=(k == KD - 1))
                    mm.then_inc(w_used, 1)

            def turn_hid(p, b):
                wait(pe, hid_done, p, b, 1, 1)
                wait(pe, hT_done, p, b, 1, 0)
                hk = hid[:].rearrange("p (q k) -> p k q", k=KF)
                for k in range(KF):
                    mm = nc.tensor.transpose(hT_ps[:, k, :], hk[:, k, :], ident[:])
                mm.then_inc(hT_mm, 1)

            def down(p, b):
                wait(pe, hT_done, p, b, 1, 1)
                for k in range(KF):
                    pe.wait_ge(weights.loaded[b][8 + k], val(p, 0, 8, 16))
                    for j in range(2):
                        if k == 0:
                            wait(pe, y_done, p, b, 2, j - 1)
                        mm = nc.tensor.matmul(y_ps[j][:], hT[:, b, k, :], weights.d[b][:, k, j * 512:(j + 1) * 512],
                                              start=(k == 0), stop=(k == KF - 1))
                        if k == KF - 1:
                            mm.then_inc(y_mm, 1)
                    if k < KF - 1:
                        mm.then_inc(d_used, 1)

            def body(p, last):
                for b in range(2):
                    gate_up(p, b)
                    if b == 0 or not last:
                        turn_x(p, b, 1)
                    if b == 1:
                        down(p, 0)
                    elif p[0] is not None or p[1]:
                        down(shifted(p, -1), 1)
                    turn_hid(p, b)

            turn_x(FIRST, 0, 0)
            down(pairs(pe, body), 1)

        @block.vector
        def _(dve):
            vec = nc.vector

            def turn_x(p, b, ahead):
                par = (b + ahead) % 2
                for j in range(2):
                    wait(dve, xT_hi, p, b, 2, 2 * ahead + j + 1)
                    vec.tensor_tensor(xTl[:, par, 4 * j:4 * j + 4, :], tp[j][:], xTh[:, par, 4 * j:4 * j + 4, :].bitcast(F32),
                                      ALU.subtract).then_inc(xT_lo, 1)

            def split(p, b, j):
                wait(dve, w_hi, p, b, 8, j + 1)
                vec.tensor_tensor(wl[:, j % RING, :], weights.gate_up(b, j), wh[:, j % RING, :].bitcast(F32), ALU.subtract
                                  ).then_inc(w_lo, 1)

            def y_out(p, b):
                wait(dve, scattered[b], p, 0, 8, 0)
                for j in range(2):
                    wait(dve, y_mm, p, b, 2, j + 1)
                    vec.tensor_copy(yb[:, b, j * 512:(j + 1) * 512], y_ps[j][:]).then_inc(y_done, 1)

            def body(p, last):
                for b in range(2):
                    for j in range(RING, 8):
                        split(p, b, j)
                    if b == 0 or not last:
                        for j in range(RING):
                            split(*((p, 1) if b == 0 else (shifted(p, 1), 0)), j)
                        turn_x(p, b, 1)
                    wait(dve, silu_done, p, b, 1, 1)
                    wait(dve, w_used, p, b, 8, 8)
                    vec.tensor_tensor(hid[:], hid[:], u_ps[:], ALU.mult).then_inc(hid_done, 1)
                    if b == 1:
                        y_out(p, 0)
                    elif p[0] is not None or p[1]:
                        y_out(shifted(p, -1), 1)
                    wait(dve, hT_mm, p, b, 1, 1)
                    wait(dve, y_mm, p, b, 2, -2)
                    vec.tensor_copy(hT[:, b], hT_ps[:]).then_inc(hT_done, 1)

            for j in range(RING):
                split(FIRST, 0, j)
            turn_x(FIRST, 0, 0)
            y_out(pairs(dve, body, peeled=2), 1)
            for i in range(NT):
                dve.wait_ge(y2_loaded[i % 4], 16 * (i // 4 + 1))
                for c in range(2):
                    if c:
                        dve.wait_ge(comb, 2 * i + 1)
                    vec.scalar_tensor_tensor(hacc[:, i, :], y2[i % 4][:, c, :], wtok[:, c, i:i + 1], hacc[:, i, :],
                                             ALU.mult, ALU.add).then_inc(comb, 1)


def layer(nc, x, norm_mix, norm_ffn, ssd_w_in, ssd_conv_w, ssd_conv_b, ssd_dt_bias, ssd_a_log, ssd_d, ssd_norm,
          ssd_w_out, moe_w_group, moe_b_group, moe_w_expert, moe_b_expert, moe_w_gate, moe_w_up, moe_w_down, out):
    T, D = x.shape[1:]
    with ExitStack() as ctx:
        hacc = ctx.enter_context(nc.sbuf_tensor("hacc", [P, T // P, D], F32))
        ridx = ctx.enter_context(nc.sbuf_tensor("ridx", [P, 2, MAXB], I32))
        etab = ctx.enter_context(nc.sbuf_tensor("etab", [P, MAXB], I32))
        npairs = ctx.enter_context(nc.sbuf_tensor("npairs", [P, 3], I32))
        wtok = ctx.enter_context(nc.sbuf_tensor("wtok", [P, 2, T // P], F32))
        acum_dram = nc.dram_tensor("acum_dram", [GROUPS * R * (T // P), P], F32).ap()
        u2_dram = nc.dram_tensor("u2_dram", [T, D], F32).ap()
        y_dram = nc.dram_tensor("y_dram", [2 * T, D], F32).ap()
        lg = ctx.enter_context(nc.sbuf_tensor("lg", [P, T // P, EG + NE], F32))
        weights = Weights(nc, ctx, moe_w_gate[0], moe_w_up[0], moe_w_down[0])
        mamba(nc, hacc, lg, weights, x[0], norm_mix[0], ssd_w_in[0], ssd_conv_w[0], ssd_conv_b[0], ssd_dt_bias[0], ssd_a_log[0],
              ssd_d[0], ssd_norm[0], ssd_w_out[0], acum_dram, norm_ffn[0], moe_w_group[0], moe_w_expert[0], u2_dram)
        weights.keep(nc, ctx)
        xg = ctx.enter_context(nc.sbuf_tensor("xg", [P, 2, D], F32))
        zero = ctx.enter_context(nc.sbuf_tensor("zero", [P, 1], I32))
        ident = ctx.enter_context(nc.sbuf_tensor("ident2", [P, P], F32))
        routing(nc, lg, ridx, etab, npairs, wtok, weights, xg, zero, ident, moe_b_group[0], moe_b_expert[0])
        experts(nc, hacc, ridx, etab, npairs, wtok, weights, xg, zero, ident, u2_dram, y_dram, out[0])


_INS = ["x", "norm_mix", "norm_ffn", "ssd_w_in", "ssd_conv_w", "ssd_conv_b", "ssd_dt_bias", "ssd_a_log", "ssd_d",
        "ssd_norm", "ssd_w_out", "moe_w_group", "moe_b_group", "moe_w_expert", "moe_b_expert", "moe_w_gate",
        "moe_w_up", "moe_w_down"]
_OUTS = [((1, 1024, 1024), "float32")]


def kernel(**inputs):
    import numpy as _np
    import concourse.bacc as _bacc
    from concourse import mybir as _mybir
    from concourse.bass_utils import run_bass_kernel_spmd as _run

    nc = _bacc.Bacc("TRN2", target_bir_lowering=False, num_devices=1)
    arrays, args = {}, []
    for name in _INS:
        a = _np.ascontiguousarray(inputs[name])
        arrays[f"in_{name}_dram"] = a
        args.append(nc.dram_tensor(f"in_{name}_dram", a.shape, _mybir.dt.from_np(a.dtype), kind="ExternalInput").ap())
    for i, (shape, dtype) in enumerate(_OUTS):
        dt = _mybir.dt.from_np(_np.dtype(dtype))
        args.append(nc.dram_tensor(f"out_{i}_dram", shape, dt, kind="ExternalOutput").ap())
    layer(nc, *args)
    r = _run(nc, [arrays], core_ids=[0])
    return r.results[0]["out_0_dram"]
```
